# Optimizing a Trainium2 kernel written in Bass

```python
import math
import jax, jax.numpy as jnp
from jax import lax
import numpy as np

D_MODEL = 2048
BATCH = 1
SEQ = 256
DEPTH = 2

GRID_W = 64
CTX_LEN = 256
N_MIXERS = 2
N_SSD = (DEPTH + 1) // 2
N_MLA = DEPTH // 2

SSD_EXPAND = 2
D_INNER = SSD_EXPAND * D_MODEL
SSD_HEAD_DIM = 64
SSD_HEADS = D_INNER // SSD_HEAD_DIM
SSD_GROUPS = 8
SSD_STATE = 128
SSD_CONV = 5
SSD_CHUNK = 128
SSD_GN = SSD_GROUPS * SSD_STATE
CONV_CH = D_INNER + 2 * SSD_GN
SSD_IN = 2 * D_INNER + 2 * SSD_GN + 2 * SSD_HEADS
DT_MIN = 1e-3
DT_MAX = 1e-1

MLA_HEADS = 16
Q_RANK = 512
KV_RANK = 512
QK_NOPE = 128
QK_ROPE = 64
V_DIM = 128
MLA_GATE = MLA_HEADS * V_DIM
MLA_IN = Q_RANK + KV_RANK + QK_ROPE + MLA_GATE
ATTN_BLOCK = 128
ROPE_BASE = 10000.0

ALPHA = (2 * DEPTH) ** 0.25
BETA = (8 * DEPTH) ** -0.25
LN_EPS = 1e-5
RMS_EPS = 1e-6

kernel_name = 'hybrid_ssd_mla_deepnorm_prefix'

def layer_norm(x, g, b):
    xf = x.astype(jnp.float32)
    mu = jnp.mean(xf, -1, keepdims=True)
    var = jnp.mean(jnp.square(xf - mu), -1, keepdims=True)
    y = (xf - mu) * lax.rsqrt(var + LN_EPS) * g.astype(jnp.float32) + b.astype(jnp.float32)
    return y.astype(x.dtype)

def rms_norm(x, g):
    xf = x.astype(jnp.float32)
    y = xf * lax.rsqrt(jnp.mean(jnp.square(xf), -1, keepdims=True) + RMS_EPS)
    return (y * g.astype(jnp.float32)).astype(x.dtype)

def depthwise_conv(u, w, b):
    pad = SSD_CONV // 2
    y = lax.conv_general_dilated(u, w[:, None, :].astype(u.dtype), window_strides=(1,),
                                 padding=[(pad, pad)], dimension_numbers=('NWC', 'WIO', 'NWC'),
                                 feature_group_count=u.shape[-1])
    return y + b.astype(u.dtype)

def axial_rope_angles(n_tokens):
    rows = n_tokens // GRID_W
    rr, cc = jnp.meshgrid(jnp.arange(rows, dtype=jnp.float32), jnp.arange(GRID_W, dtype=jnp.float32), indexing='ij')
    n_freq = QK_ROPE // 4
    inv_freq = ROPE_BASE ** (-jnp.arange(n_freq, dtype=jnp.float32) / n_freq)
    ang = jnp.concatenate([rr.reshape(-1)[:, None] * inv_freq, cc.reshape(-1)[:, None] * inv_freq], -1)
    return jnp.cos(ang), jnp.sin(ang)

def apply_rope(t, cos, sin):
    tp = t.reshape(t.shape[:-1] + (QK_ROPE // 2, 2))
    t1, t2 = tp[..., 0], tp[..., 1]
    cos = cos.astype(t.dtype)
    sin = sin.astype(t.dtype)
    return jnp.stack([t1 * cos - t2 * sin, t1 * sin + t2 * cos], -1).reshape(t.shape)

def ssd_scan(xh, dt, A, Bm, Cm, h0):
    b, L, H, P = xh.shape
    G, N = Bm.shape[-2], Bm.shape[-1]
    E = H // G
    Q = SSD_CHUNK
    nc = L // Q
    x = (xh * dt[..., None]).reshape(b, nc, Q, G, E, P)
    a = jnp.moveaxis((dt * A).reshape(b, nc, Q, G, E), 2, -1)
    a_cs = jnp.cumsum(a, axis=-1)
    Bc = Bm.reshape(b, nc, Q, G, N)
    Cc = Cm.reshape(b, nc, Q, G, N)
    lower = jnp.tril(jnp.ones((Q, Q), dtype=bool))
    seg = a_cs[..., :, None] - a_cs[..., None, :]
    decay_in = jnp.exp(jnp.where(lower, seg, -jnp.inf))
    cb = jnp.einsum('bclgn,bcsgn->bcgls', Cc, Bc)
    y_diag = jnp.einsum('bcgels,bcsgep->bclgep', cb[:, :, :, None] * decay_in, x)
    to_end = jnp.moveaxis(jnp.exp(a_cs[..., -1:] - a_cs), -1, 2)
    chunk_states = jnp.einsum('bclgn,bclgep->bcgepn', Bc, x * to_end[..., None])
    chunk_decay = jnp.exp(a_cs[..., -1])

    def step(h, inp):
        s, d = inp
        return h * d[..., None, None] + s, h

    h_last, h_in = lax.scan(step, h0.reshape(b, G, E, P, N),
                            (jnp.moveaxis(chunk_states, 1, 0), jnp.moveaxis(chunk_decay, 1, 0)))
    h_in = jnp.moveaxis(h_in, 0, 1)
    from_start = jnp.moveaxis(jnp.exp(a_cs), -1, 2)
    y_off = jnp.einsum('bclgn,bcgepn->bclgep', Cc, h_in) * from_start[..., None]
    y = (y_diag + y_off).reshape(b, L, H, P)
    return y, h_last.reshape(b, H, P, N)

def ssd_mixer(u_x, u_c, w_in, conv_w, conv_b, dt_bias, a_log, d_skip, norm_w, w_out, need_ctx):
    A = (-jnp.exp(a_log.astype(jnp.float32))).astype(u_x.dtype)

    def project(u):
        b, L = u.shape[:2]
        h = u @ w_in
        z = h[..., :D_INNER]
        xbc = jax.nn.silu(depthwise_conv(h[..., D_INNER:D_INNER + CONV_CH], conv_w, conv_b))
        dt = jax.nn.softplus(h[..., D_INNER + CONV_CH:].reshape(b, L, 2, SSD_HEADS) + dt_bias)
        xh = xbc[..., :D_INNER].reshape(b, L, SSD_HEADS, SSD_HEAD_DIM)
        Bm = xbc[..., D_INNER:D_INNER + SSD_GN].reshape(b, L, SSD_GROUPS, SSD_STATE)
        Cm = xbc[..., D_INNER + SSD_GN:].reshape(b, L, SSD_GROUPS, SSD_STATE)
        return z, xh, dt, Bm, Cm

    def run(p, d, h0, reverse):
        _, xh, dt, Bm, Cm = p
        f = (lambda t: jnp.flip(t, 1)) if reverse else (lambda t: t)
        y, h = ssd_scan(f(xh), f(dt[:, :, d]), A[d], f(Bm), f(Cm), h0)
        return f(y), h

    def finish(p, y_f, y_b):
        z, xh, _, _, _ = p
        b, L = z.shape[:2]
        y = (y_f + y_b + d_skip[:, None] * xh).reshape(b, L, D_INNER) * jax.nn.silu(z)
        y = rms_norm(y.reshape(b, L, SSD_GROUPS, D_INNER // SSD_GROUPS),
                     norm_w.reshape(SSD_GROUPS, D_INNER // SSD_GROUPS)).reshape(b, L, D_INNER)
        return y @ w_out

    pc = project(u_c)
    px = project(u_x)
    h0 = jnp.zeros((u_x.shape[0], SSD_HEADS, SSD_HEAD_DIM, SSD_STATE), u_x.dtype)
    yc_f, hc_f = run(pc, 0, h0, False)
    yc_b, hc_b = run(pc, 1, h0, True)
    yx_f, _ = run(px, 0, hc_f, False)
    yx_b, _ = run(px, 1, hc_b, True)
    out_x = finish(px, yx_f, yx_b)
    out_c = finish(pc, yc_f, yc_b) if need_ctx else None
    return out_x, out_c

def mla_attend(qn, qr, kn, kr, v):
    scale = (QK_NOPE + QK_ROPE) ** -0.5
    s = (jnp.einsum('bhqd,bhkd->bhqk', qn, kn) + jnp.einsum('bhqr,bkr->bhqk', qr, kr)) * scale
    p = jax.nn.softmax(s.astype(jnp.float32), axis=-1).astype(v.dtype)
    return jnp.einsum('bhqk,bhkd->bhqd', p, v)

def mla_mixer(u_x, u_c, w_in, q_norm, kv_norm, w_uq, w_ukv, w_o, need_ctx):
    b, L = u_x.shape[:2]
    Lc = u_c.shape[1]
    cos, sin = axial_rope_angles(L)

    def project(u):
        bb, n = u.shape[:2]
        h = u @ w_in
        cq = rms_norm(h[..., :Q_RANK], q_norm)
        ckv = rms_norm(h[..., Q_RANK:Q_RANK + KV_RANK], kv_norm)
        kr = h[..., Q_RANK + KV_RANK:Q_RANK + KV_RANK + QK_ROPE]
        gate = h[..., Q_RANK + KV_RANK + QK_ROPE:]
        q = (cq @ w_uq).reshape(bb, n, MLA_HEADS, QK_NOPE + QK_ROPE)
        kv = (ckv @ w_ukv).reshape(bb, n, MLA_HEADS, QK_NOPE + V_DIM)
        return q[..., :QK_NOPE], q[..., QK_NOPE:], kv[..., :QK_NOPE], kr, kv[..., QK_NOPE:], gate

    qn, qr, kn, kr, v, gate = project(u_x)
    qr = apply_rope(qr, cos[:, None], sin[:, None])
    kr = apply_rope(kr, cos, sin)
    qn_c, qr_c, kn_c, kr_c, v_c, gate_c = project(u_c)

    kn_all = jnp.concatenate([kn_c, kn], 1).transpose(0, 2, 1, 3)
    kr_all = jnp.concatenate([kr_c, kr], 1)
    v_all = jnp.concatenate([v_c, v], 1).transpose(0, 2, 1, 3)
    nb = L // ATTN_BLOCK
    qn_b = qn.reshape(b, nb, ATTN_BLOCK, MLA_HEADS, QK_NOPE).transpose(1, 0, 3, 2, 4)
    qr_b = qr.reshape(b, nb, ATTN_BLOCK, MLA_HEADS, QK_ROPE).transpose(1, 0, 3, 2, 4)
    o = lax.map(lambda qs: mla_attend(qs[0], qs[1], kn_all, kr_all, v_all), (qn_b, qr_b))
    o = o.transpose(1, 0, 3, 2, 4).reshape(b, L, MLA_GATE)
    out_x = (jax.nn.silu(gate) * o) @ w_o

    out_c = None
    if need_ctx:
        o_c = mla_attend(qn_c.transpose(0, 2, 1, 3), qr_c.transpose(0, 2, 1, 3),
                         kn_c.transpose(0, 2, 1, 3), kr_c, v_c.transpose(0, 2, 1, 3))
        o_c = o_c.transpose(0, 2, 1, 3).reshape(b, Lc, MLA_GATE)
        out_c = (jax.nn.silu(gate_c) * o_c) @ w_o
    return out_x, out_c

def setup_inputs(seed: int = 0) -> dict:
    key = jax.random.key(seed)
    ks = iter(jax.random.split(key, 40))

    def nrm(shape, scale):
        return jax.random.normal(next(ks), shape, jnp.float32) * scale

    def unif(shape, lo, hi):
        return jax.random.uniform(next(ks), shape, jnp.float32, lo, hi)

    dt0 = jnp.exp(unif((N_SSD, 2, SSD_HEADS), math.log(DT_MIN), math.log(DT_MAX)))
    return {
        'x': nrm((BATCH, SEQ, D_MODEL), 1.0),
        'c': nrm((BATCH, D_MODEL), 1.0),
        'ctx': nrm((BATCH, CTX_LEN, D_MODEL), 1.0),
        'c_ctx': nrm((D_MODEL,), 1.0),
        'ada_w': nrm((DEPTH, D_MODEL, 3 * D_MODEL), D_MODEL ** -0.5),
        'ada_b': nrm((DEPTH, 3 * D_MODEL), 0.02),
        'ln_g': 1.0 + nrm((DEPTH, D_MODEL), 0.05),
        'ln_b': nrm((DEPTH, D_MODEL), 0.02),
        'ssd_w_in': nrm((N_SSD, D_MODEL, SSD_IN), D_MODEL ** -0.5),
        'ssd_conv_w': nrm((N_SSD, SSD_CONV, CONV_CH), SSD_CONV ** -0.5),
        'ssd_conv_b': nrm((N_SSD, CONV_CH), 0.02),
        'ssd_dt_bias': dt0 + jnp.log(-jnp.expm1(-dt0)),
        'ssd_a_log': jnp.log(unif((N_SSD, 2, SSD_HEADS), 1.0, 16.0)),
        'ssd_d': 1.0 + nrm((N_SSD, SSD_HEADS), 0.1),
        'ssd_norm_w': 1.0 + nrm((N_SSD, D_INNER), 0.05),
        'ssd_w_out': nrm((N_SSD, D_INNER, D_MODEL), BETA * D_INNER ** -0.5),
        'mla_w_in': nrm((N_MLA, D_MODEL, MLA_IN), D_MODEL ** -0.5),
        'mla_q_norm': 1.0 + nrm((N_MLA, Q_RANK), 0.05),
        'mla_kv_norm': 1.0 + nrm((N_MLA, KV_RANK), 0.05),
        'mla_w_uq': nrm((N_MLA, Q_RANK, MLA_HEADS * (QK_NOPE + QK_ROPE)), Q_RANK ** -0.5),
        'mla_w_ukv': nrm((N_MLA, KV_RANK, MLA_HEADS * (QK_NOPE + V_DIM)), KV_RANK ** -0.5),
        'mla_w_o': nrm((N_MLA, MLA_GATE, D_MODEL), BETA * MLA_GATE ** -0.5),
    }

def reference(x, c, ctx, c_ctx, ada_w, ada_b, ln_g, ln_b,
              ssd_w_in, ssd_conv_w, ssd_conv_b, ssd_dt_bias, ssd_a_log, ssd_d, ssd_norm_w, ssd_w_out,
              mla_w_in, mla_q_norm, mla_kv_norm, mla_w_uq, mla_w_ukv, mla_w_o):
    for i in range(DEPTH):
        need_ctx = i < DEPTH - 1
        mod_x = jax.nn.silu(c) @ ada_w[i] + ada_b[i]
        mod_c = jax.nn.silu(c_ctx) @ ada_w[i] + ada_b[i]
        sh_x, sc_x, g_x = jnp.split(mod_x[:, None, :], 3, axis=-1)
        sh_c, sc_c, g_c = jnp.split(mod_c, 3, axis=-1)
        u_x = x * (1.0 + sc_x) + sh_x
        u_c = ctx * (1.0 + sc_c) + sh_c
        j = i // N_MIXERS
        if i % N_MIXERS == 0:
            y_x, y_c = ssd_mixer(u_x, u_c, ssd_w_in[j], ssd_conv_w[j], ssd_conv_b[j], ssd_dt_bias[j],
                                 ssd_a_log[j], ssd_d[j], ssd_norm_w[j], ssd_w_out[j], need_ctx)
        else:
            y_x, y_c = mla_mixer(u_x, u_c, mla_w_in[j], mla_q_norm[j], mla_kv_norm[j],
                                 mla_w_uq[j], mla_w_ukv[j], mla_w_o[j], need_ctx)
        x = layer_norm(ALPHA * x + g_x * y_x, ln_g[i], ln_b[i])
        if need_ctx:
            ctx = layer_norm(ALPHA * ctx + g_c * y_c, ln_g[i], ln_b[i])
    return x


_drawn_inputs = setup_inputs


def setup_inputs(seed=0):
    import zlib

    import numpy as np

    out = dict(_drawn_inputs(seed))
    spreads = {}
    factors = {'ctx': 3.468,
     'ada_b': 5.238,
     'ssd_conv_b': 8.0,
     'ssd_d': 8.0,
     'ssd_norm_w': 5.28,
     'mla_q_norm': 8.0,
     'mla_kv_norm': 8.0}
    for name, (base, spread) in spreads.items():
        noise = np.random.default_rng([zlib.crc32(name.encode()), seed]).standard_normal(out[name].shape)
        drawn = base * np.exp(spread * noise) if base else spread * noise
        out[name] = __import__('jax').numpy.asarray(drawn.astype(out[name].dtype))
    for name, factor in factors.items():
        out[name] = (out[name] * factor).astype(out[name].dtype)
    return out
```

```python
from contextlib import ExitStack

import numpy as np
import concourse.bass as bass
from concourse import mybir

F32 = mybir.dt.float32
F32R = mybir.dt.float32r
ALU = mybir.AluOpType
ACT = mybir.ActivationFunctionType
AX = mybir.AxisListType

P = 128
D = 2048
KT = D // P
T = 512
TC = 256
NC = T // P
GROUPS = 8
GT = 4
HG = 8
HD = 64
TAPS = 5
RING = 4
UNIT = 1024
RANK = 512
HEADS = 16
SCALE = (128 + 64) ** -0.5
ALPHA = 4 ** 0.25
LN_EPS = 1e-5
RMS_EPS = 1e-6
SKIP = -1e30

DT_UNITS = 2
PROJ_UNITS = 20
WOUT_AT = DT_UNITS + GROUPS * PROJ_UNITS
WOUT_UNITS = 16
MLA_AT = WOUT_AT + 4 * WOUT_UNITS
GATE_UNITS = 32
LATENT_UNITS = 18
HEAD_AT = MLA_AT + GATE_UNITS + LATENT_UNITS
HEAD_UNITS = 7
WO_AT = HEAD_AT + 4 * HEAD_UNITS
WO_UNITS = 8
UNITS = WO_AT + 4 * WO_UNITS
SPLIT_AHEAD = 3

ADA0 = 32
ADA_TILES = 96
ADA0_RING = 6
ADA_PER_GROUP = 8

CONV_AT = 0
NORM_AT = CONV_AT + GROUPS * 36
ADA0_AT = NORM_AT + 32
ADAL_AT = ADA0_AT + 32
LNG_AT = ADAL_AT + 64
LNB_AT = LNG_AT + 16
QN_AT = LNB_AT + 16
KVN_AT = QN_AT + 4
COND_AT = KVN_AT + 4
PARS = COND_AT + 32

DT_ROW, WST_ROW, ECS_ROW, ETOT_ROW, NCS_ROW, A_ROW, D_ROW = 0, 8, 16, 24, 32, 40, 48

LINKS_PER_GROUP = 44
STEPS = [(0, 0), (0, 1), (0, 2), (0, 3), (1, 1), (1, 0), (1, 3), (1, 2)]
READS_STATE = [n for n in range(8) if n not in (0, 4)]
MAKES_STATE = [n for n in range(8) if n not in (3, 7)]
SUM_BANK = [3, 6]
X_BANK = [6, 7, 4, 5]


class Step:

    def __init__(self, eng, sem):
        self.eng, self.sem, self.base, self.n = eng, sem, 0, 0

    def link(self, ins):
        self.n += 1
        ins.then_inc(self.sem, 1)
        self.eng.wait_ge(self.sem, self.base + self.n)

    def enter(self, i, start, per):
        self.base, self.n = i * per + start, 0

    def leave(self, turns, start, per):
        assert self.n == per, f"{self.n} links in a turn"
        self.base, self.n = start + turns * per, 0


def program(nc, hbm):
    with ExitStack() as ctx:
        def sem(name):
            return ctx.enter_context(nc.semaphore(name))

        place = [-(-nc.sbuf_base // 32) * 32]

        def sb(name, shape, dtype=F32):
            t = nc.alloc_sbuf_tensor_at(name, [P] + shape, dtype, offset=place[0])
            place[0] += int(np.prod(shape)) * 4
            place[0] = -(-place[0] // 32) * 32
            assert place[0] <= nc.sbuf_usable_end, (name, place[0])
            return t

        raw = sb("raw", [RING, UNIT])
        w_hi = sb("w_hi", [RING, UNIT], F32R)
        w_lo = sb("w_lo", [RING, UNIT], F32R)
        par = sb("par", [PARS])
        ident = sb("ident", [P])
        ones = sb("ones", [P])
        rot = sb("rot", [P])
        ident_r = sb("ident_r", [P], F32R)
        tri = sb("tri", [2, P], F32R)
        skip = sb("skip", [2, P], F32R)
        cond = sb("cond", [KT, 2])
        mod0 = sb("mod0", [32, 2])
        modl = sb("modl", [64, 2])
        us = sb("us", [KT, 2])
        ub = sb("ub", [KT, 2])
        stat = sb("stat", [64])
        region_u = place[0]
        u_hi = sb("u_hi", [KT, T], F32R)
        u_lo = sb("u_lo", [KT, T], F32R)
        region_l = place[0]

        ada0 = sb("ada0", [ADA0_RING, KT, P])
        xcm = sb("xcm", [KT, T])
        utmp0 = sb("utmp0", [2, T])
        place[0] = region_l
        ada = sb("ada", [2, 8, P])
        sz = sb("sz", [NC, T])
        pad = sb("pad", [2, 2, TC + TAPS - 1])
        xbc = sb("xbc", [6, T])
        ccur = sb("ccur", [T])
        xtok = sb("xtok", [NC, T])
        btok = sb("btok", [NC, P])
        cbs = sb("cbs", [NC, P])
        em = sb("em", [2, 4, P])
        xdt = sb("xdt", [T])
        xw = sb("xw", [T])
        y = sb("y", [NC, T])
        yoff = sb("yoff", [T])
        state = sb("state", [T])
        y_t = sb("y_t", [GT, T])
        tab = sb("tab", [49, 64])
        gt = sb("gt", [49, HG])
        a_hi = sb("a_hi", [8, HG], F32R)
        a_lo = sb("a_lo", [8, HG], F32R)
        convg = sb("convg", [36])
        normg = sb("normg", [4])
        place[0] = region_u
        y_all = sb("y_all", [2 * KT, T])
        place[0] = region_l
        r_c = sb("r_c", [2, D])
        r_x = sb("r_x", [2, D])
        yr_hi = sb("yr_hi", [2, 2, T], F32R)
        yr_lo = sb("yr_lo", [2, 2, T], F32R)
        region_rows = place[0]
        gate0 = sb("gate0", [2, D])
        wtmp = sb("wtmp", [2, T])
        place[0] = region_rows
        rows0 = sb("rows0", [2, D])
        utmp1 = sb("utmp1", [2, T])
        bn = sb("bn", [NC, 24])
        place[0] = region_l
        sq = sb("sq", [2, T])
        rsd = sb("rsd", [2, T])
        gate1 = sb("gate1", [D])
        place[0] = region_l + 2 * D * 4 * 2
        gates = sb("gates", [HEADS, TC])
        cq = sb("cq", [4, TC])
        ckv = sb("ckv", [4, T])
        cq_hi = sb("cq_hi", [4, TC], F32R)
        cq_lo = sb("cq_lo", [4, TC], F32R)
        ckv_hi = sb("ckv_hi", [4, T], F32R)
        ckv_lo = sb("ckv_lo", [4, T], F32R)
        kr = sb("kr", [T])
        trig = sb("trig", [2, TC])
        place[0] = region_u
        og_hi = sb("og_hi", [HEADS, TC], F32R)
        og_lo = sb("og_lo", [HEADS, TC], F32R)
        region_h = place[0]
        qn = sb("qn", [4, TC])
        qr = sb("qr", [2, TC])
        qrt = sb("qrt", [2, TC])
        kn = sb("kn", [4, T])
        v = sb("v", [NC, T])
        prob = sb("prob", [2, T])
        prob_t = sb("prob_t", [NC, TC])
        place[0] = region_h
        rows1 = sb("rows1", [2, D])

        ps = ctx.enter_context(nc.psum_tensor("ps", [P, 8, T], F32))

        par_loaded, const_loaded, xcm_loaded, rows_loaded = (
            sem("par_loaded"), sem("const_loaded"), sem("xcm_loaded"), sem("rows_loaded"))
        tri_loaded = sem("tri_loaded")
        raw_loaded = [sem(f"raw_loaded{q}") for q in range(RING)]
        ada0_loaded = [sem(f"ada0_loaded{q}") for q in range(ADA0_RING)]
        ada_loaded = [sem(f"ada_loaded{q}") for q in range(2)]
        hi_ready, lo_ready, w_used = sem("hi_ready"), sem("lo_ready"), sem("w_used")
        ada0_used, ada_used = sem("ada0_used"), sem("ada_used")
        cond_ready, mod0_full, mod0_ready = sem("cond_ready"), sem("mod0_full"), sem("mod0_ready")
        consts_ready = sem("consts_ready")
        utmp_ready, uhi_ready, u_ready = sem("utmp_ready"), sem("uhi_ready"), sem("u_ready")
        dt_full, dt_taken, dt_abs, dt_exp, a_ready = (
            sem("dt_full"), sem("dt_taken"), sem("dt_abs"), sem("dt_exp"), sem("a_ready"))
        arow_exp = sem("arow_exp")
        cs_full, cs_diff, cs_exp, tab_ready = sem("cs_full"), sem("cs_diff"), sem("cs_exp"), sem("tab_ready")
        pads_clear, tile_full, tile_evac, pad_ready = (
            sem("pads_clear"), sem("tile_full"), sem("tile_evac"), sem("pad_ready"))
        conv_done, silu_done = sem("conv_done"), sem("silu_done")
        xt_full, xtok_ready, bt_full, btok_ready = (
            sem("xt_full"), sem("xtok_ready"), sem("bt_full"), sem("btok_ready"))
        cb_full, cbs_ready, slice_ready = sem("cb_full"), sem("cbs_ready"), sem("slice_ready")
        seg_full, decay_ready, m_ready, xdt_ready, xw_ready = (
            sem("seg_full"), sem("decay_ready"), sem("m_ready"), sem("xdt_ready"), sem("xw_ready"))
        yd_full, yd_taken, yo_full, yo_taken = (
            sem("yd_full"), sem("yd_taken"), sem("yo_full"), sem("yo_taken"))
        st_full, state_ready = sem("st_full"), sem("state_ready")
        gated, sq_done, var_ready, root_ready, y_normed = (
            sem("gated"), sem("sq_done"), sem("var_ready"), sem("root_ready"), sem("y_normed"))
        ada_full, ada_taken = sem("ada_full"), sem("ada_taken")
        yt_full, yt_evac, y_spilled = sem("yt_full"), sem("yt_evac"), sem("y_spilled")
        y_loaded, res_loaded = sem("y_loaded"), sem("res_loaded")
        g0_full, g0_taken, g0_taken_act = sem("g0_full"), sem("g0_taken"), sem("g0_taken_act")
        yhi_ready, ylo_ready, wo_full, wo_taken = (
            sem("yhi_ready"), sem("ylo_ready"), sem("wo_full"), sem("wo_taken"))
        rows0_loaded, lnvar_ready, lnroot_ready, ln_ready = (
            sem("rows0_loaded"), sem("lnvar_ready"), sem("lnroot_ready"), sem("ln_ready"))
        rt_full, rt_taken = sem("rt_full"), sem("rt_taken")
        x1_ready, trig_loaded = sem("x1_ready"), sem("trig_loaded")
        g1_full, g1_taken = sem("g1_full"), sem("g1_taken")
        gt_full, gt_taken = sem("gt_full"), sem("gt_taken")
        lat_full, lat_taken, sq_ready, sq_used = (
            sem("lat_full"), sem("lat_taken"), sem("sq_ready"), sem("sq_used"))
        ms_full, msv_ready, msroot_ready, cn_ready, chi_ready, clo_ready = (
            sem("ms_full"), sem("msv_ready"), sem("msroot_ready"), sem("cn_ready"),
            sem("chi_ready"), sem("clo_ready"))
        kr_full, kr_ready, krot_full = sem("kr_full"), sem("kr_ready"), sem("krot_full")
        hq_full, hq_act, hq_dve = sem("hq_full"), sem("hq_act"), sem("hq_dve")
        qrot_full, qr_ready = sem("qrot_full"), sem("qr_ready")
        s_full, max_ready, p_ready, p_scaled = (
            sem("s_full"), sem("max_ready"), sem("p_ready"), sem("p_scaled"))
        pt_full, pt_ready, o_full, o_taken, ogh_ready, ogl_ready = (
            sem("pt_full"), sem("pt_ready"), sem("o_full"), sem("o_taken"),
            sem("ogh_ready"), sem("ogl_ready"))
        out_taken, rows1_loaded, fvar_ready, froot_ready, out_ready, stored = (
            sem("out_taken"), sem("rows1_loaded"), sem("fvar_ready"), sem("froot_ready"),
            sem("out_ready"), sem("stored"))
        dve_step, act_step = sem("dve_step"), sem("act_step")

        block = ctx.enter_context(nc.Block())

        @block.sync
        def _(sp):
            def load_unit(s, slot, first=False):
                if not first:
                    sp.wait_ge(lo_ready, s - RING + 1)
                sp.dma_start(raw[:, slot, :], hbm["stream"][s]).then_inc(raw_loaded[slot], 16)

            sp.dma_start(par[:], hbm["par"]).then_inc(par_loaded, 16)
            for t in range(ADA0):
                if t >= ADA0_RING:
                    sp.wait_ge(ada0_used, t - ADA0_RING + 1)
                sp.dma_start(ada0[:, t % ADA0_RING], hbm["ada"][t]).then_inc(
                    ada0_loaded[t % ADA0_RING], 16)
                if t == 3:
                    sp.dma_start(xcm[:], hbm["x_cm"]).then_inc(xcm_loaded, 16)
                    for n, c in enumerate((ident, ones, rot)):
                        sp.dma_start(c[:], hbm["consts"][n]).then_inc(const_loaded, 16)
                    sp.dma_start(utmp0[:, 0, :].rearrange("p (a b) -> p a b", a=4),
                                 hbm["consts"][3:7].rearrange("a p b -> p a b")).then_inc(tri_loaded, 16)
            for s in range(RING):
                load_unit(s, s, first=True)
            sp.wait_ge(u_ready, KT)
            sp.dma_start(y[:, 0, 0:128], hbm["dt_bias"].to_broadcast([P, 128])).then_inc(rows_loaded, 16)
            sp.dma_start(y[:, 1, 0:128], hbm["a_log"].to_broadcast([P, 128])).then_inc(rows_loaded, 16)
            sp.dma_start(tab[:, D_ROW, :], hbm["d_skip"].to_broadcast([P, 64])).then_inc(rows_loaded, 16)
            for s in range(RING, DT_UNITS + PROJ_UNITS):
                load_unit(s, s % RING)

            def load_ada(g, t):
                for half in range(2):
                    if t:
                        sp.wait_ge(ada_used, g * 2 * ADA_PER_GROUP + (2 * t + half - 1))
                    elif not isinstance(g, int) or g > 0:
                        sp.wait_ge(ada_used, g * 2 * ADA_PER_GROUP)
                    sp.dma_start(ada[:, half], hbm["ada"][g * ADA_PER_GROUP + (ADA0 + t)][
                        :, half * 8:half * 8 + 8, :]).then_inc(ada_loaded[half], 16)

            def load_group(g, proj):
                for j in range(PROJ_UNITS):
                    if proj:
                        load_unit(DT_UNITS + PROJ_UNITS * (g + 1) + j, (DT_UNITS + j) % RING)
                    if j == 1:
                        load_ada(g, 0)
                    elif j % 2 == 0 and j >= 8:
                        load_ada(g, j // 2 - 3)
                load_ada(g, ADA_PER_GROUP - 1)

            load_group(0, True)
            with sp.Fori(1, GROUPS - 1) as i:
                load_group(i, True)
            for s in range(WOUT_AT, WOUT_AT + RING):
                load_unit(s, s % RING)
            load_group(GROUPS - 1, False)
            sp.wait_ge(w_used, WOUT_AT)
            for g in range(GROUPS):
                if g >= GROUPS - 1:
                    sp.wait_ge(y_spilled, 16 * GROUPS)
                elif g == 0:
                    sp.wait_ge(y_spilled, 16 * (GROUPS - 1))
                sp.dma_start(y_all[:, g * GT:g * GT + GT, :], hbm["y"][g]).then_inc(y_loaded, 16)
            sp.wait_ge(y_normed, GROUPS)
            sp.wait_ge(ada_taken, GROUPS)
            for n, rows in enumerate((r_c, r_x)):
                sp.dma_start(rows[:], hbm["x_tm"][2 * n:2 * n + 2].rearrange("c p n -> p c n")).then_inc(
                    res_loaded, 16)
            with sp.Fori(0, 2) as i:
                for b in range(2):
                    for u in range(WOUT_UNITS):
                        k = b * WOUT_UNITS + u + RING
                        load_unit(WOUT_AT + k + i * 2 * WOUT_UNITS, (WOUT_AT + k) % RING)
            sp.wait_ge(wo_taken, NC * 6)
            for n in range(2):
                sp.dma_start(rows0[:, n, :], hbm["ln_rows"][0, n].to_broadcast([P, D])).then_inc(rows0_loaded, 16)
            sp.dma_start(trig[:], hbm["trig"]).then_inc(trig_loaded, 16)
            with sp.Fori(0, (UNITS - MLA_AT - RING) // RING - 1) as i:
                for q in range(RING):
                    load_unit(i * RING + (MLA_AT + RING + q), (MLA_AT + q) % RING)
            sp.wait_ge(ogl_ready, HEADS)
            for n in range(2):
                sp.dma_start(rows1[:, n, :], hbm["ln_rows"][1, n].to_broadcast([P, D])).then_inc(rows1_loaded, 16)
            for s in range(MLA_AT + RING * ((UNITS - MLA_AT - RING) // RING), UNITS):
                load_unit(s, s % RING)
            for c in range(2):
                sp.wait_ge(out_ready, c + 1)
                sp.dma_start(hbm["out"][0, c * P:c * P + P, :], r_x[:, c]).then_inc(stored, 16)
            sp.wait_ge(stored, 32)

        @block.gpsimd
        def _(pool):
            with pool.Fori(0, UNITS // RING) as i:
                for q in range(RING):
                    pool.wait_ge(hi_ready, i * RING + q + 1)
                    nc.gpsimd.tensor_tensor(w_lo[:, q], raw[:, q], w_hi[:, q].bitcast(F32),
                                            ALU.subtract).then_inc(lo_ready, 1)

        @block.scalar
        def _(act):
            step = Step(act, act_step)

            def split_high(s, slot, turn=None, first=False):
                act.wait_ge(raw_loaded[slot], 16 * turn)
                if not first:
                    act.wait_ge(w_used, s - RING + 1)
                nc.scalar.activation(w_hi[:, slot], raw[:, slot], ACT.Copy).then_inc(hi_ready, 1)

            def split_at(base, off, n):
                s = base + off
                split_high(s if n is None else n * RING + s, s % RING,
                           turn=(s // RING + 1) if n is None else n + (s // RING + 1),
                           first=n is None and s < RING)

            act.wait_ge(par_loaded, 16)
            nc.scalar.activation(cond[:], par[:, COND_AT:COND_AT + 32].rearrange("p (k v) -> p k v", v=2),
                                 ACT.Silu).then_inc(cond_ready, 1)
            for s in range(SPLIT_AHEAD):
                split_at(0, s, None)
            for k in range(KT):
                act.wait_ge(utmp_ready, k + 1)
                nc.scalar.activation(u_hi[:, k], utmp0[:, k % 2], ACT.Copy).then_inc(uhi_ready, 1)
            split_at(0, SPLIT_AHEAD, None)
            split_at(1, SPLIT_AHEAD, None)
            act.wait_ge(rows_loaded, 48)
            nc.scalar.activation(y[:, 2, 0:128], y[:, 1, 0:128], ACT.Exp).then_inc(arow_exp, 1)
            act.wait_ge(dt_abs, 1)
            nc.scalar.activation(xw[:], xdt[:], ACT.Exp, scale=-1.0).then_inc(dt_exp, 1)

            def evac_tile(g, t):
                act.wait_ge(w_used, DT_UNITS + PROJ_UNITS * g + 2 * t + 2)
                if not (isinstance(g, int) and g == 0 and t < 2):
                    act.wait_ge(conv_done, 6 * g + t - 1)
                else:
                    act.wait_ge(pads_clear, 1)
                nc.scalar.activation(pad[:, t % 2, :, 2:2 + TC],
                                     ps[:, t % 4].rearrange("p (s n) -> p s n", s=2),
                                     ACT.Copy).then_inc(tile_evac, 1)

            def silu_tiles(g):
                for t in range(6):
                    act.wait_ge(conv_done, 6 * g + t + 1)
                    nc.scalar.activation(xbc[:, t], xbc[:, t], ACT.Silu).then_inc(silu_done, 1)

            def silu_z(g):
                for c in range(NC):
                    act.wait_ge(w_used, DT_UNITS + PROJ_UNITS * (g + 1))
                    nc.scalar.activation(sz[:, c], ps[:, c], ACT.Silu).then_inc(tile_evac, 1)

            for j in range(PROJ_UNITS):
                split_at(DT_UNITS, j + SPLIT_AHEAD, None)
                if j % 2 == 0 and 2 <= j < 14:
                    evac_tile(0, j // 2 - 1)
                if j == 5:
                    act.wait_ge(cs_diff, 1)
                    nc.scalar.activation(tab[:, ECS_ROW:ECS_ROW + 8].rearrange("p r h -> p (r h)"), ps[:, 5], ACT.Exp).then_inc(cs_exp, 1)
                    nc.scalar.activation(tab[:, ETOT_ROW:ETOT_ROW + 8].rearrange("p r h -> p (r h)"), ps[:, 6], ACT.Exp).then_inc(cs_exp, 1)
                    nc.scalar.activation(xw[:], xw[:], ACT.Exp).then_inc(cs_exp, 1)
            silu_tiles(0)
            silu_z(0)

            def group(g, proj):
                for j in range(PROJ_UNITS):
                    if proj:
                        s = DT_UNITS + PROJ_UNITS + j + SPLIT_AHEAD
                        act.wait_ge(raw_loaded[s % RING], 16 * (s // RING + 1) + g * 16 * (PROJ_UNITS // RING))
                        act.wait_ge(w_used, g * PROJ_UNITS + (s - RING + 1))
                        nc.scalar.activation(w_hi[:, s % RING], raw[:, s % RING], ACT.Copy).then_inc(hi_ready, 1)
                        if j % 2 == 0 and 2 <= j < 14:
                            evac_tile(g + 1, j // 2 - 1)
                    if j == 1:
                        for c in range(NC):
                            act.wait_ge(xt_full, NC * g + c + 1)
                            act.wait_ge(gated, NC * g)
                            nc.scalar.activation(xtok[:, c], ps[:, X_BANK[c]], ACT.Copy).then_inc(xtok_ready, 1)
                    if j == 2:
                        act.wait_ge(bt_full, g + 1)
                        act.wait_ge(st_full, 6 * g)
                        nc.scalar.activation(btok[:].rearrange("p c n -> p (c n)"), ps[:, 6], ACT.Copy).then_inc(btok_ready, 1)
                    if 2 <= j < 18:
                        h = j - 2
                        d, c = STEPS[h // 2]
                        act.wait_ge(seg_full, 16 * g + h + 1)
                        act.wait_ge(slice_ready, g + 1)
                        act.wait_ge(yd_full, 16 * g + max(h - 1, 0))
                        for a in range(4):
                            hd = h % 2 * 4 + a
                            ins = nc.scalar.activation(em[:, h % 2, a], ps[:, 4, a * P:a * P + P], ACT.Exp,
                                                       bias=gt[:, NCS_ROW + 2 * c + d, hd:hd + 1])
                        ins.then_inc(decay_ready, 1)
                    if j in (13, 15, 17, 19):
                        m = (j - 13) // 2
                        c = STEPS[4 + m][1]
                        act.wait_ge(gated, NC * g + m + 1)
                        nc.scalar.activation(sz[:, c], y[:, c], ACT.Square,
                                             accum_out=stat[:, c:c + 1]).then_inc(sq_done, 1)
                act.wait_ge(var_ready, g + 1)
                nc.scalar.activation(stat[:, 8:12], stat[:, 4:8], ACT.Sqrt).then_inc(root_ready, 1)
                if proj:
                    silu_tiles(g + 1)
                    silu_z(g + 1)
                for k in range(GT):
                    act.wait_ge(yt_full, GT * g + k + 1)
                    act.wait_ge(y_spilled, 16 * g)
                    nc.scalar.activation(y_t[:, k], ps[:, 4 + k], ACT.Copy,
                                         scale=normg[:, k:k + 1]).then_inc(yt_evac, 1)
                act.wait_ge(yt_evac, GT * g + GT)
                act.dma_start(hbm["y"][g], y_t[:]).then_inc(y_spilled, 16)

            group(0, True)
            with act.Fori(1, GROUPS - 1) as i:
                group(i, True)
            group(GROUPS - 1, False)

            act.wait_ge(y_spilled, 16 * GROUPS)
            for b in range(4):
                act.wait_ge(g0_full, b + 1)
                nc.scalar.activation(gate0[:, 0, b * T:b * T + T], ps[:, b], ACT.Copy).then_inc(g0_taken_act, 1)

            def y_high(q_next, kt, slot):
                nc.scalar.activation(yr_hi[:, slot], y_all[:, kt:kt + 2], ACT.Copy).then_inc(yhi_ready, 1)

            act.wait_ge(y_loaded, 16 * GROUPS)
            y_high(0, 0, 0)
            with act.Fori(0, 2) as i:
                for b in range(2):
                    for u in range(WOUT_UNITS):
                        s = WOUT_AT + b * WOUT_UNITS + u + SPLIT_AHEAD
                        split_high(i * 2 * WOUT_UNITS + s, s % RING, turn=i * (2 * WOUT_UNITS // RING) + (s // RING + 1))
                        y_high(None, 2 * ((u + 1) % WOUT_UNITS), (u + 1) % 2)

            act.wait_ge(lnvar_ready, 1)
            nc.scalar.activation(stat[:, 20:24], stat[:, 16:20], ACT.Sqrt).then_inc(lnroot_ready, 1)
            for k in range(KT):
                act.wait_ge(utmp_ready, KT + k + 1)
                nc.scalar.activation(u_hi[:, k], utmp1[:, k % 2], ACT.Copy).then_inc(uhi_ready, 1)

            with act.Fori(0, 4) as i:
                for t in range(4):
                    for half in range(2):
                        s = MLA_AT + 2 * t + half + SPLIT_AHEAD
                        split_high(i * 8 + s, s % RING, turn=i * 2 + (s // RING + 1))
                    act.wait_ge(w_used, i * 8 + (MLA_AT + 2 * t + 2))
                    nc.scalar.activation(gates[:, bass.ds(i * 4 + t, 1), :].rearrange("p a n -> p (a n)"),
                                         ps[:, t, 0:TC], ACT.Silu).then_inc(gt_taken, 1)
            lat = MLA_AT + GATE_UNITS
            for j in range(LATENT_UNITS):
                s = lat + j + SPLIT_AHEAD
                split_high(s, s % RING, turn=s // RING + 1)
                if j % 2 == 1:
                    t = j // 2
                    act.wait_ge(w_used, lat + j + 1)
                    if t == 0:
                        act.wait_ge(x1_ready, 1)
                    if t < 4:
                        src, dst = ps[:, 4 + t, 0:TC], cq[:, t]
                    elif t < 8:
                        src, dst = ps[:, t - 4], ckv[:, t - 4]
                    else:
                        src, dst = ps[:, 4], kr[:]
                    nc.scalar.activation(dst, src, ACT.Copy).then_inc(lat_taken, 1)
                    if t < 8:
                        if t >= 2:
                            act.wait_ge(sq_used, t - 1)
                        n = TC if t < 4 else T
                        nc.scalar.activation(sq[:, t % 2, 0:n], src, ACT.Square).then_inc(sq_ready, 1)
            for m in range(2):
                act.wait_ge(msv_ready, m + 1)
                n = (TC, T)[m]
                nc.scalar.activation(rsd[:, m, 0:n], rsd[:, m, 0:n], ACT.Sqrt).then_inc(msroot_ready, 1)
            for t in range(8):
                act.wait_ge(cn_ready, t + 1)
                src, dst = (cq[:, t], cq_hi[:, t]) if t < 4 else (ckv[:, t - 4], ckv_hi[:, t - 4])
                nc.scalar.activation(dst, src, ACT.Copy).then_inc(chi_ready, 1)

            for b in range(4):
                for j in range(HEAD_UNITS):
                    s = HEAD_AT + b * HEAD_UNITS + j + SPLIT_AHEAD
                    split_high(s, s % RING, turn=s // RING + 1)
                    if j < 2:
                        act.wait_ge(w_used, s - SPLIT_AHEAD + 1)
                        act.wait_ge(s_full, 8 * b)
                        nc.scalar.activation(qn[:, 2 * j:2 * j + 2].rearrange("p a n -> p (a n)"), ps[:, j], ACT.Copy).then_inc(hq_act, 1)
                    if j in (3, 4):
                        act.wait_ge(w_used, s - SPLIT_AHEAD + 1)
                        for n in range(2):
                            nc.scalar.activation(kn[:, 2 * (j - 3) + n], ps[:, 3 + 2 * (j - 3) + n], ACT.Copy).then_inc(hq_act, 1)
                act.wait_ge(w_used, HEAD_AT + HEAD_UNITS * (b + 1))
                act.wait_ge(o_full, 4 * b)
                for n in range(2):
                    nc.scalar.activation(v[:, n], ps[:, n], ACT.Copy).then_inc(hq_act, 1)

                def exp_scores(n):
                    m = 8 * b + n
                    act.wait_ge(max_ready, m + 1)
                    if m >= 2:
                        act.wait_ge(pt_full, m - 1)
                    nc.scalar.activation(prob[:, n % 2], ps[:, 4 + n % 2], ACT.Exp, bias=stat[:, 32 + n:33 + n],
                                         scale=SCALE, accum_out=stat[:, 40 + n:41 + n]).then_inc(p_ready, 1)

                def gated_high(hh):
                    act.wait_ge(o_taken, 4 * b + hh + 1)
                    nc.scalar.activation(og_hi[:, 4 * b + hh], sq[:, hh % 2, 0:TC], ACT.Copy).then_inc(ogh_ready, 1)

                for n in range(8):
                    exp_scores(n)
                    if n % 2 == 1 and n >= 3:
                        gated_high(n // 2 - 1)
                gated_high(3)

            with act.Fori(0, 3) as i:
                for u in range(WO_UNITS):
                    s = WO_AT + u + SPLIT_AHEAD
                    split_high(i * WO_UNITS + s, s % RING, turn=i * (WO_UNITS // RING) + (s // RING + 1))
            for s in range(WO_AT + 3 * WO_UNITS + SPLIT_AHEAD, UNITS):
                split_high(s, s % RING, turn=s // RING + 1)
            act.wait_ge(fvar_ready, 1)
            nc.scalar.activation(stat[:, 28:30], stat[:, 24:26], ACT.Sqrt).then_inc(froot_ready, 1)

        @block.vector
        def _(dve):
            step = Step(dve, dve_step)
            link = step.link
            vec = nc.vector

            dve.wait_ge(const_loaded, 48)
            dve.wait_ge(tri_loaded, 16)
            dve.wait_ge(par_loaded, 16)
            link(vec.tensor_copy(ident_r[:], ident[:]))
            link(vec.tensor_copy(tri[:].rearrange("p a b -> p (a b)"), utmp0[:, 0, 0:256]))
            link(vec.tensor_copy(skip[:].rearrange("p a b -> p (a b)"), utmp0[:, 0, 256:512]))
            vec.memset(stat[:], 0.0).then_inc(consts_ready, 1)

            dve.wait_ge(ada0_used, ADA0)
            link(vec.tensor_tensor(mod0[:], ps[:, 7, 0:64].rearrange("p (t v) -> p t v", v=2),
                                   par[:, ADA0_AT:ADA0_AT + 32].unsqueeze(2).to_broadcast([P, 32, 2]), ALU.add))
            link(vec.tensor_scalar(mod0[:, 16:32], mod0[:, 16:32], 1.0, None, ALU.add))

            def modulate(n, k, dst, src, scale, shift):
                if n >= 2:
                    dve.wait_ge(u_ready, n - 1)
                for s in range(2):
                    ins = vec.tensor_scalar(dst[:, s * TC:s * TC + TC], src[:, s * TC:s * TC + TC],
                                            scale[:, s:s + 1], shift[:, s:s + 1], ALU.mult, ALU.add)
                    if s == 0:
                        link(ins)
                return ins.then_inc(utmp_ready, 1)

            def low_u(n, k, src):
                dve.wait_ge(uhi_ready, n + 1)
                vec.tensor_tensor(u_lo[:, k], src, u_hi[:, k].bitcast(F32), ALU.subtract).then_inc(u_ready, 1)

            dve.wait_ge(xcm_loaded, 16)
            for k in range(KT):
                modulate(k, k, utmp0[:, k % 2], xcm[:, k], mod0[:, 16 + k], mod0[:, k])
                if k:
                    low_u(k - 1, k - 1, utmp0[:, (k - 1) % 2])
            low_u(KT - 1, KT - 1, utmp0[:, (KT - 1) % 2])
            dve.wait_ge(u_ready, KT)
            link(vec.memset(pad[:, :, :, 0:2], 0.0))
            vec.memset(pad[:, :, :, 2 + TC:4 + TC], 0.0).then_inc(pads_clear, 1)

            chunks = lambda ap: ap.rearrange("p (c h) -> p c h", c=NC)
            dve.wait_ge(w_used, DT_UNITS)
            dve.wait_ge(rows_loaded, 48)
            link(vec.tensor_tensor(chunks(yoff[:]), ps[:, 0:4, 0:128],
                                   y[:, 0, 0:128].unsqueeze(1).to_broadcast([P, NC, 128]), ALU.add))
            vec.scalar_tensor_tensor(out=xdt[:], in0=yoff[:], scalar=-1.0, in1=yoff[:], op0=ALU.mult,
                                     op1=ALU.max).then_inc(dt_abs, 1)
            dve.wait_ge(dt_exp, 1)
            link(vec.tensor_scalar(xdt[:], xw[:], 2.0, None, ALU.add))
            link(vec.reciprocal(xdt[:], xdt[:]))
            link(vec.tensor_tensor(xdt[:], xdt[:], xw[:], ALU.mult))
            link(vec.tensor_tensor(xw[:], xdt[:], xdt[:], ALU.mult))
            link(vec.tensor_scalar(state[:], xw[:], 1.0 / 15.0, None, ALU.mult))
            for m in (13, 11, 9, 7, 5, 3):
                link(vec.scalar_tensor_tensor(out=state[:], in0=state[:], scalar=1.0 / m, in1=xw[:],
                                              op0=ALU.add, op1=ALU.mult))
            link(vec.scalar_tensor_tensor(out=state[:], in0=state[:], scalar=1.0, in1=xdt[:],
                                          op0=ALU.add, op1=ALU.mult))
            link(vec.tensor_scalar(yoff[:], yoff[:], 0.0, None, ALU.max))
            flat = lambda r: tab[:, r:r + 8].rearrange("p r h -> p (r h)")
            link(vec.scalar_tensor_tensor(out=flat(DT_ROW), in0=state[:], scalar=2.0, in1=yoff[:],
                                          op0=ALU.mult, op1=ALU.add))
            dve.wait_ge(arow_exp, 1)
            link(vec.tensor_tensor(chunks(flat(A_ROW)), chunks(flat(DT_ROW)),
                                   y[:, 2, 0:128].unsqueeze(1).to_broadcast([P, NC, 128]), ALU.mult))
            vec.tensor_scalar(flat(A_ROW), flat(A_ROW), -1.0, None, ALU.mult).then_inc(a_ready, 1)
            dve.wait_ge(cs_full, 1)
            link(vec.tensor_scalar(flat(NCS_ROW), ps[:, 5], -1.0, None, ALU.mult))
            vec.tensor_tensor(xw[:], ps[:, 6], flat(NCS_ROW), ALU.add).then_inc(cs_diff, 1)
            dve.wait_ge(cs_exp, 3)
            link(vec.tensor_tensor(flat(WST_ROW), xw[:], flat(DT_ROW), ALU.mult))

            def conv_weights(g_next):
                if isinstance(g_next, int):
                    src = par[:, CONV_AT + 36 * g_next:CONV_AT + 36 * g_next + 36]
                else:
                    src = par[:, bass.ds(g_next * 36 + CONV_AT, 36)]
                link(vec.tensor_copy(convg[:], src))

            def conv(g, t):
                out = xbc[:, t].rearrange("p (s n) -> p s n", s=2)
                dve.wait_ge(tile_evac, 10 * g + t + 1)
                if not (isinstance(g, int) and g == 0):
                    dve.wait_ge(xt_full, NC * g)
                    dve.wait_ge(bt_full, g)
                    dve.wait_ge(cb_full, g)
                link(vec.tensor_scalar(out, pad[:, t % 2, :, 0:TC], convg[:, 5 * t:5 * t + 1],
                                       convg[:, 30 + t:31 + t], ALU.mult, ALU.add))
                for j in range(1, TAPS):
                    ins = vec.scalar_tensor_tensor(out=out, in0=pad[:, t % 2, :, j:j + TC],
                                                   scalar=convg[:, 5 * t + j:5 * t + j + 1], in1=out,
                                                   op0=ALU.mult, op1=ALU.add)
                    if j < TAPS - 1:
                        link(ins)
                ins.then_inc(conv_done, 1)

            conv_weights(0)
            for t in range(6):
                conv(0, t)

            def group(g, proj):
                if isinstance(g, int):
                    src = tab[:, :, g * HG:g * HG + HG]
                    nsrc = par[:, NORM_AT + GT * g:NORM_AT + GT * g + GT]
                else:
                    src = tab[:, :, bass.ds(g * HG, HG)]
                    nsrc = par[:, bass.ds(g * GT + NORM_AT, GT)]
                dve.wait_ge(decay_ready, 16 * g)
                dve.wait_ge(seg_full, 16 * g)
                link(vec.tensor_copy(gt[:], src))
                link(vec.tensor_copy(a_hi[:], gt[:, A_ROW:A_ROW + 8]))
                vec.tensor_tensor(a_lo[:], gt[:, A_ROW:A_ROW + 8], a_hi[:].bitcast(F32),
                                  ALU.subtract).then_inc(slice_ready, 1)
                dve.wait_ge(yt_evac, GT * g)
                link(vec.tensor_copy(normg[:], nsrc))
                if proj:
                    conv_weights(g + 1)

                dve.wait_ge(cb_full, g + 1)
                link(vec.tensor_copy(cbs[:].rearrange("p c n -> p (c n)"), ps[:, 7]))
                dve.wait_ge(yo_full, 6 * g)
                vec.tensor_copy(ccur[:], xbc[:, 5]).then_inc(cbs_ready, 1)

                heads = lambda ap: ap.rearrange("p (h d) -> p h d", h=HG)
                per_head = lambda row: gt[:, row, :].unsqueeze(2).to_broadcast([P, HG, HD])

                def scaled_x(n):
                    d, c = STEPS[n]
                    dve.wait_ge(xtok_ready, NC * g + NC)
                    dve.wait_ge(yd_full, 16 * g + 2 * n)
                    vec.tensor_tensor(heads(xdt[:]), heads(xtok[:, c]), per_head(DT_ROW + 2 * c + d),
                                      ALU.mult).then_inc(xdt_ready, 1)
                    if n in MAKES_STATE:
                        dve.wait_ge(st_full, 6 * g + len([m for m in MAKES_STATE if m < n]))
                        vec.tensor_tensor(heads(xw[:]), heads(xtok[:, c]), per_head(WST_ROW + 2 * c + d),
                                          ALU.mult).then_inc(xw_ready, 1)

                def masked(h):
                    c = STEPS[h // 2][1]
                    dve.wait_ge(decay_ready, 16 * g + h + 1)
                    vec.tensor_tensor(em[:, h % 2], em[:, h % 2], cbs[:, c].unsqueeze(1).to_broadcast([P, 4, P]),
                                      ALU.mult).then_inc(m_ready, 1)

                dve.wait_ge(cbs_ready, g + 1)
                scaled_x(0)
                for n in range(8):
                    d, c = STEPS[n]
                    masked(2 * n)
                    if n in READS_STATE:
                        dve.wait_ge(yo_full, 6 * g + READS_STATE.index(n) + 1)
                        vec.tensor_tensor(heads(yoff[:]), heads(ps[:, 7]), per_head(ECS_ROW + 2 * c + d),
                                          ALU.mult).then_inc(yo_taken, 1)
                    masked(2 * n + 1)
                    if n in MAKES_STATE:
                        if n in READS_STATE:
                            link(vec.tensor_tensor(heads(state[:]), heads(state[:]), per_head(ETOT_ROW + 2 * c + d), ALU.mult))
                        dve.wait_ge(st_full, 6 * g + MAKES_STATE.index(n) + 1)
                        if n in READS_STATE:
                            vec.tensor_tensor(state[:], state[:], ps[:, 7], ALU.add).then_inc(state_ready, 1)
                        else:
                            vec.tensor_copy(state[:], ps[:, 7]).then_inc(state_ready, 1)
                    if d == 0:
                        link(vec.tensor_tensor(heads(y[:, c]), heads(xtok[:, c]), per_head(D_ROW), ALU.mult))
                    dve.wait_ge(yd_full, 16 * g + 2 * n + 2)
                    ins = vec.tensor_tensor(y[:, c], y[:, c], ps[:, 6], ALU.add).then_inc(yd_taken, 1)
                    dve.wait_ge(yd_taken, 8 * g + n + 1)
                    if n in READS_STATE:
                        dve.wait_ge(yo_taken, 6 * g + READS_STATE.index(n) + 1)
                        link(vec.tensor_tensor(y[:, c], y[:, c], yoff[:], ALU.add))
                    if d == 1:
                        dve.wait_ge(tile_evac, 10 * g + 7 + c)
                        vec.tensor_tensor(y[:, c], y[:, c], sz[:, c], ALU.mult).then_inc(gated, 1)
                    if n < 7:
                        scaled_x(n + 1)
                    if proj and 1 <= n < 7:
                        conv(g + 1, n - 1)

                dve.wait_ge(ada_used, g * 2 * ADA_PER_GROUP + 2 * ADA_PER_GROUP)
                if isinstance(g, int):
                    dst = modl[:, ADA_PER_GROUP * g:ADA_PER_GROUP * (g + 1), :]
                    bias = par[:, ADAL_AT + ADA_PER_GROUP * g:ADAL_AT + ADA_PER_GROUP * (g + 1)]
                else:
                    dst = modl[:, bass.ds(g * ADA_PER_GROUP, ADA_PER_GROUP), :]
                    bias = par[:, bass.ds(g * ADA_PER_GROUP + ADAL_AT, ADA_PER_GROUP)]
                vec.tensor_tensor(dst, ps[:, 5, 0:16].rearrange("p (t v) -> p t v", v=2),
                                  bias.unsqueeze(2).to_broadcast([P, ADA_PER_GROUP, 2]),
                                  ALU.add).then_inc(ada_taken, 1)

                dve.wait_ge(sq_done, NC * g + NC)
                vec.tensor_scalar(stat[:, 4:8], stat[:, 0:4], 1.0 / T, RMS_EPS, ALU.mult,
                                  ALU.add).then_inc(var_ready, 1)
                dve.wait_ge(root_ready, g + 1)
                link(vec.reciprocal(stat[:, 12:16], stat[:, 8:12]))
                for c in range(NC):
                    ins = vec.tensor_scalar(y[:, c], y[:, c], stat[:, 12 + c:13 + c], None, ALU.mult)
                ins.then_inc(y_normed, 1)

            group(0, True)
            start = step.base + step.n
            with dve.Fori(1, GROUPS - 1) as i:
                step.enter(i - 1, start, LINKS_PER_GROUP)
                group(i, True)
            step.leave(GROUPS - 2, start, LINKS_PER_GROUP)
            group(GROUPS - 1, False)

            dve.wait_ge(y_spilled, 16 * GROUPS)
            for b in range(4):
                dve.wait_ge(g0_full, 4 + b + 1)
                vec.tensor_copy(gate0[:, 1, b * T:b * T + T], ps[:, 4 + b]).then_inc(g0_taken, 1)
            dve.wait_ge(g0_taken, 4)
            dve.wait_ge(g0_taken_act, 4)
            vec.memset(wtmp[:, 0], 0.0).then_inc(wo_taken, 2 * NC)

            def y_low(q_next, kt, slot):
                dve.wait_ge(yhi_ready, q_next)
                vec.tensor_tensor(yr_lo[:, slot], y_all[:, kt:kt + 2], yr_hi[:, slot].bitcast(F32),
                                  ALU.subtract).then_inc(ylo_ready, 1)

            y_low(1, 0, 0)
            start = step.base + step.n
            with dve.Fori(0, 2) as i:
                step.enter(i, start, 2 * NC)
                for b in range(2):
                    for u in range(WOUT_UNITS):
                        y_low(i * 2 * WOUT_UNITS + (b * WOUT_UNITS + u + 2), 2 * ((u + 1) % WOUT_UNITS), (u + 1) % 2)
                    dve.wait_ge(res_loaded, 32)
                    for c in range(NC):
                        col = bass.ds(i * 2 * T + b * T, T)
                        dve.wait_ge(w_used, i * 2 * WOUT_UNITS + (WOUT_AT + (b + 1) * WOUT_UNITS))
                        link(vec.tensor_tensor(wtmp[:, c % 2], ps[:, 4 * b + c], gate0[:, c // 2, col], ALU.mult))
                        rows = (r_c if c < 2 else r_x)[:, c % 2, col]
                        vec.scalar_tensor_tensor(out=rows, in0=rows, scalar=ALPHA, in1=wtmp[:, c % 2],
                                                 op0=ALU.mult, op1=ALU.add).then_inc(wo_taken, 1)
            step.leave(2, start, 2 * NC)

            def normalise(rows, n, var_sem, root_sem, at):
                for c in range(n):
                    for q in range(4):
                        ins = vec.bn_stats(bn[:, c, 6 * q:6 * q + 6], rows[c][:, q * T:q * T + T])
                    link(ins)
                    link(vec.bn_aggr(stat[:, 48 + 2 * c:50 + 2 * c], bn[:, c]))
                    ins = vec.tensor_scalar(stat[:, at + c:at + c + 1], stat[:, 49 + 2 * c:50 + 2 * c], LN_EPS, None, ALU.add)
                ins.then_inc(var_sem, 1)
                dve.wait_ge(root_sem, 1)
                link(vec.reciprocal(stat[:, 56:56 + n], stat[:, at + 4:at + 4 + n]))

            dve.wait_ge(wo_taken, NC * 6)
            rows = [r_c[:, 0], r_c[:, 1], r_x[:, 0], r_x[:, 1]]
            normalise(rows, 4, lnvar_ready, lnroot_ready, 16)
            for c in range(4):
                vec.tensor_scalar(rows[c], rows[c], stat[:, 48 + 2 * c:49 + 2 * c], stat[:, 56 + c:57 + c],
                                  ALU.subtract, ALU.mult).then_inc(ln_ready, 1)
            link(vec.tensor_scalar(us[:], modl[:, 32:48], 1.0, None, ALU.add))
            link(vec.tensor_tensor(ub[:], us[:], par[:, LNB_AT:LNB_AT + 16].unsqueeze(2).to_broadcast([P, KT, 2]), ALU.mult))
            link(vec.tensor_tensor(ub[:], ub[:], modl[:, 16:32], ALU.add))
            link(vec.tensor_tensor(us[:], us[:], par[:, LNG_AT:LNG_AT + 16].unsqueeze(2).to_broadcast([P, KT, 2]), ALU.mult))
            dve.wait_ge(ln_ready, 4)
            for k in range(KT):
                dve.wait_ge(rt_full, k + 1)
                modulate(KT + k, k, utmp1[:, k % 2], ps[:, k % 4], us[:, k], ub[:, k])
                if k:
                    low_u(KT + k - 1, k - 1, utmp1[:, (k - 1) % 2])
            low_u(2 * KT - 1, KT - 1, utmp1[:, (KT - 1) % 2])
            dve.wait_ge(rows0_loaded, 32)
            for c in range(2):
                link(vec.tensor_tensor(r_x[:, c], r_x[:, c], rows0[:, 0], ALU.mult))
                ins = vec.tensor_tensor(r_x[:, c], r_x[:, c], rows0[:, 1], ALU.add)
            ins.then_inc(x1_ready, 1)
            for b in range(4):
                dve.wait_ge(g1_full, b + 1)
                vec.tensor_copy(gate1[:, b * T:b * T + T], ps[:, 4 + b]).then_inc(g1_taken, 1)

            for m in range(2):
                n = (TC, T)[m]
                dve.wait_ge(sq_used, 4 * m + 4)
                vec.tensor_scalar(rsd[:, m, 0:n], ps[:, SUM_BANK[m], 0:n], 1.0 / RANK, RMS_EPS, ALU.mult,
                                  ALU.add).then_inc(msv_ready, 1)
            for m in range(2):
                n = (TC, T)[m]
                dve.wait_ge(msroot_ready, m + 1)
                link(vec.reciprocal(rsd[:, m, 0:n], rsd[:, m, 0:n]))
                for t in range(4):
                    src = (cq, ckv)[m][:, t]
                    w = par[:, (QN_AT, KVN_AT)[m] + t:(QN_AT, KVN_AT)[m] + t + 1]
                    dve.wait_ge(lat_taken, 4 * m + t + 1)
                    vec.scalar_tensor_tensor(out=src, in0=src, scalar=w, in1=rsd[:, m, 0:n], op0=ALU.mult,
                                             op1=ALU.mult).then_inc(cn_ready, 1)
                for t in range(4):
                    hi, lo = ((cq_hi, cq_lo), (ckv_hi, ckv_lo))[m]
                    dve.wait_ge(chi_ready, 4 * m + t + 1)
                    vec.tensor_tensor(lo[:, t], (cq, ckv)[m][:, t], hi[:, t].bitcast(F32),
                                      ALU.subtract).then_inc(clo_ready, 1)
            dve.wait_ge(krot_full, 1)
            dve.wait_ge(trig_loaded, 16)
            vec.tensor_tensor(sq[:, 0, 0:TC], ps[:, 7, 0:TC], trig[:, 1], ALU.mult)
            link(vec.tensor_tensor(kr[:, TC:T], kr[:, TC:T], trig[:, 0], ALU.mult))
            vec.tensor_tensor(kr[:, TC:T], kr[:, TC:T], sq[:, 0, 0:TC], ALU.add).then_inc(kr_ready, 1)

            for b in range(4):
                dve.wait_ge(w_used, HEAD_AT + HEAD_UNITS * b + 3)
                dve.wait_ge(s_full, 8 * b)
                vec.tensor_copy(qr[:].rearrange("p a n -> p (a n)"), ps[:, 2]).then_inc(hq_dve, 1)
                dve.wait_ge(w_used, HEAD_AT + HEAD_UNITS * (b + 1))
                dve.wait_ge(o_full, 4 * b)
                for n in range(2):
                    vec.tensor_copy(v[:, 2 + n], ps[:, 2 + n]).then_inc(hq_dve, 1)
                dve.wait_ge(qrot_full, b + 1)
                dve.wait_ge(hq_dve, 3 * b + 1)
                both = lambda ap: ap.unsqueeze(1).to_broadcast([P, 2, TC])
                vec.tensor_tensor(qrt[:], ps[:, 7].rearrange("p (a n) -> p a n", a=2), both(trig[:, 1]), ALU.mult)
                link(vec.tensor_tensor(qr[:], qr[:], both(trig[:, 0]), ALU.mult))
                vec.tensor_tensor(qr[:], qr[:], qrt[:], ALU.add).then_inc(qr_ready, 1)

                def max_scores(n):
                    m = 8 * b + n
                    dve.wait_ge(s_full, m + 1)
                    link(vec.reduce_max(stat[:, 32 + n:33 + n], ps[:, 4 + n % 2], AX.X))
                    vec.tensor_scalar(stat[:, 32 + n:33 + n], stat[:, 32 + n:33 + n], -SCALE, None,
                                      ALU.mult).then_inc(max_ready, 1)

                def scale_probs(n):
                    m = 8 * b + n
                    dve.wait_ge(p_ready, m + 1)
                    link(vec.reciprocal(stat[:, 40 + n:41 + n], stat[:, 40 + n:41 + n]))
                    vec.tensor_scalar(prob[:, n % 2], prob[:, n % 2], stat[:, 40 + n:41 + n], None,
                                      ALU.mult).then_inc(p_scaled, 1)

                def take_transposed(n):
                    m = 8 * b + n
                    dve.wait_ge(pt_full, m + 1)
                    if n % 2 == 0 and m >= 2:
                        dve.wait_ge(o_full, m // 2)
                    vec.tensor_copy(prob_t[:, :, n % 2 * P:n % 2 * P + P],
                                    ps[:, 6].rearrange("p (k q) -> p k q", k=4)).then_inc(pt_ready, 1)

                def gate_output(hh):
                    hd = 4 * b + hh
                    dve.wait_ge(o_full, hd + 1)
                    if hd >= 2:
                        dve.wait_ge(ogl_ready, hd - 1)
                    vec.tensor_tensor(sq[:, hh % 2, 0:TC], ps[:, 7, 0:TC], gates[:, hd], ALU.mult).then_inc(o_taken, 1)
                    dve.wait_ge(ogh_ready, hd + 1)
                    vec.tensor_tensor(og_lo[:, hd], sq[:, hh % 2, 0:TC], og_hi[:, hd].bitcast(F32),
                                      ALU.subtract).then_inc(ogl_ready, 1)

                max_scores(0)
                for n in range(8):
                    if n < 7:
                        max_scores(n + 1)
                    scale_probs(n)
                    take_transposed(n)
                    if n % 2 == 1 and n >= 3:
                        gate_output(n // 2 - 1)
                gate_output(3)

            dve.wait_ge(g1_taken, 4)
            dve.wait_ge(x1_ready, 1)
            vec.memset(stat[:, 63:64], 0.0).then_inc(out_taken, 4)
            for nb in range(4):
                for c in range(2):
                    dve.wait_ge(w_used, WO_AT + WO_UNITS * (nb + 1))
                    cols = slice(nb * T, nb * T + T)
                    link(vec.tensor_tensor(sq[:, c], ps[:, 2 * (nb % 2) + c], gate1[:, cols], ALU.mult))
                    ins = vec.scalar_tensor_tensor(out=r_x[:, c, cols], in0=r_x[:, c, cols], scalar=ALPHA,
                                                   in1=sq[:, c], op0=ALU.mult, op1=ALU.add)
                    ins.then_inc(out_taken, 1)
            dve.wait_ge(out_taken, 12)
            normalise([r_x[:, 0], r_x[:, 1]], 2, fvar_ready, froot_ready, 24)
            dve.wait_ge(rows1_loaded, 32)
            for c in range(2):
                link(vec.tensor_scalar(r_x[:, c], r_x[:, c], stat[:, 48 + 2 * c:49 + 2 * c],
                                       stat[:, 56 + c:57 + c], ALU.subtract, ALU.mult))
                link(vec.tensor_tensor(r_x[:, c], r_x[:, c], rows1[:, 0], ALU.mult))
                vec.tensor_tensor(r_x[:, c], r_x[:, c], rows1[:, 1], ALU.add).then_inc(out_ready, 1)

        @block.tensor
        def _(pe):
            mm = nc.tensor.matmul

            def product(out, lhs, rhs, first, last):
                mm(out, lhs[0], rhs[0], start=first, stop=False)
                mm(out, lhs[0], rhs[1], start=False, stop=False)
                return mm(out, lhs[1], rhs[0], start=False, stop=last)

            def weights(slot, cols):
                view = lambda w: w[:, slot].rearrange("p (k n) -> p k n", n=cols)
                return view(w_hi), view(w_lo)

            pe.wait_ge(cond_ready, 1)
            for t in range(ADA0):
                pe.wait_ge(ada0_loaded[t % ADA0_RING], 16 * (t // ADA0_RING + 1))
                for k in range(KT):
                    ins = mm(ps[:, 7, 2 * t:2 * t + 2], ada0[:, t % ADA0_RING, k], cond[:, k],
                             start=(k == 0), stop=(k == KT - 1))
                ins.then_inc(ada0_used, 1)

            pe.wait_ge(u_ready, KT)
            for half in range(2):
                pe.wait_ge(lo_ready, half + 1)
                w = weights(half, P)
                for c in range(NC):
                    cols = slice(c * P, c * P + P)
                    for k in range(8):
                        kt = half * 8 + k
                        ins = product(ps[:, c, 0:P], (u_hi[:, kt, cols], u_lo[:, kt, cols]),
                                      (w[0][:, k], w[1][:, k]), kt == 0, kt == KT - 1)
                ins.then_inc(w_used, 1)

            def project(g, j):
                pe.wait_ge(lo_ready, PROJ_UNITS * g + (DT_UNITS + j + 1))
                slot = (DT_UNITS + j) % RING
                if j < 12:
                    t, half = divmod(j, 2)
                    w = weights(slot, P)
                    if half == 0:
                        if isinstance(g, int) and g == 0 and t < 4:
                            pe.wait_ge(dt_abs, 1)
                        else:
                            pe.wait_ge(tile_evac, 10 * g + max(t - 3, 0))
                    for k in range(8):
                        kt = half * 8 + k
                        ins = product(ps[:, t % 4], (w[0][:, k], w[1][:, k]), (u_hi[:, kt], u_lo[:, kt]),
                                      kt == 0, kt == KT - 1)
                else:
                    u = j - 12
                    w = weights(slot, T)
                    if u == 0:
                        pe.wait_ge(tile_evac, 10 * g + 6)
                    for c in range(NC):
                        for k in range(2):
                            kt = 2 * u + k
                            cols = slice(c * P, c * P + P)
                            ins = product(ps[:, c], (u_hi[:, kt, cols], u_lo[:, kt, cols]),
                                          (w[0][:, k], w[1][:, k]), kt == 0, kt == KT - 1)
                ins.then_inc(w_used, 1)

            for j in range(PROJ_UNITS):
                project(0, j)
                if j == 3:
                    pe.wait_ge(a_ready, 1)
                    pe.wait_ge(consts_ready, 1)
                    rows = tab[:, A_ROW:A_ROW + 8].rearrange("p (c d) h -> p c d h", d=2)
                    out = ps[:, 5].rearrange("p (c d h) -> p c d h", c=NC, d=2)
                    for d in range(2):
                        mm(out[:, :, d], tri[:, d].bitcast(F32), rows[:, :, d], start=True, stop=True)
                    mm(ps[:, 6], ones[:], tab[:, A_ROW:A_ROW + 8].rearrange("p r h -> p (r h)"),
                       start=True, stop=True).then_inc(cs_full, 1)

            def scan(g, j):
                if j == 1:
                    pe.wait_ge(silu_done, 6 * g + 6)
                    for c in range(NC):
                        if c == 0:
                            pe.wait_ge(yt_evac, GT * g)
                        for k in range(GT):
                            ins = nc.tensor.transpose(ps[:, X_BANK[c], k * P:k * P + P],
                                                      xbc[:, k, c * P:c * P + P], ident[:])
                        ins.then_inc(xt_full, 1)
                if j == 2:
                    pe.wait_ge(xtok_ready, NC * g + 1)
                    for c in range(NC):
                        ins = nc.tensor.transpose(ps[:, 6, c * P:c * P + P], xbc[:, 4, c * P:c * P + P], ident[:])
                    ins.then_inc(bt_full, 1)
                    pe.wait_ge(xtok_ready, NC * g + 2)
                    for c in range(NC):
                        ins = mm(ps[:, 7, c * P:c * P + P], xbc[:, 4, c * P:c * P + P],
                                 xbc[:, 5, c * P:c * P + P], start=True, stop=True)
                    ins.then_inc(cb_full, 1)
                if 3 <= j < 19:
                    n, half = divmod(j - 3, 2)
                    if half == 0:
                        if n == 0:
                            pe.wait_ge(btok_ready, g + 1)
                        pe.wait_ge(yd_taken, 8 * g + n)
                        pe.wait_ge(xdt_ready, 8 * g + n + 1)
                    pe.wait_ge(m_ready, 16 * g + (j - 3) + 1)
                    for a in range(4):
                        hd = 4 * half + a
                        ins = mm(ps[:, 6, hd * HD:hd * HD + HD], em[:, half, a], xdt[:, hd * HD:hd * HD + HD],
                                 start=True, stop=True)
                    ins.then_inc(yd_full, 1)
                    if half == 0 and n in READS_STATE:
                        c = STEPS[n][1]
                        pe.wait_ge(state_ready, 6 * g + len([m for m in MAKES_STATE if m < n]))
                        mm(ps[:, 7], ccur[:, c * P:c * P + P], state[:], start=True, stop=True).then_inc(yo_full, 1)
                    if half == 1 and n in MAKES_STATE:
                        c = STEPS[n][1]
                        if n == 0:
                            pe.wait_ge(cbs_ready, g + 1)
                        pe.wait_ge(yo_taken, 6 * g + len([m for m in READS_STATE if m <= n]))
                        pe.wait_ge(xw_ready, 6 * g + MAKES_STATE.index(n) + 1)
                        mm(ps[:, 7], btok[:, c], xw[:], start=True, stop=True).then_inc(st_full, 1)
                if 2 <= j < 18:
                    h = j - 2
                    d, c = STEPS[h // 2]
                    if h == 0:
                        pe.wait_ge(slice_ready, g + 1)
                        pe.wait_ge(xtok_ready, NC * g + 3)
                    pe.wait_ge(decay_ready, 16 * g + h)
                    for a in range(4):
                        hd = h % 2 * 4 + a
                        out = ps[:, 4, a * P:a * P + P]
                        for n, part in enumerate((a_hi, a_lo)):
                            mm(out, part[:, 2 * c + d, hd:hd + 1].to_broadcast([P, P]), tri[:, d],
                               start=(n == 0), stop=False)
                        ins = mm(out, ident_r[:], skip[:, d], start=False, stop=True)
                    ins.then_inc(seg_full, 1)
                if j % 2 == 1 and 3 <= j < 3 + 2 * ADA_PER_GROUP:
                    t = (j - 3) // 2
                    if t == 0:
                        pe.wait_ge(xtok_ready, NC * g + NC)
                    for half in range(2):
                        pe.wait_ge(ada_loaded[half], g * 16 * ADA_PER_GROUP + 16 * (t + 1))
                        for k in range(8):
                            kt = half * 8 + k
                            ins = mm(ps[:, 5, 2 * t:2 * t + 2], ada[:, half, k], cond[:, kt],
                                     start=(kt == 0), stop=(kt == KT - 1))
                        ins.then_inc(ada_used, 1)

            def group(g, proj):
                for j in range(PROJ_UNITS):
                    scan(g, j)
                    if proj:
                        project(g + 1, j)
                pe.wait_ge(y_normed, g + 1)
                pe.wait_ge(decay_ready, 16 * g + 16)
                pe.wait_ge(ada_taken, g + 1)
                for k in range(GT):
                    for c in range(NC):
                        ins = nc.tensor.transpose(ps[:, 4 + k, c * P:c * P + P], y[:, c, k * P:k * P + P], ident[:])
                    ins.then_inc(yt_full, 1)

            pe.wait_ge(cs_exp, 3)
            group(0, True)
            with pe.Fori(1, GROUPS - 1) as i:
                group(i, True)
            group(GROUPS - 1, False)

            pe.wait_ge(ada_taken, GROUPS)
            pe.wait_ge(yt_evac, GT * GROUPS)
            pe.wait_ge(tile_evac, 10 * GROUPS)
            for s in range(2):
                for t in range(KT):
                    ins = mm(ps[:, 4 * s + t // 4, t % 4 * P:t % 4 * P + P],
                             modl[:, t, s:s + 1].to_broadcast([P, P]), ident[:], start=True, stop=True)
                    if t % 4 == 3:
                        ins.then_inc(g0_full, 1)

            with pe.Fori(0, 2) as i:
                for b in range(2):
                    pe.wait_ge(wo_taken, i * 2 * NC + (b + 1) * NC)
                    for u in range(WOUT_UNITS):
                        at = b * WOUT_UNITS + u
                        pe.wait_ge(ylo_ready, i * 2 * WOUT_UNITS + (at + 1))
                        pe.wait_ge(lo_ready, i * 2 * WOUT_UNITS + (WOUT_AT + at + 1))
                        w = weights((WOUT_AT + at) % RING, T)
                        for c in range(NC):
                            cols = slice(c * P, c * P + P)
                            for k in range(2):
                                ins = product(ps[:, 4 * b + c], (yr_hi[:, u % 2, k, cols], yr_lo[:, u % 2, k, cols]),
                                              (w[0][:, k], w[1][:, k]), u == 0 and k == 0,
                                              u == WOUT_UNITS - 1 and k == 1)
                        ins.then_inc(w_used, 1)

            pe.wait_ge(ln_ready, 4)
            for k in range(KT):
                if k >= 4:
                    pe.wait_ge(utmp_ready, KT + k - 3)
                for c in range(NC):
                    ins = nc.tensor.transpose(ps[:, k % 4, c * P:c * P + P],
                                              (r_c, r_x)[c // 2][:, c % 2, k * P:k * P + P], ident[:])
                ins.then_inc(rt_full, 1)
            for t in range(KT):
                ins = mm(ps[:, 4 + t // 4, t % 4 * P:t % 4 * P + P],
                         modl[:, 48 + t, 1:2].to_broadcast([P, P]), ident[:], start=True, stop=True)
                if t % 4 == 3:
                    ins.then_inc(g1_full, 1)

            pe.wait_ge(u_ready, 2 * KT)
            with pe.Fori(0, 4) as i:
                for t in range(4):
                    if t == 2:
                        pe.wait_ge(gt_taken, i * 4 + 1)
                    for half in range(2):
                        s = MLA_AT + 2 * t + half
                        pe.wait_ge(lo_ready, i * 8 + (s + 1))
                        w = weights(s % RING, P)
                        for k in range(8):
                            kt = half * 8 + k
                            ins = product(ps[:, t, 0:TC], (w[0][:, k], w[1][:, k]),
                                          (u_hi[:, kt, TC:T], u_lo[:, kt, TC:T]), kt == 0, kt == KT - 1)
                        ins.then_inc(w_used, 1)
                pe.wait_ge(gt_taken, i * 4 + 2)

            def sum_squares(t):
                m, q = divmod(t, 4)
                n = (TC, T)[m]
                pe.wait_ge(sq_ready, t + 1)
                mm(ps[:, SUM_BANK[m], 0:n], ones[:], sq[:, t % 2, 0:n], start=(q == 0), stop=(q == 3)).then_inc(sq_used, 1)

            pe.wait_ge(g1_taken, 4)
            pe.wait_ge(gt_taken, HEADS)
            for j in range(LATENT_UNITS):
                t, half = divmod(j, 2)
                s = MLA_AT + GATE_UNITS + j
                pe.wait_ge(lo_ready, s + 1)
                if t == 7 and half == 0:
                    pe.wait_ge(msv_ready, 1)
                if t == 8 and half == 0:
                    pe.wait_ge(sq_ready, 1)
                w = weights(s % RING, P)
                lo = TC if t < 4 else 0
                out = ps[:, 4 + t, 0:TC] if t < 4 else ps[:, t - 4] if t < 8 else ps[:, 4]
                for k in range(8):
                    kt = half * 8 + k
                    ins = product(out, (w[0][:, k], w[1][:, k]), (u_hi[:, kt, lo:T], u_lo[:, kt, lo:T]),
                                  kt == 0, kt == KT - 1)
                ins.then_inc(w_used, 1)
                if half == 1 and t >= 1:
                    sum_squares(t - 1)
            pe.wait_ge(lat_taken, 9)
            mm(ps[:, 7, 0:TC], rot[:], kr[:, TC:T], start=True, stop=True).then_inc(krot_full, 1)

            for b in range(4):
                at = HEAD_AT + HEAD_UNITS * b
                for j in range(HEAD_UNITS):
                    s = at + j
                    pe.wait_ge(lo_ready, s + 1)
                    if j == 0:
                        pe.wait_ge(clo_ready, 4)
                        pe.wait_ge(hq_act, 8 * b)
                        pe.wait_ge(hq_dve, 3 * b)
                        pe.wait_ge(lat_taken, 8)
                    if j == 3:
                        pe.wait_ge(clo_ready, 8)
                        pe.wait_ge(p_ready, 8 * b)
                        pe.wait_ge(pt_ready, 8 * b)
                    if j == 5:
                        pe.wait_ge(hq_act, 8 * b + 4)
                        pe.wait_ge(hq_dve, 3 * b + 1)
                    if j < 5:
                        w = weights(s % RING, 2 * P)
                        lat_hi, lat_lo = (cq_hi, cq_lo) if j < 3 else (ckv_hi, ckv_lo)
                        for a in range(2):
                            out = ps[:, j, a * TC:a * TC + TC] if j < 3 else ps[:, 3 + 2 * (j - 3) + a]
                            for k in range(4):
                                cols = slice(a * P, a * P + P)
                                ins = product(out, (w[0][:, k, cols], w[1][:, k, cols]),
                                              (lat_hi[:, k], lat_lo[:, k]), k == 0, k == 3)
                    else:
                        w = weights(s % RING, T)
                        for c in range(NC):
                            cols = slice(c * P, c * P + P)
                            for k in range(2):
                                kt = 2 * (j - 5) + k
                                ins = product(ps[:, c], (ckv_hi[:, kt, cols], ckv_lo[:, kt, cols]),
                                              (w[0][:, k], w[1][:, k]), kt == 0, kt == 3)
                    ins.then_inc(w_used, 1)
                    if j == 4:
                        pe.wait_ge(hq_dve, 3 * b + 1)
                        pe.wait_ge(o_taken, 4 * b)
                        if b == 0:
                            pe.wait_ge(kr_ready, 1)
                        mm(ps[:, 7], rot[:], qr[:].rearrange("p a n -> p (a n)"), start=True,
                           stop=True).then_inc(qrot_full, 1)

                def scores(n):
                    hh, qt = divmod(n, 2)
                    if n == 0:
                        pe.wait_ge(hq_act, 8 * b + 6)
                        pe.wait_ge(qr_ready, b + 1)
                    pe.wait_ge(p_ready, 8 * b + max(n - 1, 0))
                    q = slice(qt * P, qt * P + P)
                    half = slice(64 * (hh % 2), 64 * (hh % 2) + 64)
                    mm(ps[:, 4 + n % 2], qn[:, hh, q], kn[:, hh], start=True, stop=False)
                    mm(ps[:, 4 + n % 2], qr[half, hh // 2, q], kr[half, :], start=False, stop=True).then_inc(s_full, 1)

                def transpose_probs(n):
                    pe.wait_ge(p_scaled, 8 * b + n + 1)
                    pe.wait_ge(pt_ready, 8 * b + n)
                    for c in range(NC):
                        ins = nc.tensor.transpose(ps[:, 6, c * P:c * P + P], prob[:, n % 2, c * P:c * P + P], ident[:])
                    ins.then_inc(pt_full, 1)

                def head_output(hh):
                    pe.wait_ge(pt_ready, 8 * b + 2 * hh + 2)
                    pe.wait_ge(o_taken, 4 * b + hh)
                    pe.wait_ge(hq_act, 8 * b + 8)
                    pe.wait_ge(hq_dve, 3 * b + 3)
                    for c in range(NC):
                        ins = mm(ps[:, 7, 0:TC], v[:, c, hh * P:hh * P + P], prob_t[:, c], start=(c == 0), stop=(c == 3))
                    ins.then_inc(o_full, 1)

                scores(0)
                for n in range(8):
                    if n < 7:
                        scores(n + 1)
                    transpose_probs(n)
                    if n % 2 == 1:
                        head_output(n // 2)

            pe.wait_ge(ogl_ready, HEADS)
            with pe.Fori(0, 2) as i:
                for b in range(2):
                    pe.wait_ge(out_taken, i * 4 + (2 * b + 2))
                    for u in range(WO_UNITS):
                        s = WO_AT + b * WO_UNITS + u
                        pe.wait_ge(lo_ready, i * 2 * WO_UNITS + (s + 1))
                        w = weights(s % RING, T)
                        for c in range(2):
                            cols = slice(c * P, c * P + P)
                            for k in range(2):
                                kt = 2 * u + k
                                ins = product(ps[:, 2 * b + c], (og_hi[:, kt, cols], og_lo[:, kt, cols]),
                                              (w[0][:, k], w[1][:, k]), kt == 0, kt == KT - 1)
                        ins.then_inc(w_used, 1)


def _constants():
    eye = np.eye(P, dtype=np.float32)
    rot = np.zeros((P, P), np.float32)
    even = np.arange(0, P, 2)
    rot[even + 1, even] = -1.0
    rot[even, even + 1] = 1.0
    forward = np.triu(np.ones((P, P), np.float32))
    backward = np.tril(np.ones((P, P), np.float32))
    consts = np.stack([eye, np.ones((P, P), np.float32), rot, forward, backward,
                       (1 - forward) * np.float32(SKIP), (1 - backward) * np.float32(SKIP)])
    freq = np.float32(10000.0) ** (-np.arange(16, dtype=np.float32) / np.float32(16))
    token = np.arange(TC)
    ang = np.concatenate([(token // 64).astype(np.float32)[:, None] * freq,
                          (token % 64).astype(np.float32)[:, None] * freq], -1)
    ang = np.repeat(ang, 2, axis=1).T
    ang = np.concatenate([ang, ang])
    trig = np.stack([np.cos(ang), np.sin(ang)], 1).astype(np.float32)
    return consts.astype(np.float32), trig


def _stationary(w, cols, k_per_unit):
    k, n = w.shape
    w = w.reshape(k // (P * k_per_unit), k_per_unit, P, n // cols, cols)
    return w.transpose(3, 0, 2, 1, 4).reshape(-1, P, k_per_unit * cols)


def _layout(inp):
    def a(name):
        return np.asarray(inp[name])
    w_in = a("ssd_w_in")[0]
    inner, state_at = 4096, 2 * 4096
    units = [_stationary(w_in[:, 10240:10368], P, 8)]
    for g in range(GROUPS):
        x = w_in[:, inner + g * T:inner + (g + 1) * T]
        bm = w_in[:, state_at + g * P:state_at + (g + 1) * P]
        cm = w_in[:, state_at + 1024 + g * P:state_at + 1024 + (g + 1) * P]
        units += [_stationary(x, P, 8), _stationary(bm, P, 8), _stationary(cm, P, 8),
                  _stationary(w_in[:, g * T:(g + 1) * T], T, 2)]
    units.append(_stationary(a("ssd_w_out")[0], T, 2))
    m_in = a("mla_w_in")[0]
    kr = m_in[:, 1024:1088]
    units += [_stationary(m_in[:, 1088:], P, 8), _stationary(m_in[:, :1024], P, 8),
              _stationary(np.concatenate([kr, kr], 1), P, 8)]
    uq = a("mla_w_uq")[0].reshape(RANK, HEADS, 192)
    ukv = a("mla_w_ukv")[0].reshape(RANK, HEADS, 256)
    for b in range(4):
        h = slice(4 * b, 4 * b + 4)
        units += [_stationary(uq[:, h, :128].reshape(RANK, 512), 256, 4),
                  _stationary(uq[:, h, 128:].reshape(RANK, 256), 256, 4),
                  _stationary(ukv[:, h, :128].reshape(RANK, 512), 256, 4),
                  _stationary(ukv[:, h, 128:].reshape(RANK, 512), T, 2)]
    units.append(_stationary(a("mla_w_o")[0], T, 2))
    stream = np.concatenate(units)
    assert stream.shape == (UNITS, P, UNIT), stream.shape

    ada = np.concatenate([_stationary(a("ada_w")[n], P, KT) for n in range(2)]).reshape(ADA_TILES, P, KT, P)

    def tiles(vec):
        return vec.reshape(-1, P).T

    conv_w, conv_b = a("ssd_conv_w")[0], a("ssd_conv_b")[0]
    par = []
    for g in range(GROUPS):
        cols = np.concatenate([np.arange(g * T, (g + 1) * T), inner + np.arange(g * P, (g + 1) * P),
                               inner + 1024 + np.arange(g * P, (g + 1) * P)])
        par.append(conv_w[:, cols].reshape(TAPS, 6, P).transpose(2, 1, 0).reshape(P, 30))
        par.append(tiles(conv_b[cols]))
    par += [tiles(a("ssd_norm_w")[0]), tiles(a("ada_b")[0]), tiles(a("ada_b")[1]),
            tiles(a("ln_g")[0]), tiles(a("ln_b")[0]), tiles(a("mla_q_norm")[0]), tiles(a("mla_kv_norm")[0]),
            np.stack([tiles(a("c_ctx")), tiles(a("c")[0])], -1).reshape(P, 32)]
    tokens = np.concatenate([a("ctx")[0], a("x")[0]])
    consts, trig = _constants()
    return {
        "stream": stream, "ada": ada, "par": np.concatenate(par, 1), "consts": consts, "trig": trig,
        "x_cm": tokens.T.reshape(KT, P, T).transpose(1, 0, 2), "x_tm": tokens.reshape(NC, P, D),
        "dt_bias": a("ssd_dt_bias")[0].reshape(1, P), "a_log": a("ssd_a_log")[0].reshape(1, P),
        "d_skip": a("ssd_d")[0].reshape(1, 64),
        "ln_rows": np.stack([a("ln_g"), a("ln_b")], 1).reshape(2, 2, 1, D),
    }


def kernel(**inputs):
    import concourse.bacc as bacc
    from concourse.bass_utils import run_bass_kernel_spmd

    nc = bacc.Bacc("TRN2", target_bir_lowering=False, num_devices=1)
    arrays = {f"in_{k}": np.ascontiguousarray(v) for k, v in _layout(inputs).items()}
    hbm = {k[3:]: nc.dram_tensor(k, v.shape, F32, kind="ExternalInput").ap() for k, v in arrays.items()}
    hbm["y"] = nc.dram_tensor("inner_rows", (GROUPS, P, GT, T), F32, kind="Internal").ap()
    hbm["out"] = nc.dram_tensor("out", (1, TC, D), F32, kind="ExternalOutput").ap()
    program(nc, hbm)
    r = run_bass_kernel_spmd(nc, [arrays], core_ids=[0])
    return r.results[0]["out"]
```

```python
from contextlib import ExitStack

import numpy as np
import concourse.bass as bass
from concourse import mybir

F32 = mybir.dt.float32
F32R = mybir.dt.float32r
ALU = mybir.AluOpType
ACT = mybir.ActivationFunctionType
AX = mybir.AxisListType

P = 128
D = 2048
KT = D // P
T = 512
TC = 256
NC = T // P
GROUPS = 8
GT = 4
HG = 8
HD = 64
TAPS = 5
RING = 4
UNIT = 1024
RANK = 512
HEADS = 16
SCALE = (128 + 64) ** -0.5
ALPHA = 4 ** 0.25
LN_EPS = 1e-5
RMS_EPS = 1e-6

DT_UNITS = 2
PROJ_UNITS = 20
WOUT_AT = DT_UNITS + GROUPS * PROJ_UNITS
WOUT_UNITS = 16
EARLY = WOUT_UNITS - 2
EARLY_FROM = 4
MLA_AT = WOUT_AT + 4 * WOUT_UNITS
GATE_UNITS = 32
LATENT_UNITS = 18
HEAD_AT = MLA_AT + GATE_UNITS + LATENT_UNITS
HEAD_UNITS = 7
WO_AT = HEAD_AT + 4 * HEAD_UNITS
WO_UNITS = 8
UNITS = WO_AT + 4 * WO_UNITS
SPLIT_AHEAD = 3

ADA0 = 32
ADA0_RING = 4
ADA0_ON_PE = [t for t in range(ADA0) if t % 8 in (2, 5, 7)]
ADA0_ON_DVE = [t for t in range(ADA0) if t not in ADA0_ON_PE]
ADAL = 64
ADA_K = D // GROUPS
ADA_UNITS = 16
ADA_DOTS = 8

CONV_AT = 0
NORM_AT = CONV_AT + GROUPS * 36
ADA0_AT = NORM_AT + 32
ADAL_AT = ADA0_AT + 32
LNG_AT = ADAL_AT + 64
LNB_AT = LNG_AT + 16
QN_AT = LNB_AT + 16
KVN_AT = QN_AT + 4
COND_AT = KVN_AT + 4
PARS = COND_AT + 32

DT_ROW, WST_ROW, ECS_ROW, ETOT_ROW, A_ROW, D_ROW = 0, 8, 16, 24, 32, 40
TAB_ROWS = 41

LINKS_PER_GROUP = 60
STEPS = [(0, 0), (0, 1), (0, 2), (0, 3), (1, 1), (1, 0), (1, 3), (1, 2)]
DIAG = [0, 1, 3, 2]
READS_STATE = [n for n in range(8) if n not in (0, 4)]
MAKES_STATE = [n for n in range(8) if n not in (3, 7)]
SUM_BANK = [3, 6]
X_BANK = [6, 7, 4, 5]


class Step:

    def __init__(self, eng, sem):
        self.eng, self.sem, self.base, self.n = eng, sem, 0, 0

    def link(self, ins):
        self.n += 1
        ins.then_inc(self.sem, 1)
        self.eng.wait_ge(self.sem, self.base + self.n)

    def enter(self, i, start, per):
        self.base, self.n = i * per + start, 0

    def leave(self, turns, start, per):
        assert self.n == per, f"{self.n} links in a turn"
        self.base, self.n = start + turns * per, 0


def program(nc, hbm):
    with ExitStack() as ctx:
        def sem(name):
            return ctx.enter_context(nc.semaphore(name))

        place = [-(-nc.sbuf_base // 32) * 32]

        def sb(name, shape, dtype=F32):
            t = nc.alloc_sbuf_tensor_at(name, [P] + shape, dtype, offset=place[0])
            place[0] += int(np.prod(shape)) * 4
            place[0] = -(-place[0] // 32) * 32
            assert place[0] <= nc.sbuf_usable_end, (name, place[0])
            return t

        raw = sb("raw", [RING, UNIT])
        w_hi = sb("w_hi", [RING, UNIT], F32R)
        w_lo = sb("w_lo", [RING, UNIT], F32R)
        par = sb("par", [PARS])
        ident = sb("ident", [P])
        ones = sb("ones", [P])
        tri = sb("tri", [2, P], F32R)
        strict = sb("strict", [2, P], F32R)
        cond = sb("cond", [KT, 2])
        mod0 = sb("mod0", [32, 2])
        modl = sb("modl", [64, 2])
        us = sb("us", [KT, 2])
        ub = sb("ub", [KT, 2])
        stat = sb("stat", [64])
        region_u = place[0]
        u_hi = sb("u_hi", [KT, T], F32R)
        u_lo = sb("u_lo", [KT, T], F32R)
        region_l = place[0]

        ada0 = sb("ada0", [ADA0_RING, KT, P])
        cond_rows = sb("cond_rows", [2, D])
        xcm = sb("xcm", [KT, T])
        utmp0 = sb("utmp0", [2, T])
        place[0] = region_l
        ada = sb("ada", [2, 4, ADA_K])
        condg = sb("condg", [2, ADA_K])
        part = sb("part", [ADAL, 2])
        sz = sb("sz", [NC, T])
        region_y = place[0]
        pad = sb("pad", [2, 2, TC + TAPS - 1])
        xbc = sb("xbc", [6, T])
        after_xbc = place[0]
        ccur = sb("ccur", [T])
        xtok = sb("xtok", [NC, T])
        y_t = xtok
        btok = sb("btok", [NC, P])
        cbs = sb("cbs", [2, NC, P])
        am = sb("am", [2, 2, 4, P], F32R)
        em = sb("em", [2, 4, P])
        tmp = sb("tmp", [T])
        xw = sb("xw", [T])
        y = sb("y", [NC, T])
        state = sb("state", [T])
        tab = sb("tab", [TAB_ROWS, 64])
        gt = sb("gt", [TAB_ROWS, HG])
        a_hi = sb("a_hi", [8, HG], F32R)
        a_lo = sb("a_lo", [8, HG], F32R)
        convg = sb("convg", [36])
        normg = sb("normg", [4])
        place[0] = region_u
        y_all = sb("y_all", [2 * KT, T])
        place[0] = region_l
        r_c = sb("r_c", [2, D])
        place[0] = region_y
        yr_hi = sb("yr_hi", [2, 2, T], F32R)
        yr_lo = sb("yr_lo", [2, 2, T], F32R)
        assert place[0] <= after_xbc
        r_x = sb("r_x", [2, D])
        region_rows = place[0]
        gate0 = sb("gate0", [2, D])
        wtmp = sb("wtmp", [2, T])
        place[0] = region_rows
        rows0 = sb("rows0", [2, D])
        utmp1 = sb("utmp1", [2, T])
        bn = sb("bn", [NC, 24])
        place[0] = region_l
        sq = sb("sq", [2, T])
        rsd = sb("rsd", [2, T])
        gate1 = sb("gate1", [D])
        gates = sb("gates", [HEADS, TC])
        kr = sb("kr", [T])
        assert place[0] <= region_y + 16384
        place[0] = region_rows
        cq = sb("cq", [4, TC])
        ckv = sb("ckv", [4, T])
        cq_hi = sb("cq_hi", [4, TC], F32R)
        cq_lo = sb("cq_lo", [4, TC], F32R)
        ckv_hi = sb("ckv_hi", [4, T], F32R)
        ckv_lo = sb("ckv_lo", [4, T], F32R)
        trig = sb("trig", [2, TC])
        rot = sb("rot", [P])
        place[0] = region_u
        og_hi = sb("og_hi", [HEADS, TC], F32R)
        og_lo = sb("og_lo", [HEADS, TC], F32R)
        region_h = place[0]
        qn = sb("qn", [4, TC])
        qr = sb("qr", [2, TC])
        qrt = sb("qrt", [2, TC])
        kn = sb("kn", [4, T])
        v = sb("v", [NC, T])
        prob = sb("prob", [2, T])
        prob_t = sb("prob_t", [NC, TC])
        place[0] = region_h
        rows1 = sb("rows1", [2, D])

        ps = ctx.enter_context(nc.psum_tensor("ps", [P, 8, T], F32))

        par_loaded, const_loaded, xcm_loaded, rows_loaded = (
            sem("par_loaded"), sem("const_loaded"), sem("xcm_loaded"), sem("rows_loaded"))
        tri_loaded = sem("tri_loaded")
        raw_loaded = [sem(f"raw_loaded{q}") for q in range(RING)]
        ada0_loaded = [sem(f"ada0_loaded{q}") for q in range(ADA0_RING)]
        ada_loaded = [sem(f"ada_loaded{q}") for q in range(2)]
        hi_ready, lo_ready, w_used = sem("hi_ready"), sem("lo_ready"), sem("w_used")
        ada0_pe, ada0_dve, ada_used = sem("ada0_pe"), sem("ada0_dve"), sem("ada_used")
        condg_loaded, condg_ready, am_ready = sem("condg_loaded"), sem("condg_ready"), sem("am_ready")
        rot_loaded = sem("rot_loaded")
        cond_loaded, cond_ready = sem("cond_loaded"), sem("cond_ready")
        consts_ready = sem("consts_ready")
        utmp_ready, uhi_ready, u_ready = sem("utmp_ready"), sem("uhi_ready"), sem("u_ready")
        dt_full, dt_taken, dt_abs, dt_exp, a_ready = (
            sem("dt_full"), sem("dt_taken"), sem("dt_abs"), sem("dt_exp"), sem("a_ready"))
        arow_exp = sem("arow_exp")
        cs_full, cs_diff, cs_exp, tab_ready = sem("cs_full"), sem("cs_diff"), sem("cs_exp"), sem("tab_ready")
        pads_clear, tile_full, tile_evac, pad_ready = (
            sem("pads_clear"), sem("tile_full"), sem("tile_evac"), sem("pad_ready"))
        conv_done, silu_done = sem("conv_done"), sem("silu_done")
        xt_full, xtok_ready, bt_full, btok_ready = (
            sem("xt_full"), sem("xtok_ready"), sem("bt_full"), sem("btok_ready"))
        cb_full, cbs_ready, slice_ready = sem("cb_full"), sem("cbs_ready"), sem("slice_ready")
        seg_full, decay_ready, m_ready, xdt_ready, xw_ready = (
            sem("seg_full"), sem("decay_ready"), sem("m_ready"), sem("xdt_ready"), sem("xw_ready"))
        yd_full, yd_taken, yo_full, yo_taken = (
            sem("yd_full"), sem("yd_taken"), sem("yo_full"), sem("yo_taken"))
        st_full, state_ready = sem("st_full"), sem("state_ready")
        gated, sq_done, var_ready, root_ready, y_normed = (
            sem("gated"), sem("sq_done"), sem("var_ready"), sem("root_ready"), sem("y_normed"))
        ada_taken = sem("ada_taken")
        yt_full, yt_evac, y_spilled = sem("yt_full"), sem("yt_evac"), sem("y_spilled")
        y_loaded, res_loaded = [sem(f"y_loaded{g}") for g in range(GROUPS - 1)], sem("res_loaded")
        g0_full, g0_taken, g0_taken_act = sem("g0_full"), sem("g0_taken"), sem("g0_taken_act")
        yhi_ready, ylo_ready, wo_full, wo_taken = (
            sem("yhi_ready"), sem("ylo_ready"), sem("wo_full"), sem("wo_taken"))
        rows0_loaded, lnvar_ready, lnroot_ready, ln_ready = (
            sem("rows0_loaded"), sem("lnvar_ready"), sem("lnroot_ready"), sem("ln_ready"))
        rt_full, rt_taken = sem("rt_full"), sem("rt_taken")
        x1_ready, trig_loaded = sem("x1_ready"), sem("trig_loaded")
        g1_full, g1_taken = sem("g1_full"), sem("g1_taken")
        gt_full, gt_taken = sem("gt_full"), sem("gt_taken")
        lat_full, lat_taken, sq_ready, sq_used = (
            sem("lat_full"), sem("lat_taken"), sem("sq_ready"), sem("sq_used"))
        ms_full, msv_ready, msroot_ready, cn_ready, chi_ready, clo_ready = (
            sem("ms_full"), sem("msv_ready"), sem("msroot_ready"), sem("cn_ready"),
            sem("chi_ready"), sem("clo_ready"))
        kr_full, kr_ready, krot_full = sem("kr_full"), sem("kr_ready"), sem("krot_full")
        hq_full, hq_act, hq_dve = sem("hq_full"), sem("hq_act"), sem("hq_dve")
        qrot_full, qr_ready = sem("qrot_full"), sem("qr_ready")
        s_full, max_ready, p_ready, p_scaled = (
            sem("s_full"), sem("max_ready"), sem("p_ready"), sem("p_scaled"))
        pt_full, pt_ready, o_full, o_taken, ogh_ready, ogl_ready = (
            sem("pt_full"), sem("pt_ready"), sem("o_full"), sem("o_taken"),
            sem("ogh_ready"), sem("ogl_ready"))
        out_taken, rows1_loaded, fvar_ready, froot_ready, out_ready, stored = (
            sem("out_taken"), sem("rows1_loaded"), sem("fvar_ready"), sem("froot_ready"),
            sem("out_ready"), sem("stored"))
        dve_step, act_step = sem("dve_step"), sem("act_step")

        block = ctx.enter_context(nc.Block())

        @block.sync
        def _(sp):
            def load_unit(s, slot, first=False):
                if not first:
                    sp.wait_ge(lo_ready, s - RING + 1)
                sp.dma_start(raw[:, slot, :], hbm["stream"][s]).then_inc(raw_loaded[slot], 16)

            sp.dma_start(par[:], hbm["par"]).then_inc(par_loaded, 16)
            sp.dma_start(cond_rows[:], hbm["cond_rows"].to_broadcast([P, 2, D])).then_inc(cond_loaded, 16)
            for t in range(ADA0):
                if t >= ADA0_RING:
                    if t - ADA0_RING in ADA0_ON_PE:
                        sp.wait_ge(ada0_pe, ADA0_ON_PE.index(t - ADA0_RING) + 1)
                    else:
                        sp.wait_ge(ada0_dve, ADA0_ON_DVE.index(t - ADA0_RING) + 1)
                sp.dma_start(ada0[:, t % ADA0_RING], hbm["ada0"][t].rearrange("p (k n) -> p k n", k=KT)).then_inc(
                    ada0_loaded[t % ADA0_RING], 16)
                if t == 3:
                    sp.dma_start(xcm[:], hbm["x_cm"]).then_inc(xcm_loaded, 16)
                    for n, c in enumerate((ident, ones)):
                        sp.dma_start(c[:], hbm["consts"][n]).then_inc(const_loaded, 16)
                    sp.dma_start(utmp0[:, 0, :].rearrange("p (a b) -> p a b", a=4),
                                 hbm["consts"][3:7].rearrange("a p b -> p a b")).then_inc(tri_loaded, 16)
            for s in range(RING):
                load_unit(s, s, first=True)
            sp.wait_ge(u_ready, KT)
            sp.dma_start(y[:, 0, 0:128], hbm["dt_bias"].to_broadcast([P, 128])).then_inc(rows_loaded, 16)
            sp.dma_start(y[:, 1, 0:128], hbm["a_log"].to_broadcast([P, 128])).then_inc(rows_loaded, 16)
            sp.dma_start(tab[:, D_ROW, :], hbm["d_skip"].to_broadcast([P, 64])).then_inc(rows_loaded, 16)
            for s in range(RING, DT_UNITS + PROJ_UNITS):
                load_unit(s, s % RING)

            def load_ada(g, n):
                for u in (2 * n, 2 * n + 1):
                    if u >= 2:
                        sp.wait_ge(ada_used, g * ADA_UNITS * ADA_DOTS + (u - 1) * ADA_DOTS)
                    elif not isinstance(g, int) or g > 0:
                        sp.wait_ge(ada_used, g * ADA_UNITS * ADA_DOTS + (u - 1) * ADA_DOTS)
                    sp.dma_start(ada[:, u % 2], hbm["ada"][g * ADA_UNITS + u]).then_inc(ada_loaded[u % 2], 16)

            def load_cond(g):
                if not isinstance(g, int) or g > 0:
                    sp.wait_ge(ada_used, g * ADA_UNITS * ADA_DOTS)
                sp.dma_start(condg[:], hbm["cond_groups"][g].to_broadcast([P, 2, ADA_K])).then_inc(condg_loaded, 16)

            def load_group(g):
                for j in range(PROJ_UNITS):
                    load_unit(DT_UNITS + PROJ_UNITS * (g + 1) + j, (DT_UNITS + j) % RING)
                    if j == 6:
                        load_cond(g)
                    if j % 2 == 0 and j >= 8:
                        load_ada(g, j // 2 - 4)
                load_ada(g, 6)
                load_ada(g, 7)

            load_group(0)
            with sp.Fori(1, GROUPS - 1) as i:
                load_group(i)
            for s in range(WOUT_AT, WOUT_AT + RING):
                load_unit(s, s % RING)
            sp.wait_ge(w_used, WOUT_AT)
            for g in range(GROUPS - 1):
                if g == GROUPS - 2:
                    sp.wait_ge(y_spilled, 16 * (GROUPS - 1))
                elif g == 0:
                    sp.wait_ge(y_spilled, 16 * (GROUPS - 2))
                sp.dma_start(y_all[:, g * GT:g * GT + GT, :], hbm["y"][g]).then_inc(y_loaded[g], 16)
            load_cond(GROUPS - 1)
            load_ada(GROUPS - 1, 0)
            for j in range(RING, PROJ_UNITS):
                load_unit(WOUT_AT + j, (WOUT_AT + j) % RING)
                if j % 2 == 0 and j < 18:
                    load_ada(GROUPS - 1, j // 2 - 1)
            late = WOUT_AT + PROJ_UNITS
            sp.wait_ge(y_normed, GROUPS)
            sp.wait_ge(ada_taken, GROUPS)
            for n, rows in enumerate((r_c, r_x)):
                sp.dma_start(rows[:], hbm["x_tm"][2 * n:2 * n + 2].rearrange("c p n -> p c n")).then_inc(
                    res_loaded, 16)
            with sp.Fori(0, (MLA_AT + RING - late) // RING) as i:
                for q in range(RING):
                    load_unit(i * RING + (late + q), (late + q) % RING)
            sp.wait_ge(wo_taken, NC * 4)
            for n in range(2):
                sp.dma_start(rows0[:, n, :], hbm["ln_rows"][0, n].to_broadcast([P, D])).then_inc(rows0_loaded, 16)
            sp.dma_start(trig[:], hbm["trig"]).then_inc(trig_loaded, 16)
            sp.dma_start(rot[:], hbm["consts"][2]).then_inc(rot_loaded, 16)
            with sp.Fori(0, (UNITS - MLA_AT - RING) // RING - 1) as i:
                for q in range(RING):
                    load_unit(i * RING + (MLA_AT + RING + q), (MLA_AT + q) % RING)
            sp.wait_ge(ogl_ready, HEADS)
            for n in range(2):
                sp.dma_start(rows1[:, n, :], hbm["ln_rows"][1, n].to_broadcast([P, D])).then_inc(rows1_loaded, 16)
            for s in range(MLA_AT + RING * ((UNITS - MLA_AT - RING) // RING), UNITS):
                load_unit(s, s % RING)
            for c in range(2):
                sp.wait_ge(out_ready, c + 1)
                sp.dma_start(hbm["out"][0, c * P:c * P + P, :], r_x[:, c]).then_inc(stored, 16)
            sp.wait_ge(stored, 32)

        @block.gpsimd
        def _(pool):
            def low(s, slot):
                pool.wait_ge(hi_ready, s + 1)
                nc.gpsimd.tensor_tensor(w_lo[:, slot], raw[:, slot], w_hi[:, slot].bitcast(F32),
                                        ALU.subtract).then_inc(lo_ready, 1)

            ahead = DT_UNITS + PROJ_UNITS + SPLIT_AHEAD
            for s in range(ahead):
                low(s, s % RING)

            def group(g, proj):
                for j in range(PROJ_UNITS):
                    h, odd = divmod(j, 2)
                    if odd and h < 8:
                        c = DIAG[h // 2]
                        pool.wait_ge(slice_ready, g + 1)
                        pool.wait_ge(seg_full, g * 8 + h)
                        for n, a in enumerate((a_hi, a_lo)):
                            for d in range(2):
                                heads = a[:, 2 * c + d, h % 2 * 4:h % 2 * 4 + 4].bitcast(F32)
                                ins = nc.gpsimd.tensor_tensor(
                                    am[:, n, d], tri[:, d].bitcast(F32).unsqueeze(1).to_broadcast([P, 4, P]),
                                    heads.unsqueeze(2).to_broadcast([P, 4, P]), ALU.mult)
                        ins.then_inc(am_ready, 1)
                    if proj:
                        low(g * PROJ_UNITS + (ahead + j), (ahead + j) % RING)
                    elif 0 <= j - EARLY_FROM < EARLY:
                        s = WOUT_AT + SPLIT_AHEAD + j - EARLY_FROM
                        low(s, s % RING)

            pool.wait_ge(consts_ready, 1)
            group(0, True)
            with pool.Fori(1, GROUPS - 1) as i:
                group(i, True)
            group(GROUPS - 1, False)
            at = WOUT_AT + SPLIT_AHEAD + EARLY
            with pool.Fori(0, (UNITS - at) // RING) as i:
                for q in range(RING):
                    low(i * RING + (at + q), (at + q) % RING)
            for s in range(UNITS - (UNITS - at) % RING, UNITS):
                low(s, s % RING)

        @block.scalar
        def _(act):
            step = Step(act, act_step)

            def split_high(s, slot, turn=None, first=False):
                act.wait_ge(raw_loaded[slot], 16 * turn)
                if not first:
                    act.wait_ge(w_used, s - RING + 1)
                nc.scalar.activation(w_hi[:, slot], raw[:, slot], ACT.Copy).then_inc(hi_ready, 1)

            def split_at(base, off, n):
                s = base + off
                split_high(s if n is None else n * RING + s, s % RING,
                           turn=(s // RING + 1) if n is None else n + (s // RING + 1),
                           first=n is None and s < RING)

            act.wait_ge(par_loaded, 16)
            nc.scalar.activation(cond[:], par[:, COND_AT:COND_AT + 32].rearrange("p (k v) -> p k v", v=2),
                                 ACT.Silu).then_inc(cond_ready, 1)
            act.wait_ge(cond_loaded, 16)
            nc.scalar.activation(cond_rows[:], cond_rows[:], ACT.Silu).then_inc(cond_ready, 1)
            for s in range(SPLIT_AHEAD):
                split_at(0, s, None)
            for k in range(KT):
                act.wait_ge(utmp_ready, k + 1)
                nc.scalar.activation(u_hi[:, k], utmp0[:, k % 2], ACT.Copy).then_inc(uhi_ready, 1)
            split_at(0, SPLIT_AHEAD, None)
            split_at(1, SPLIT_AHEAD, None)
            act.wait_ge(rows_loaded, 48)
            nc.scalar.activation(y[:, 2, 0:128], y[:, 1, 0:128], ACT.Exp).then_inc(arow_exp, 1)
            act.wait_ge(dt_abs, 1)
            nc.scalar.activation(xw[:], y[:, 3], ACT.Exp, scale=-1.0).then_inc(dt_exp, 1)

            def evac_tile(g, t):
                act.wait_ge(w_used, DT_UNITS + PROJ_UNITS * g + 2 * t + 2)
                if not (isinstance(g, int) and g == 0 and t < 2):
                    act.wait_ge(conv_done, 6 * g + t - 1)
                else:
                    act.wait_ge(pads_clear, 1)
                nc.scalar.activation(pad[:, t % 2, :, 2:2 + TC],
                                     ps[:, t % 4].rearrange("p (s n) -> p s n", s=2),
                                     ACT.Copy).then_inc(tile_evac, 1)

            def silu_tiles(g):
                for t in range(6):
                    act.wait_ge(conv_done, 6 * g + t + 1)
                    nc.scalar.activation(xbc[:, t], xbc[:, t], ACT.Silu).then_inc(silu_done, 1)

            def silu_z(g):
                for c in range(NC):
                    act.wait_ge(w_used, DT_UNITS + PROJ_UNITS * (g + 1))
                    nc.scalar.activation(sz[:, c], ps[:, c], ACT.Silu).then_inc(tile_evac, 1)

            for j in range(PROJ_UNITS):
                split_at(DT_UNITS, j + SPLIT_AHEAD, None)
                if j % 2 == 0 and 2 <= j < 14:
                    evac_tile(0, j // 2 - 1)
                if j == 5:
                    act.wait_ge(cs_diff, 1)
                    nc.scalar.activation(tab[:, ECS_ROW:ECS_ROW + 8].rearrange("p r h -> p (r h)"), ps[:, 5], ACT.Exp).then_inc(cs_exp, 1)
                    nc.scalar.activation(tab[:, ETOT_ROW:ETOT_ROW + 8].rearrange("p r h -> p (r h)"), ps[:, 6], ACT.Exp).then_inc(cs_exp, 1)
                    nc.scalar.activation(xw[:], xw[:], ACT.Exp).then_inc(cs_exp, 1)
            silu_tiles(0)
            silu_z(0)

            def y_high(u):
                u = u % WOUT_UNITS
                nc.scalar.activation(yr_hi[:, u % 2], y_all[:, 2 * u:2 * u + 2], ACT.Copy).then_inc(yhi_ready, 1)

            def group(g, proj):
                for j in range(PROJ_UNITS):
                    if not proj and j == EARLY_FROM - 1:
                        act.wait_ge(bt_full, GROUPS)
                        act.wait_ge(cbs_ready, GROUPS)
                        act.wait_ge(y_loaded[0], 16)
                        y_high(0)
                    if not proj and 0 <= j - EARLY_FROM < EARLY:
                        u = j - EARLY_FROM
                        s = WOUT_AT + u + SPLIT_AHEAD
                        split_high(s, s % RING, turn=s // RING + 1)
                        if u + 1 < EARLY:
                            act.wait_ge(y_loaded[(u + 1) // 2], 16)
                            y_high(u + 1)
                    if proj:
                        s = DT_UNITS + PROJ_UNITS + j + SPLIT_AHEAD
                        act.wait_ge(raw_loaded[s % RING], 16 * (s // RING + 1) + g * 16 * (PROJ_UNITS // RING))
                        act.wait_ge(w_used, g * PROJ_UNITS + (s - RING + 1))
                        nc.scalar.activation(w_hi[:, s % RING], raw[:, s % RING], ACT.Copy).then_inc(hi_ready, 1)
                        if j % 2 == 0 and 2 <= j < 14:
                            evac_tile(g + 1, j // 2 - 1)
                    if j == 1:
                        for c in range(NC):
                            act.wait_ge(xt_full, NC * g + c + 1)
                            act.wait_ge(y_spilled, 16 * g)
                            act.wait_ge(gated, NC * g)
                            nc.scalar.activation(xtok[:, c], ps[:, X_BANK[c]], ACT.Copy).then_inc(xtok_ready, 1)
                    if j == 2:
                        act.wait_ge(bt_full, g + 1)
                        act.wait_ge(st_full, 6 * g)
                        nc.scalar.activation(btok[:].rearrange("p c n -> p (c n)"), ps[:, 6], ACT.Copy).then_inc(btok_ready, 1)
                    if j == 3:
                        act.wait_ge(condg_loaded, 16 * g + 16)
                        nc.scalar.activation(condg[:], condg[:], ACT.Silu).then_inc(condg_ready, 1)
                    if j % 2 == 0 and 2 <= j < 18:
                        h = j // 2 - 1
                        act.wait_ge(seg_full, 8 * g + h + 1)
                        act.wait_ge(yd_full, 8 * g + max(h - 1, 0))
                        nc.scalar.activation(em[:, h % 2].rearrange("p a n -> p (a n)"), ps[:, 4 + h % 2],
                                             ACT.Exp).then_inc(decay_ready, 1)
                    if j in (13, 15, 17, 19):
                        m = (j - 13) // 2
                        c = STEPS[4 + m][1]
                        act.wait_ge(gated, NC * g + m + 1)
                        nc.scalar.activation(sz[:, c], y[:, c], ACT.Square,
                                             accum_out=stat[:, c:c + 1]).then_inc(sq_done, 1)
                act.wait_ge(var_ready, g + 1)
                nc.scalar.activation(stat[:, 8:12], stat[:, 4:8], ACT.Sqrt).then_inc(root_ready, 1)
                if proj:
                    silu_tiles(g + 1)
                    silu_z(g + 1)
                for k in range(GT):
                    act.wait_ge(yt_full, GT * g + k + 1)
                    dst = y_t[:, k] if proj else y_all[:, GT * g + k]
                    nc.scalar.activation(dst, ps[:, 4 + k], ACT.Copy, scale=normg[:, k:k + 1]).then_inc(yt_evac, 1)
                if proj:
                    act.wait_ge(yt_evac, GT * g + GT)
                    act.dma_start(hbm["y"][g], y_t[:]).then_inc(y_spilled, 16)

            group(0, True)
            with act.Fori(1, GROUPS - 1) as i:
                group(i, True)
            group(GROUPS - 1, False)

            act.wait_ge(yt_evac, GT * GROUPS)
            y_high(EARLY)
            for b in range(4):
                act.wait_ge(g0_full, b + 1)
                nc.scalar.activation(gate0[:, 0, b * T:b * T + T], ps[:, 4 + b], ACT.Copy).then_inc(g0_taken_act, 1)
            for u in range(EARLY, WOUT_UNITS):
                s = WOUT_AT + u + SPLIT_AHEAD
                split_high(s, s % RING, turn=s // RING + 1)
                y_high(u + 1)
            with act.Fori(0, 3) as i:
                for u in range(WOUT_UNITS):
                    s = WOUT_AT + WOUT_UNITS + u + SPLIT_AHEAD
                    split_high(i * WOUT_UNITS + s, s % RING, turn=i * (WOUT_UNITS // RING) + (s // RING + 1))
                    y_high(u + 1)

            act.wait_ge(lnvar_ready, 1)
            nc.scalar.activation(stat[:, 20:24], stat[:, 16:20], ACT.Sqrt).then_inc(lnroot_ready, 1)
            for k in range(KT):
                act.wait_ge(utmp_ready, KT + k + 1)
                nc.scalar.activation(u_hi[:, k], utmp1[:, k % 2], ACT.Copy).then_inc(uhi_ready, 1)

            with act.Fori(0, 4) as i:
                for t in range(4):
                    for half in range(2):
                        s = MLA_AT + 2 * t + half + SPLIT_AHEAD
                        split_high(i * 8 + s, s % RING, turn=i * 2 + (s // RING + 1))
                    act.wait_ge(w_used, i * 8 + (MLA_AT + 2 * t + 2))
                    nc.scalar.activation(gates[:, bass.ds(i * 4 + t, 1), :].rearrange("p a n -> p (a n)"),
                                         ps[:, t, 0:TC], ACT.Silu).then_inc(gt_taken, 1)
            lat = MLA_AT + GATE_UNITS
            for j in range(LATENT_UNITS):
                s = lat + j + SPLIT_AHEAD
                split_high(s, s % RING, turn=s // RING + 1)
                if j % 2 == 1:
                    t = j // 2
                    act.wait_ge(w_used, lat + j + 1)
                    if t == 0:
                        act.wait_ge(x1_ready, 1)
                    if t < 4:
                        src, dst = ps[:, 4 + t, 0:TC], cq[:, t]
                    elif t < 8:
                        src, dst = ps[:, t - 4], ckv[:, t - 4]
                    else:
                        src, dst = ps[:, 4], kr[:]
                    nc.scalar.activation(dst, src, ACT.Copy).then_inc(lat_taken, 1)
                    if t < 8:
                        if t >= 2:
                            act.wait_ge(sq_used, t - 1)
                        n = TC if t < 4 else T
                        nc.scalar.activation(sq[:, t % 2, 0:n], src, ACT.Square).then_inc(sq_ready, 1)
            for m in range(2):
                act.wait_ge(msv_ready, m + 1)
                n = (TC, T)[m]
                nc.scalar.activation(rsd[:, m, 0:n], rsd[:, m, 0:n], ACT.Sqrt).then_inc(msroot_ready, 1)
            for t in range(8):
                act.wait_ge(cn_ready, t + 1)
                src, dst = (cq[:, t], cq_hi[:, t]) if t < 4 else (ckv[:, t - 4], ckv_hi[:, t - 4])
                nc.scalar.activation(dst, src, ACT.Copy).then_inc(chi_ready, 1)

            for b in range(4):
                for j in range(HEAD_UNITS):
                    s = HEAD_AT + b * HEAD_UNITS + j + SPLIT_AHEAD
                    split_high(s, s % RING, turn=s // RING + 1)
                    if j < 2:
                        act.wait_ge(w_used, s - SPLIT_AHEAD + 1)
                        act.wait_ge(s_full, 8 * b)
                        nc.scalar.activation(qn[:, 2 * j:2 * j + 2].rearrange("p a n -> p (a n)"), ps[:, j], ACT.Copy).then_inc(hq_act, 1)
                    if j in (3, 4):
                        act.wait_ge(w_used, s - SPLIT_AHEAD + 1)
                        for n in range(2):
                            nc.scalar.activation(kn[:, 2 * (j - 3) + n], ps[:, 3 + 2 * (j - 3) + n], ACT.Copy).then_inc(hq_act, 1)
                act.wait_ge(w_used, HEAD_AT + HEAD_UNITS * (b + 1))
                act.wait_ge(o_full, 4 * b)
                for n in range(2):
                    nc.scalar.activation(v[:, n], ps[:, n], ACT.Copy).then_inc(hq_act, 1)

                def exp_scores(n):
                    m = 8 * b + n
                    act.wait_ge(max_ready, m + 1)
                    if m >= 2:
                        act.wait_ge(pt_full, m - 1)
                    nc.scalar.activation(prob[:, n % 2], ps[:, 4 + n % 2], ACT.Exp, bias=stat[:, 32 + n:33 + n],
                                         scale=SCALE, accum_out=stat[:, 40 + n:41 + n]).then_inc(p_ready, 1)

                def gated_high(hh):
                    act.wait_ge(o_taken, 4 * b + hh + 1)
                    nc.scalar.activation(og_hi[:, 4 * b + hh], sq[:, hh % 2, 0:TC], ACT.Copy).then_inc(ogh_ready, 1)

                for n in range(8):
                    exp_scores(n)
                    if n % 2 == 1 and n >= 3:
                        gated_high(n // 2 - 1)
                gated_high(3)

            with act.Fori(0, 3) as i:
                for u in range(WO_UNITS):
                    s = WO_AT + u + SPLIT_AHEAD
                    split_high(i * WO_UNITS + s, s % RING, turn=i * (WO_UNITS // RING) + (s // RING + 1))
            for s in range(WO_AT + 3 * WO_UNITS + SPLIT_AHEAD, UNITS):
                split_high(s, s % RING, turn=s // RING + 1)
            act.wait_ge(fvar_ready, 1)
            nc.scalar.activation(stat[:, 28:30], stat[:, 24:26], ACT.Sqrt).then_inc(froot_ready, 1)

        @block.vector
        def _(dve):
            step = Step(dve, dve_step)
            link = step.link
            vec = nc.vector

            dve.wait_ge(const_loaded, 32)
            dve.wait_ge(tri_loaded, 16)
            dve.wait_ge(par_loaded, 16)
            link(vec.tensor_copy(tri[:].rearrange("p a b -> p (a b)"), utmp0[:, 0, 0:256]))
            link(vec.tensor_copy(strict[:].rearrange("p a b -> p (a b)"), utmp0[:, 0, 256:512]))
            vec.memset(stat[:], 0.0).then_inc(consts_ready, 1)

            dve.wait_ge(cond_ready, 2)
            flat_w = lambda ap: ap.rearrange("p k n -> p (k n)")
            for t in ADA0_ON_DVE:
                dve.wait_ge(ada0_loaded[t % ADA0_RING], 16 * (t // ADA0_RING + 1))
                for s in range(2):
                    ins = vec.scalar_tensor_tensor(
                        out=flat_w(ps[:, 0:4]), in0=flat_w(ada0[:, t % ADA0_RING]), scalar=1.0,
                        in1=cond_rows[:, s], op0=ALU.mult, op1=ALU.mult, accum_out=mod0[:, t, s:s + 1])
                    if s == 0:
                        link(ins)
                ins.then_inc(ada0_dve, 1)
                dve.wait_ge(ada0_dve, ADA0_ON_DVE.index(t) + 1)
            dve.wait_ge(ada0_pe, len(ADA0_ON_PE))
            for t in ADA0_ON_PE:
                ins = vec.tensor_copy(mod0[:, t], ps[:, 7, 2 * t:2 * t + 2])
            link(ins)
            link(vec.tensor_tensor(mod0[:], mod0[:],
                                   par[:, ADA0_AT:ADA0_AT + 32].unsqueeze(2).to_broadcast([P, 32, 2]), ALU.add))
            link(vec.tensor_copy(modl[:], par[:, ADAL_AT:ADAL_AT + ADAL].unsqueeze(2).to_broadcast([P, ADAL, 2])))
            link(vec.tensor_scalar(mod0[:, 16:32], mod0[:, 16:32], 1.0, None, ALU.add))

            def modulate(n, k, dst, src, scale, shift):
                if n >= 2:
                    dve.wait_ge(u_ready, n - 1)
                for s in range(2):
                    ins = vec.tensor_scalar(dst[:, s * TC:s * TC + TC], src[:, s * TC:s * TC + TC],
                                            scale[:, s:s + 1], shift[:, s:s + 1], ALU.mult, ALU.add)
                    if s == 0:
                        link(ins)
                return ins.then_inc(utmp_ready, 1)

            def low_u(n, k, src):
                dve.wait_ge(uhi_ready, n + 1)
                vec.tensor_tensor(u_lo[:, k], src, u_hi[:, k].bitcast(F32), ALU.subtract).then_inc(u_ready, 1)

            dve.wait_ge(xcm_loaded, 16)
            for k in range(KT):
                modulate(k, k, utmp0[:, k % 2], xcm[:, k], mod0[:, 16 + k], mod0[:, k])
                if k:
                    low_u(k - 1, k - 1, utmp0[:, (k - 1) % 2])
            low_u(KT - 1, KT - 1, utmp0[:, (KT - 1) % 2])
            dve.wait_ge(u_ready, KT)
            link(vec.memset(pad[:, :, :, 0:2], 0.0))
            vec.memset(pad[:, :, :, 2 + TC:4 + TC], 0.0).then_inc(pads_clear, 1)

            chunks = lambda ap: ap.rearrange("p (c h) -> p c h", c=NC)
            dve.wait_ge(w_used, DT_UNITS)
            dve.wait_ge(rows_loaded, 48)
            link(vec.tensor_tensor(chunks(tmp[:]), ps[:, 0:4, 0:128],
                                   y[:, 0, 0:128].unsqueeze(1).to_broadcast([P, NC, 128]), ALU.add))
            vec.scalar_tensor_tensor(out=y[:, 3], in0=tmp[:], scalar=-1.0, in1=tmp[:], op0=ALU.mult,
                                     op1=ALU.max).then_inc(dt_abs, 1)
            dve.wait_ge(dt_exp, 1)
            link(vec.tensor_scalar(y[:, 3], xw[:], 2.0, None, ALU.add))
            link(vec.reciprocal(y[:, 3], y[:, 3]))
            link(vec.tensor_tensor(y[:, 3], y[:, 3], xw[:], ALU.mult))
            link(vec.tensor_tensor(xw[:], y[:, 3], y[:, 3], ALU.mult))
            link(vec.tensor_scalar(state[:], xw[:], 1.0 / 15.0, None, ALU.mult))
            for m in (13, 11, 9, 7, 5, 3):
                link(vec.scalar_tensor_tensor(out=state[:], in0=state[:], scalar=1.0 / m, in1=xw[:],
                                              op0=ALU.add, op1=ALU.mult))
            link(vec.scalar_tensor_tensor(out=state[:], in0=state[:], scalar=1.0, in1=y[:, 3],
                                          op0=ALU.add, op1=ALU.mult))
            link(vec.tensor_scalar(tmp[:], tmp[:], 0.0, None, ALU.max))
            flat = lambda r: tab[:, r:r + 8].rearrange("p r h -> p (r h)")
            link(vec.scalar_tensor_tensor(out=flat(DT_ROW), in0=state[:], scalar=2.0, in1=tmp[:],
                                          op0=ALU.mult, op1=ALU.add))
            dve.wait_ge(arow_exp, 1)
            link(vec.tensor_tensor(chunks(flat(A_ROW)), chunks(flat(DT_ROW)),
                                   y[:, 2, 0:128].unsqueeze(1).to_broadcast([P, NC, 128]), ALU.mult))
            vec.tensor_scalar(flat(A_ROW), flat(A_ROW), -1.0, None, ALU.mult).then_inc(a_ready, 1)
            dve.wait_ge(cs_full, 1)
            link(vec.tensor_scalar(state[:], ps[:, 5], -1.0, None, ALU.mult))
            vec.tensor_tensor(xw[:], ps[:, 6], state[:], ALU.add).then_inc(cs_diff, 1)
            dve.wait_ge(cs_exp, 3)
            link(vec.tensor_tensor(flat(WST_ROW), xw[:], flat(DT_ROW), ALU.mult))

            def conv_weights(g_next):
                if isinstance(g_next, int):
                    src = par[:, CONV_AT + 36 * g_next:CONV_AT + 36 * g_next + 36]
                else:
                    src = par[:, bass.ds(g_next * 36 + CONV_AT, 36)]
                link(vec.tensor_copy(convg[:], src))

            def conv(g, t):
                out = xbc[:, t].rearrange("p (s n) -> p s n", s=2)
                dve.wait_ge(tile_evac, 10 * g + t + 1)
                if not (isinstance(g, int) and g == 0):
                    dve.wait_ge(xt_full, NC * g)
                    dve.wait_ge(bt_full, g)
                    dve.wait_ge(cb_full, g)
                link(vec.tensor_scalar(out, pad[:, t % 2, :, 0:TC], convg[:, 5 * t:5 * t + 1],
                                       convg[:, 30 + t:31 + t], ALU.mult, ALU.add))
                for j in range(1, TAPS):
                    ins = vec.scalar_tensor_tensor(out=out, in0=pad[:, t % 2, :, j:j + TC],
                                                   scalar=convg[:, 5 * t + j:5 * t + j + 1], in1=out,
                                                   op0=ALU.mult, op1=ALU.add)
                    if j < TAPS - 1:
                        link(ins)
                ins.then_inc(conv_done, 1)

            conv_weights(0)
            for t in range(6):
                conv(0, t)

            def y_low(count, u):
                dve.wait_ge(yhi_ready, count)
                u = u % WOUT_UNITS
                vec.tensor_tensor(yr_lo[:, u % 2], y_all[:, 2 * u:2 * u + 2], yr_hi[:, u % 2].bitcast(F32),
                                  ALU.subtract).then_inc(ylo_ready, 1)

            def group(g, proj):
                if isinstance(g, int):
                    src = tab[:, :, g * HG:g * HG + HG]
                    nsrc = par[:, NORM_AT + GT * g:NORM_AT + GT * g + GT]
                else:
                    src = tab[:, :, bass.ds(g * HG, HG)]
                    nsrc = par[:, bass.ds(g * GT + NORM_AT, GT)]
                dve.wait_ge(am_ready, 8 * g)
                link(vec.tensor_copy(gt[:], src))
                link(vec.tensor_copy(a_hi[:], gt[:, A_ROW:A_ROW + 8]))
                vec.tensor_tensor(a_lo[:], gt[:, A_ROW:A_ROW + 8], a_hi[:].bitcast(F32),
                                  ALU.subtract).then_inc(slice_ready, 1)
                dve.wait_ge(yt_evac, GT * g)
                link(vec.tensor_copy(normg[:], nsrc))
                if proj:
                    conv_weights(g + 1)
                dve.wait_ge(ada_taken, g)

                dve.wait_ge(cb_full, g + 1)
                for d in range(2):
                    ins = vec.tensor_tensor(cbs[:, d], ps[:, 7].rearrange("p (c n) -> p c n", c=NC),
                                            tri[:, d].bitcast(F32).unsqueeze(1).to_broadcast([P, NC, P]), ALU.mult)
                link(ins)
                dve.wait_ge(yo_full, 6 * g)
                vec.tensor_copy(ccur[:], xbc[:, 5]).then_inc(cbs_ready, 1)

                heads = lambda ap: ap.rearrange("p (h d) -> p h d", h=HG)
                per_head = lambda row: gt[:, row, :].unsqueeze(2).to_broadcast([P, HG, HD])

                def state_x(n):
                    d, c = STEPS[n]
                    dve.wait_ge(st_full, 6 * g + len([m for m in MAKES_STATE if m < n]))
                    vec.tensor_tensor(heads(xw[:]), heads(xtok[:, c]), per_head(WST_ROW + 2 * c + d),
                                      ALU.mult).then_inc(xw_ready, 1)

                def weighed(h):
                    c = DIAG[h // 2]
                    row = lambda d, a: gt[:, DT_ROW + 2 * c + d, h % 2 * 4 + a:h % 2 * 4 + a + 1]
                    for a in range(4):
                        ins = vec.tensor_scalar(tmp[:, a * P:a * P + P], cbs[:, 0, c], row(0, a), None, ALU.mult)
                    link(ins)
                    for a in range(4):
                        ins = vec.scalar_tensor_tensor(out=tmp[:, a * P:a * P + P], in0=cbs[:, 1, c], scalar=row(1, a),
                                                       in1=tmp[:, a * P:a * P + P], op0=ALU.mult, op1=ALU.add)
                    link(ins)
                    dve.wait_ge(decay_ready, 8 * g + h + 1)
                    vec.tensor_tensor(em[:, h % 2], em[:, h % 2], tmp[:].rearrange("p (a n) -> p a n", a=4),
                                      ALU.mult).then_inc(m_ready, 1)

                def ada_share(n):
                    if n == 0:
                        dve.wait_ge(condg_ready, g + 1)
                    dve.wait_ge(m_ready, 8 * g + n + 1)
                    for u in (2 * n, 2 * n + 1):
                        dve.wait_ge(ada_loaded[u % 2], g * 16 * (ADA_UNITS // 2) + 16 * (u // 2 + 1))
                        for t in range(4):
                            for s in range(2):
                                m = u * ADA_DOTS + 2 * t + s
                                if m >= 2:
                                    dve.wait_ge(ada_used, g * ADA_UNITS * ADA_DOTS + (m - 1))
                                vec.scalar_tensor_tensor(
                                    out=tmp[:, s * ADA_K:s * ADA_K + ADA_K], in0=ada[:, u % 2, t], scalar=1.0, in1=condg[:, s],
                                    op0=ALU.mult, op1=ALU.mult, accum_out=part[:, 4 * u + t, s:s + 1]).then_inc(ada_used, 1)
                    dve.wait_ge(ada_used, g * ADA_UNITS * ADA_DOTS + (2 * n + 2) * ADA_DOTS)

                dve.wait_ge(xtok_ready, NC * g + NC)
                dve.wait_ge(cbs_ready, g + 1)
                state_x(0)
                for n in range(8):
                    d, c = STEPS[n]
                    weighed(n)
                    if not proj and 2 * n < EARLY:
                        y_low(2 * n + 1, 2 * n)
                    if n in READS_STATE:
                        dve.wait_ge(yo_full, 6 * g + READS_STATE.index(n) + 1)
                        dve.wait_ge(m_ready, 8 * g + n + 1)
                        vec.tensor_tensor(heads(tmp[:]), heads(ps[:, 7]), per_head(ECS_ROW + 2 * c + d),
                                          ALU.mult).then_inc(yo_taken, 1)
                    if n in MAKES_STATE and n in READS_STATE:
                        link(vec.tensor_tensor(heads(state[:]), heads(state[:]), per_head(ETOT_ROW + 2 * c + d), ALU.mult))
                    if d == 0:
                        link(vec.tensor_tensor(heads(y[:, c]), heads(xtok[:, c]), per_head(D_ROW), ALU.mult))
                    if n in READS_STATE:
                        dve.wait_ge(yo_taken, 6 * g + READS_STATE.index(n) + 1)
                        link(vec.tensor_tensor(y[:, c], y[:, c], tmp[:], ALU.add))
                    if n in MAKES_STATE:
                        dve.wait_ge(st_full, 6 * g + MAKES_STATE.index(n) + 1)
                        if n in READS_STATE:
                            vec.tensor_tensor(state[:], state[:], ps[:, 7], ALU.add).then_inc(state_ready, 1)
                        else:
                            vec.tensor_copy(state[:], ps[:, 7]).then_inc(state_ready, 1)
                    if n + 1 in MAKES_STATE:
                        state_x(n + 1)
                    if n % 2 == 1:
                        own = DIAG[n // 2]
                        dve.wait_ge(yd_full, 8 * g + n + 1)
                        vec.tensor_tensor(y[:, own], y[:, own], ps[:, 6], ALU.add).then_inc(yd_taken, 1)
                        dve.wait_ge(yd_taken, 4 * g + n // 2 + 1)
                    if d == 1:
                        dve.wait_ge(tile_evac, 10 * g + 7 + c)
                        vec.tensor_tensor(y[:, c], y[:, c], sz[:, c], ALU.mult).then_inc(gated, 1)
                    if proj and n < 6:
                        conv(g + 1, n)
                    if not proj and 2 * n + 1 < EARLY:
                        y_low(2 * n + 2, 2 * n + 1)
                    if n < 7:
                        ada_share(n)

                dve.wait_ge(sq_done, NC * g + NC)
                vec.tensor_scalar(stat[:, 4:8], stat[:, 0:4], 1.0 / T, RMS_EPS, ALU.mult,
                                  ALU.add).then_inc(var_ready, 1)
                dve.wait_ge(root_ready, g + 1)
                link(vec.reciprocal(stat[:, 12:16], stat[:, 8:12]))
                for c in range(NC):
                    ins = vec.tensor_scalar(y[:, c], y[:, c], stat[:, 12 + c:13 + c], None, ALU.mult)
                ins.then_inc(y_normed, 1)
                ada_share(7)
                vec.tensor_tensor(modl[:], modl[:], part[:], ALU.add).then_inc(ada_taken, 1)

            group(0, True)
            start = step.base + step.n
            with dve.Fori(1, GROUPS - 1) as i:
                step.enter(i - 1, start, LINKS_PER_GROUP)
                group(i, True)
            step.leave(GROUPS - 2, start, LINKS_PER_GROUP)
            group(GROUPS - 1, False)

            for u in range(EARLY, WOUT_UNITS):
                y_low(u + 1, u)
            for b in range(4):
                dve.wait_ge(g0_full, 4 + b + 1)
                vec.tensor_copy(gate0[:, 1, b * T:b * T + T], ps[:, 4 + b]).then_inc(g0_taken, 1)
            for u in range(2):
                y_low(WOUT_UNITS + u + 1, u)
            dve.wait_ge(g0_taken, 4)
            dve.wait_ge(g0_taken_act, 4)
            dve.wait_ge(res_loaded, 32)

            def add_block(block, bank):
                col = bass.ds(block * T, T)
                for c in range(NC):
                    dve.wait_ge(w_used, block * WOUT_UNITS + (WOUT_AT + WOUT_UNITS))
                    link(vec.tensor_tensor(wtmp[:, c % 2], ps[:, bank + c], gate0[:, c // 2, col], ALU.mult))
                    rows = (r_c if c < 2 else r_x)[:, c % 2, col]
                    vec.scalar_tensor_tensor(out=rows, in0=rows, scalar=ALPHA, in1=wtmp[:, c % 2],
                                             op0=ALU.mult, op1=ALU.add).then_inc(wo_taken, 1)

            add_block(0, 0)
            start = step.base + step.n
            with dve.Fori(1, 3) as i:
                step.enter(i - 1, start, NC)
                for u in range(WOUT_UNITS):
                    y_low(i * WOUT_UNITS + (u + 3), u + 2)
                add_block(i, 4)
            step.leave(2, start, NC)
            for u in range(WOUT_UNITS - 2):
                y_low(3 * WOUT_UNITS + u + 3, u + 2)
            add_block(3, 4)

            def normalise(rows, n, var_sem, root_sem, at):
                for c in range(n):
                    for q in range(4):
                        ins = vec.bn_stats(bn[:, c, 6 * q:6 * q + 6], rows[c][:, q * T:q * T + T])
                    link(ins)
                    link(vec.bn_aggr(stat[:, 48 + 2 * c:50 + 2 * c], bn[:, c]))
                    ins = vec.tensor_scalar(stat[:, at + c:at + c + 1], stat[:, 49 + 2 * c:50 + 2 * c], LN_EPS, None, ALU.add)
                ins.then_inc(var_sem, 1)
                dve.wait_ge(root_sem, 1)
                link(vec.reciprocal(stat[:, 56:56 + n], stat[:, at + 4:at + 4 + n]))

            dve.wait_ge(wo_taken, NC * 4)
            rows = [r_c[:, 0], r_c[:, 1], r_x[:, 0], r_x[:, 1]]
            normalise(rows, 4, lnvar_ready, lnroot_ready, 16)
            for c in range(4):
                vec.tensor_scalar(rows[c], rows[c], stat[:, 48 + 2 * c:49 + 2 * c], stat[:, 56 + c:57 + c],
                                  ALU.subtract, ALU.mult).then_inc(ln_ready, 1)
            link(vec.tensor_scalar(us[:], modl[:, 32:48], 1.0, None, ALU.add))
            link(vec.tensor_tensor(ub[:], us[:], par[:, LNB_AT:LNB_AT + 16].unsqueeze(2).to_broadcast([P, KT, 2]), ALU.mult))
            link(vec.tensor_tensor(ub[:], ub[:], modl[:, 16:32], ALU.add))
            link(vec.tensor_tensor(us[:], us[:], par[:, LNG_AT:LNG_AT + 16].unsqueeze(2).to_broadcast([P, KT, 2]), ALU.mult))
            dve.wait_ge(ln_ready, 4)
            for k in range(KT):
                dve.wait_ge(rt_full, k + 1)
                modulate(KT + k, k, utmp1[:, k % 2], ps[:, k % 4], us[:, k], ub[:, k])
                if k:
                    low_u(KT + k - 1, k - 1, utmp1[:, (k - 1) % 2])
            low_u(2 * KT - 1, KT - 1, utmp1[:, (KT - 1) % 2])
            dve.wait_ge(rows0_loaded, 32)
            for c in range(2):
                link(vec.tensor_tensor(r_x[:, c], r_x[:, c], rows0[:, 0], ALU.mult))
                ins = vec.tensor_tensor(r_x[:, c], r_x[:, c], rows0[:, 1], ALU.add)
            ins.then_inc(x1_ready, 1)
            for b in range(4):
                dve.wait_ge(g1_full, b + 1)
                vec.tensor_copy(gate1[:, b * T:b * T + T], ps[:, 4 + b]).then_inc(g1_taken, 1)

            for m in range(2):
                n = (TC, T)[m]
                dve.wait_ge(sq_used, 4 * m + 4)
                vec.tensor_scalar(rsd[:, m, 0:n], ps[:, SUM_BANK[m], 0:n], 1.0 / RANK, RMS_EPS, ALU.mult,
                                  ALU.add).then_inc(msv_ready, 1)
            for m in range(2):
                n = (TC, T)[m]
                dve.wait_ge(msroot_ready, m + 1)
                link(vec.reciprocal(rsd[:, m, 0:n], rsd[:, m, 0:n]))
                for t in range(4):
                    src = (cq, ckv)[m][:, t]
                    w = par[:, (QN_AT, KVN_AT)[m] + t:(QN_AT, KVN_AT)[m] + t + 1]
                    dve.wait_ge(lat_taken, 4 * m + t + 1)
                    vec.scalar_tensor_tensor(out=src, in0=src, scalar=w, in1=rsd[:, m, 0:n], op0=ALU.mult,
                                             op1=ALU.mult).then_inc(cn_ready, 1)
                for t in range(4):
                    hi, lo = ((cq_hi, cq_lo), (ckv_hi, ckv_lo))[m]
                    dve.wait_ge(chi_ready, 4 * m + t + 1)
                    vec.tensor_tensor(lo[:, t], (cq, ckv)[m][:, t], hi[:, t].bitcast(F32),
                                      ALU.subtract).then_inc(clo_ready, 1)
            dve.wait_ge(krot_full, 1)
            dve.wait_ge(trig_loaded, 16)
            vec.tensor_tensor(sq[:, 0, 0:TC], ps[:, 7, 0:TC], trig[:, 1], ALU.mult)
            link(vec.tensor_tensor(kr[:, TC:T], kr[:, TC:T], trig[:, 0], ALU.mult))
            vec.tensor_tensor(kr[:, TC:T], kr[:, TC:T], sq[:, 0, 0:TC], ALU.add).then_inc(kr_ready, 1)

            for b in range(4):
                dve.wait_ge(w_used, HEAD_AT + HEAD_UNITS * b + 3)
                dve.wait_ge(s_full, 8 * b)
                vec.tensor_copy(qr[:].rearrange("p a n -> p (a n)"), ps[:, 2]).then_inc(hq_dve, 1)
                dve.wait_ge(w_used, HEAD_AT + HEAD_UNITS * (b + 1))
                dve.wait_ge(o_full, 4 * b)
                for n in range(2):
                    vec.tensor_copy(v[:, 2 + n], ps[:, 2 + n]).then_inc(hq_dve, 1)
                dve.wait_ge(qrot_full, b + 1)
                dve.wait_ge(hq_dve, 3 * b + 1)
                both = lambda ap: ap.unsqueeze(1).to_broadcast([P, 2, TC])
                vec.tensor_tensor(qrt[:], ps[:, 7].rearrange("p (a n) -> p a n", a=2), both(trig[:, 1]), ALU.mult)
                link(vec.tensor_tensor(qr[:], qr[:], both(trig[:, 0]), ALU.mult))
                vec.tensor_tensor(qr[:], qr[:], qrt[:], ALU.add).then_inc(qr_ready, 1)

                def max_scores(n):
                    m = 8 * b + n
                    dve.wait_ge(s_full, m + 1)
                    link(vec.reduce_max(stat[:, 32 + n:33 + n], ps[:, 4 + n % 2], AX.X))
                    vec.tensor_scalar(stat[:, 32 + n:33 + n], stat[:, 32 + n:33 + n], -SCALE, None,
                                      ALU.mult).then_inc(max_ready, 1)

                def scale_probs(n):
                    m = 8 * b + n
                    dve.wait_ge(p_ready, m + 1)
                    link(vec.reciprocal(stat[:, 40 + n:41 + n], stat[:, 40 + n:41 + n]))
                    vec.tensor_scalar(prob[:, n % 2], prob[:, n % 2], stat[:, 40 + n:41 + n], None,
                                      ALU.mult).then_inc(p_scaled, 1)

                def take_transposed(n):
                    m = 8 * b + n
                    dve.wait_ge(pt_full, m + 1)
                    if n % 2 == 0 and m >= 2:
                        dve.wait_ge(o_full, m // 2)
                    vec.tensor_copy(prob_t[:, :, n % 2 * P:n % 2 * P + P],
                                    ps[:, 6].rearrange("p (k q) -> p k q", k=4)).then_inc(pt_ready, 1)

                def gate_output(hh):
                    hd = 4 * b + hh
                    dve.wait_ge(o_full, hd + 1)
                    if hd >= 2:
                        dve.wait_ge(ogl_ready, hd - 1)
                    vec.tensor_tensor(sq[:, hh % 2, 0:TC], ps[:, 7, 0:TC], gates[:, hd], ALU.mult).then_inc(o_taken, 1)
                    dve.wait_ge(ogh_ready, hd + 1)
                    vec.tensor_tensor(og_lo[:, hd], sq[:, hh % 2, 0:TC], og_hi[:, hd].bitcast(F32),
                                      ALU.subtract).then_inc(ogl_ready, 1)

                max_scores(0)
                for n in range(8):
                    if n < 7:
                        max_scores(n + 1)
                    scale_probs(n)
                    take_transposed(n)
                    if n % 2 == 1 and n >= 3:
                        gate_output(n // 2 - 1)
                gate_output(3)

            dve.wait_ge(g1_taken, 4)
            dve.wait_ge(x1_ready, 1)
            vec.memset(stat[:, 63:64], 0.0).then_inc(out_taken, 4)
            for nb in range(4):
                for c in range(2):
                    dve.wait_ge(w_used, WO_AT + WO_UNITS * (nb + 1))
                    cols = slice(nb * T, nb * T + T)
                    link(vec.tensor_tensor(sq[:, c], ps[:, 2 * (nb % 2) + c], gate1[:, cols], ALU.mult))
                    ins = vec.scalar_tensor_tensor(out=r_x[:, c, cols], in0=r_x[:, c, cols], scalar=ALPHA,
                                                   in1=sq[:, c], op0=ALU.mult, op1=ALU.add)
                    ins.then_inc(out_taken, 1)
            dve.wait_ge(out_taken, 12)
            normalise([r_x[:, 0], r_x[:, 1]], 2, fvar_ready, froot_ready, 24)
            dve.wait_ge(rows1_loaded, 32)
            for c in range(2):
                link(vec.tensor_scalar(r_x[:, c], r_x[:, c], stat[:, 48 + 2 * c:49 + 2 * c],
                                       stat[:, 56 + c:57 + c], ALU.subtract, ALU.mult))
                link(vec.tensor_tensor(r_x[:, c], r_x[:, c], rows1[:, 0], ALU.mult))
                vec.tensor_tensor(r_x[:, c], r_x[:, c], rows1[:, 1], ALU.add).then_inc(out_ready, 1)

        @block.tensor
        def _(pe):
            mm = nc.tensor.matmul

            def product(out, lhs, rhs, first, last):
                mm(out, lhs[0], rhs[0], start=first, stop=False)
                mm(out, lhs[0], rhs[1], start=False, stop=False)
                return mm(out, lhs[1], rhs[0], start=False, stop=last)

            def weights(slot, cols):
                view = lambda w: w[:, slot].rearrange("p (k n) -> p k n", n=cols)
                return view(w_hi), view(w_lo)

            pe.wait_ge(cond_ready, 1)
            for t in ADA0_ON_PE:
                pe.wait_ge(ada0_loaded[t % ADA0_RING], 16 * (t // ADA0_RING + 1))
                for k in range(KT):
                    ins = mm(ps[:, 7, 2 * t:2 * t + 2], ada0[:, t % ADA0_RING, k], cond[:, k],
                             start=(k == 0), stop=(k == KT - 1))
                ins.then_inc(ada0_pe, 1)

            pe.wait_ge(u_ready, KT)
            for half in range(2):
                pe.wait_ge(lo_ready, half + 1)
                w = weights(half, P)
                for c in range(NC):
                    cols = slice(c * P, c * P + P)
                    for k in range(8):
                        kt = half * 8 + k
                        ins = product(ps[:, c, 0:P], (u_hi[:, kt, cols], u_lo[:, kt, cols]),
                                      (w[0][:, k], w[1][:, k]), kt == 0, kt == KT - 1)
                ins.then_inc(w_used, 1)

            def project(g, j):
                pe.wait_ge(lo_ready, PROJ_UNITS * g + (DT_UNITS + j + 1))
                slot = (DT_UNITS + j) % RING
                if j < 12:
                    t, half = divmod(j, 2)
                    w = weights(slot, P)
                    if half == 0:
                        if isinstance(g, int) and g == 0 and t < 4:
                            pe.wait_ge(dt_abs, 1)
                        else:
                            pe.wait_ge(tile_evac, 10 * g + max(t - 3, 0))
                    for k in range(8):
                        kt = half * 8 + k
                        ins = product(ps[:, t % 4], (w[0][:, k], w[1][:, k]), (u_hi[:, kt], u_lo[:, kt]),
                                      kt == 0, kt == KT - 1)
                else:
                    u = j - 12
                    w = weights(slot, T)
                    if u == 0:
                        pe.wait_ge(tile_evac, 10 * g + 6)
                    for c in range(NC):
                        for k in range(2):
                            kt = 2 * u + k
                            cols = slice(c * P, c * P + P)
                            ins = product(ps[:, c], (u_hi[:, kt, cols], u_lo[:, kt, cols]),
                                          (w[0][:, k], w[1][:, k]), kt == 0, kt == KT - 1)
                ins.then_inc(w_used, 1)

            for j in range(PROJ_UNITS):
                project(0, j)
                if j == 3:
                    pe.wait_ge(a_ready, 1)
                    pe.wait_ge(consts_ready, 1)
                    rows = tab[:, A_ROW:A_ROW + 8].rearrange("p (c d) h -> p c d h", d=2)
                    out = ps[:, 5].rearrange("p (c d h) -> p c d h", c=NC, d=2)
                    for d in range(2):
                        mm(out[:, :, d], tri[:, d].bitcast(F32), rows[:, :, d], start=True, stop=True)
                    mm(ps[:, 6], ones[:], tab[:, A_ROW:A_ROW + 8].rearrange("p r h -> p (r h)"),
                       start=True, stop=True).then_inc(cs_full, 1)

            def scan(g, j):
                if j == 1:
                    pe.wait_ge(silu_done, 6 * g + 6)
                    for c in range(NC):
                        if c == 0:
                            pe.wait_ge(yt_evac, GT * g)
                        for k in range(GT):
                            ins = nc.tensor.transpose(ps[:, X_BANK[c], k * P:k * P + P],
                                                      xbc[:, k, c * P:c * P + P], ident[:])
                        ins.then_inc(xt_full, 1)
                if j == 2:
                    pe.wait_ge(xtok_ready, NC * g + 1)
                    for c in range(NC):
                        ins = nc.tensor.transpose(ps[:, 6, c * P:c * P + P], xbc[:, 4, c * P:c * P + P], ident[:])
                    ins.then_inc(bt_full, 1)
                    pe.wait_ge(xtok_ready, NC * g + 2)
                    for c in range(NC):
                        ins = mm(ps[:, 7, c * P:c * P + P], xbc[:, 4, c * P:c * P + P],
                                 xbc[:, 5, c * P:c * P + P], start=True, stop=True)
                    ins.then_inc(cb_full, 1)
                if j % 2 == 0 and 2 <= j < 18:
                    h = j // 2 - 1
                    pe.wait_ge(am_ready, 8 * g + h + 1)
                    if h < 2:
                        pe.wait_ge(xtok_ready, NC * g + 3 + h)
                    else:
                        pe.wait_ge(decay_ready, 8 * g + h - 1)
                    for n in range(2):
                        for d in range(2):
                            ins = mm(ps[:, 4 + h % 2], strict[:, d], am[:, n, d].rearrange("p a n -> p (a n)"),
                                     start=(n == 0 and d == 0), stop=(n == 1 and d == 1))
                    ins.then_inc(seg_full, 1)
                n, half = divmod(j - 3, 2)
                if 3 <= j < 19 and half == 0 and n in READS_STATE:
                    c = STEPS[n][1]
                    pe.wait_ge(state_ready, 6 * g + len([m for m in MAKES_STATE if m < n]))
                    mm(ps[:, 7], ccur[:, c * P:c * P + P], state[:], start=True, stop=True).then_inc(yo_full, 1)
                if 3 <= j < 19 and half == 1 and n in MAKES_STATE:
                    c = STEPS[n][1]
                    if n == 0:
                        pe.wait_ge(btok_ready, g + 1)
                        pe.wait_ge(cbs_ready, g + 1)
                    pe.wait_ge(yo_taken, 6 * g + len([m for m in READS_STATE if m <= n]))
                    pe.wait_ge(xw_ready, 6 * g + MAKES_STATE.index(n) + 1)
                    mm(ps[:, 7], btok[:, c], xw[:], start=True, stop=True).then_inc(st_full, 1)
                if 3 <= j < 19 and half == 1:
                    c = DIAG[n // 2]
                    if n % 2 == 0:
                        pe.wait_ge(yd_taken, 4 * g + n // 2)
                    pe.wait_ge(m_ready, 8 * g + n + 1)
                    for a in range(4):
                        hd = 4 * (n % 2) + a
                        ins = mm(ps[:, 6, hd * HD:hd * HD + HD], em[:, n % 2, a], xtok[:, c, hd * HD:hd * HD + HD],
                                 start=True, stop=True)
                    ins.then_inc(yd_full, 1)

            def wout_unit(block, u, bank):
                pe.wait_ge(ylo_ready, block * WOUT_UNITS + (u + 1))
                pe.wait_ge(lo_ready, block * WOUT_UNITS + (WOUT_AT + u + 1))
                w = weights((WOUT_AT + u) % RING, T)
                for c in range(NC):
                    if u == 0 and bank:
                        pe.wait_ge(wo_taken, block * NC + (c + 1 - NC))
                    cols = slice(c * P, c * P + P)
                    for k in range(2):
                        ins = product(ps[:, bank + c], (yr_hi[:, u % 2, k, cols], yr_lo[:, u % 2, k, cols]),
                                      (w[0][:, k], w[1][:, k]), u == 0 and k == 0,
                                      u == WOUT_UNITS - 1 and k == 1)
                ins.then_inc(w_used, 1)

            def group(g, proj):
                for j in range(PROJ_UNITS):
                    scan(g, j)
                    if not proj and 0 <= j - EARLY_FROM < EARLY:
                        if j == EARLY_FROM:
                            pe.wait_ge(tile_evac, 10 * GROUPS)
                        wout_unit(0, j - EARLY_FROM, 0)
                    if proj:
                        project(g + 1, j)
                pe.wait_ge(y_normed, g + 1)
                pe.wait_ge(yd_taken, 4 * g + 4)
                for k in range(GT):
                    for c in range(NC):
                        ins = nc.tensor.transpose(ps[:, 4 + k, c * P:c * P + P], y[:, c, k * P:k * P + P], ident[:])
                    ins.then_inc(yt_full, 1)

            pe.wait_ge(cs_exp, 3)
            group(0, True)
            with pe.Fori(1, GROUPS - 1) as i:
                group(i, True)
            group(GROUPS - 1, False)

            pe.wait_ge(ada_taken, GROUPS)
            pe.wait_ge(yt_evac, GT * GROUPS)
            for s in range(2):
                if s == 1:
                    pe.wait_ge(g0_taken_act, 4)
                for t in range(KT):
                    ins = mm(ps[:, 4 + t // 4, t % 4 * P:t % 4 * P + P],
                             modl[:, t, s:s + 1].to_broadcast([P, P]), ident[:], start=True, stop=True)
                    if t % 4 == 3:
                        ins.then_inc(g0_full, 1)
                wout_unit(0, EARLY + s, 0)
            pe.wait_ge(g0_taken, 4)
            with pe.Fori(1, 4) as i:
                for u in range(WOUT_UNITS):
                    wout_unit(i, u, 4)

            pe.wait_ge(ln_ready, 4)
            for k in range(KT):
                if k >= 4:
                    pe.wait_ge(utmp_ready, KT + k - 3)
                for c in range(NC):
                    ins = nc.tensor.transpose(ps[:, k % 4, c * P:c * P + P],
                                              (r_c, r_x)[c // 2][:, c % 2, k * P:k * P + P], ident[:])
                ins.then_inc(rt_full, 1)
            for t in range(KT):
                ins = mm(ps[:, 4 + t // 4, t % 4 * P:t % 4 * P + P],
                         modl[:, 48 + t, 1:2].to_broadcast([P, P]), ident[:], start=True, stop=True)
                if t % 4 == 3:
                    ins.then_inc(g1_full, 1)

            pe.wait_ge(u_ready, 2 * KT)
            with pe.Fori(0, 4) as i:
                for t in range(4):
                    if t == 2:
                        pe.wait_ge(gt_taken, i * 4 + 1)
                    for half in range(2):
                        s = MLA_AT + 2 * t + half
                        pe.wait_ge(lo_ready, i * 8 + (s + 1))
                        w = weights(s % RING, P)
                        for k in range(8):
                            kt = half * 8 + k
                            ins = product(ps[:, t, 0:TC], (w[0][:, k], w[1][:, k]),
                                          (u_hi[:, kt, TC:T], u_lo[:, kt, TC:T]), kt == 0, kt == KT - 1)
                        ins.then_inc(w_used, 1)
                pe.wait_ge(gt_taken, i * 4 + 2)

            def sum_squares(t):
                m, q = divmod(t, 4)
                n = (TC, T)[m]
                pe.wait_ge(sq_ready, t + 1)
                mm(ps[:, SUM_BANK[m], 0:n], ones[:], sq[:, t % 2, 0:n], start=(q == 0), stop=(q == 3)).then_inc(sq_used, 1)

            pe.wait_ge(g1_taken, 4)
            pe.wait_ge(gt_taken, HEADS)
            for j in range(LATENT_UNITS):
                t, half = divmod(j, 2)
                s = MLA_AT + GATE_UNITS + j
                pe.wait_ge(lo_ready, s + 1)
                if t == 7 and half == 0:
                    pe.wait_ge(msv_ready, 1)
                if t == 8 and half == 0:
                    pe.wait_ge(sq_ready, 1)
                w = weights(s % RING, P)
                lo = TC if t < 4 else 0
                out = ps[:, 4 + t, 0:TC] if t < 4 else ps[:, t - 4] if t < 8 else ps[:, 4]
                for k in range(8):
                    kt = half * 8 + k
                    ins = product(out, (w[0][:, k], w[1][:, k]), (u_hi[:, kt, lo:T], u_lo[:, kt, lo:T]),
                                  kt == 0, kt == KT - 1)
                ins.then_inc(w_used, 1)
                if half == 1 and t >= 1:
                    sum_squares(t - 1)
            pe.wait_ge(lat_taken, 9)
            pe.wait_ge(rot_loaded, 16)
            mm(ps[:, 7, 0:TC], rot[:], kr[:, TC:T], start=True, stop=True).then_inc(krot_full, 1)

            for b in range(4):
                at = HEAD_AT + HEAD_UNITS * b
                for j in range(HEAD_UNITS):
                    s = at + j
                    pe.wait_ge(lo_ready, s + 1)
                    if j == 0:
                        pe.wait_ge(clo_ready, 4)
                        pe.wait_ge(hq_act, 8 * b)
                        pe.wait_ge(hq_dve, 3 * b)
                        pe.wait_ge(lat_taken, 8)
                    if j == 3:
                        pe.wait_ge(clo_ready, 8)
                        pe.wait_ge(p_ready, 8 * b)
                        pe.wait_ge(pt_ready, 8 * b)
                    if j == 5:
                        pe.wait_ge(hq_act, 8 * b + 4)
                        pe.wait_ge(hq_dve, 3 * b + 1)
                    if j < 5:
                        w = weights(s % RING, 2 * P)
                        lat_hi, lat_lo = (cq_hi, cq_lo) if j < 3 else (ckv_hi, ckv_lo)
                        for a in range(2):
                            out = ps[:, j, a * TC:a * TC + TC] if j < 3 else ps[:, 3 + 2 * (j - 3) + a]
                            for k in range(4):
                                cols = slice(a * P, a * P + P)
                                ins = product(out, (w[0][:, k, cols], w[1][:, k, cols]),
                                              (lat_hi[:, k], lat_lo[:, k]), k == 0, k == 3)
                    else:
                        w = weights(s % RING, T)
                        for c in range(NC):
                            cols = slice(c * P, c * P + P)
                            for k in range(2):
                                kt = 2 * (j - 5) + k
                                ins = product(ps[:, c], (ckv_hi[:, kt, cols], ckv_lo[:, kt, cols]),
                                              (w[0][:, k], w[1][:, k]), kt == 0, kt == 3)
                    ins.then_inc(w_used, 1)
                    if j == 4:
                        pe.wait_ge(hq_dve, 3 * b + 1)
                        pe.wait_ge(o_taken, 4 * b)
                        if b == 0:
                            pe.wait_ge(kr_ready, 1)
                        mm(ps[:, 7], rot[:], qr[:].rearrange("p a n -> p (a n)"), start=True,
                           stop=True).then_inc(qrot_full, 1)

                def scores(n):
                    hh, qt = divmod(n, 2)
                    if n == 0:
                        pe.wait_ge(hq_act, 8 * b + 6)
                        pe.wait_ge(qr_ready, b + 1)
                    pe.wait_ge(p_ready, 8 * b + max(n - 1, 0))
                    q = slice(qt * P, qt * P + P)
                    half = slice(64 * (hh % 2), 64 * (hh % 2) + 64)
                    mm(ps[:, 4 + n % 2], qn[:, hh, q], kn[:, hh], start=True, stop=False)
                    mm(ps[:, 4 + n % 2], qr[half, hh // 2, q], kr[half, :], start=False, stop=True).then_inc(s_full, 1)

                def transpose_probs(n):
                    pe.wait_ge(p_scaled, 8 * b + n + 1)
                    pe.wait_ge(pt_ready, 8 * b + n)
                    for c in range(NC):
                        ins = nc.tensor.transpose(ps[:, 6, c * P:c * P + P], prob[:, n % 2, c * P:c * P + P], ident[:])
                    ins.then_inc(pt_full, 1)

                def head_output(hh):
                    pe.wait_ge(pt_ready, 8 * b + 2 * hh + 2)
                    pe.wait_ge(o_taken, 4 * b + hh)
                    pe.wait_ge(hq_act, 8 * b + 8)
                    pe.wait_ge(hq_dve, 3 * b + 3)
                    for c in range(NC):
                        ins = mm(ps[:, 7, 0:TC], v[:, c, hh * P:hh * P + P], prob_t[:, c], start=(c == 0), stop=(c == 3))
                    ins.then_inc(o_full, 1)

                scores(0)
                for n in range(8):
                    if n < 7:
                        scores(n + 1)
                    transpose_probs(n)
                    if n % 2 == 1:
                        head_output(n // 2)

            pe.wait_ge(ogl_ready, HEADS)
            with pe.Fori(0, 2) as i:
                for b in range(2):
                    pe.wait_ge(out_taken, i * 4 + (2 * b + 2))
                    for u in range(WO_UNITS):
                        s = WO_AT + b * WO_UNITS + u
                        pe.wait_ge(lo_ready, i * 2 * WO_UNITS + (s + 1))
                        w = weights(s % RING, T)
                        for c in range(2):
                            cols = slice(c * P, c * P + P)
                            for k in range(2):
                                kt = 2 * u + k
                                ins = product(ps[:, 2 * b + c], (og_hi[:, kt, cols], og_lo[:, kt, cols]),
                                              (w[0][:, k], w[1][:, k]), kt == 0, kt == KT - 1)
                        ins.then_inc(w_used, 1)


def _constants():
    eye = np.eye(P, dtype=np.float32)
    rot = np.zeros((P, P), np.float32)
    even = np.arange(0, P, 2)
    rot[even + 1, even] = -1.0
    rot[even, even + 1] = 1.0
    forward = np.triu(np.ones((P, P), np.float32))
    backward = np.tril(np.ones((P, P), np.float32))
    consts = np.stack([eye, np.ones((P, P), np.float32), rot, forward, backward,
                       1 - forward, 1 - backward])
    freq = np.float32(10000.0) ** (-np.arange(16, dtype=np.float32) / np.float32(16))
    token = np.arange(TC)
    ang = np.concatenate([(token // 64).astype(np.float32)[:, None] * freq,
                          (token % 64).astype(np.float32)[:, None] * freq], -1)
    ang = np.repeat(ang, 2, axis=1).T
    ang = np.concatenate([ang, ang])
    trig = np.stack([np.cos(ang), np.sin(ang)], 1).astype(np.float32)
    return consts.astype(np.float32), trig


def _stationary(w, cols, k_per_unit):
    k, n = w.shape
    w = w.reshape(k // (P * k_per_unit), k_per_unit, P, n // cols, cols)
    return w.transpose(3, 0, 2, 1, 4).reshape(-1, P, k_per_unit * cols)


def _layout(inp):
    def a(name):
        return np.asarray(inp[name])
    w_in = a("ssd_w_in")[0]
    inner, state_at = 4096, 2 * 4096
    units = [_stationary(w_in[:, 10240:10368], P, 8)]
    for g in range(GROUPS):
        x = w_in[:, inner + g * T:inner + (g + 1) * T]
        bm = w_in[:, state_at + g * P:state_at + (g + 1) * P]
        cm = w_in[:, state_at + 1024 + g * P:state_at + 1024 + (g + 1) * P]
        units += [_stationary(x, P, 8), _stationary(bm, P, 8), _stationary(cm, P, 8),
                  _stationary(w_in[:, g * T:(g + 1) * T], T, 2)]
    units.append(_stationary(a("ssd_w_out")[0], T, 2))
    m_in = a("mla_w_in")[0]
    kr = m_in[:, 1024:1088]
    units += [_stationary(m_in[:, 1088:], P, 8), _stationary(m_in[:, :1024], P, 8),
              _stationary(np.concatenate([kr, kr], 1), P, 8)]
    uq = a("mla_w_uq")[0].reshape(RANK, HEADS, 192)
    ukv = a("mla_w_ukv")[0].reshape(RANK, HEADS, 256)
    for b in range(4):
        h = slice(4 * b, 4 * b + 4)
        units += [_stationary(uq[:, h, :128].reshape(RANK, 512), 256, 4),
                  _stationary(uq[:, h, 128:].reshape(RANK, 256), 256, 4),
                  _stationary(ukv[:, h, :128].reshape(RANK, 512), 256, 4),
                  _stationary(ukv[:, h, 128:].reshape(RANK, 512), T, 2)]
    units.append(_stationary(a("mla_w_o")[0], T, 2))
    stream = np.concatenate(units)
    assert stream.shape == (UNITS, P, UNIT), stream.shape

    w0, w1 = a("ada_w")
    ada0 = np.stack([w0[:, t * P:t * P + P].reshape(KT, P, P).transpose(1, 0, 2).reshape(P, D)
                     if t in ADA0_ON_PE else w0[:, t * P:t * P + P].T for t in range(ADA0)])
    ada = np.concatenate([w0[:, ADA0 * P:], w1], 1).reshape(GROUPS, ADA_K, ADA_UNITS, 4, P)
    ada = ada.transpose(0, 2, 4, 3, 1).reshape(GROUPS * ADA_UNITS, P, 4, ADA_K)
    conds = np.stack([a("c_ctx"), a("c")[0]])

    def tiles(vec):
        return vec.reshape(-1, P).T

    conv_w, conv_b = a("ssd_conv_w")[0], a("ssd_conv_b")[0]
    par = []
    for g in range(GROUPS):
        cols = np.concatenate([np.arange(g * T, (g + 1) * T), inner + np.arange(g * P, (g + 1) * P),
                               inner + 1024 + np.arange(g * P, (g + 1) * P)])
        par.append(conv_w[:, cols].reshape(TAPS, 6, P).transpose(2, 1, 0).reshape(P, 30))
        par.append(tiles(conv_b[cols]))
    par += [tiles(a("ssd_norm_w")[0]), tiles(a("ada_b")[0]), tiles(a("ada_b")[1]),
            tiles(a("ln_g")[0]), tiles(a("ln_b")[0]), tiles(a("mla_q_norm")[0]), tiles(a("mla_kv_norm")[0]),
            np.stack([tiles(a("c_ctx")), tiles(a("c")[0])], -1).reshape(P, 32)]
    tokens = np.concatenate([a("ctx")[0], a("x")[0]])
    consts, trig = _constants()
    return {
        "stream": stream, "ada0": ada0, "ada": ada,
        "cond_rows": conds.reshape(1, 2, D),
        "cond_groups": conds.reshape(2, GROUPS, ADA_K).transpose(1, 0, 2).reshape(GROUPS, 1, 2, ADA_K),
         "par": np.concatenate(par, 1), "consts": consts, "trig": trig,
        "x_cm": tokens.T.reshape(KT, P, T).transpose(1, 0, 2), "x_tm": tokens.reshape(NC, P, D),
        "dt_bias": a("ssd_dt_bias")[0].reshape(1, P), "a_log": a("ssd_a_log")[0].reshape(1, P),
        "d_skip": a("ssd_d")[0].reshape(1, 64),
        "ln_rows": np.stack([a("ln_g"), a("ln_b")], 1).reshape(2, 2, 1, D),
    }


def kernel(**inputs):
    import concourse.bacc as bacc
    from concourse.bass_utils import run_bass_kernel_spmd

    nc = bacc.Bacc("TRN2", target_bir_lowering=False, num_devices=1)
    arrays = {f"in_{k}": np.ascontiguousarray(v) for k, v in _layout(inputs).items()}
    hbm = {k[3:]: nc.dram_tensor(k, v.shape, F32, kind="ExternalInput").ap() for k, v in arrays.items()}
    hbm["y"] = nc.dram_tensor("inner_rows", (GROUPS, P, GT, T), F32, kind="Internal").ap()
    hbm["out"] = nc.dram_tensor("out", (1, TC, D), F32, kind="ExternalOutput").ap()
    program(nc, hbm)
    r = run_bass_kernel_spmd(nc, [arrays], core_ids=[0])
    return r.results[0]["out"]
```

```python
from contextlib import ExitStack

import numpy as np
import concourse.bass as bass
from concourse import mybir

F32 = mybir.dt.float32
F32R = mybir.dt.float32r
ALU = mybir.AluOpType
ACT = mybir.ActivationFunctionType
AX = mybir.AxisListType

P = 128
D = 2048
KT = D // P
T = 512
TC = 256
NC = T // P
GROUPS = 8
GT = 4
HG = 8
HD = 64
TAPS = 5
RING = 4
UNIT = 1024
RANK = 512
HEADS = 16
SCALE = (128 + 64) ** -0.5
ALPHA = 4 ** 0.25
LN_EPS = 1e-5
RMS_EPS = 1e-6

DT_UNITS = 2
PROJ_UNITS = 20
WOUT_AT = DT_UNITS + GROUPS * PROJ_UNITS
WOUT_UNITS = 16
EARLY = WOUT_UNITS - 2
EARLY_FROM = 4
MLA_AT = WOUT_AT + 4 * WOUT_UNITS
GATE_UNITS = 32
LATENT_UNITS = 18
HEAD_AT = MLA_AT + GATE_UNITS + LATENT_UNITS
HEAD_UNITS = 7
WO_AT = HEAD_AT + 4 * HEAD_UNITS
WO_UNITS = 8
UNITS = WO_AT + 4 * WO_UNITS
SPLIT_AHEAD = 3

ADA0 = 32
ADA0_RING = 5
ADA0_ORDER = [n // 2 + n % 2 * KT for n in range(ADA0)]
ADA0_ON_PE = [n for n in range(30) if n % 3 == 1]
ADA0_ON_DVE = [n for n in range(ADA0) if n not in ADA0_ON_PE]
ADA0_LAG = 2
XCM = 4
ADAL = 64
ADA_K = D // GROUPS
ADA_UNITS = 16
ADA_DOTS = 8

CONV_AT = 0
NORM_AT = CONV_AT + GROUPS * 36
ADA0_AT = NORM_AT + 32
ADAL_AT = ADA0_AT + 32
LNG_AT = ADAL_AT + 64
LNB_AT = LNG_AT + 16
QN_AT = LNB_AT + 16
KVN_AT = QN_AT + 4
COND_AT = KVN_AT + 4
PARS = COND_AT + 32

DT_ROW, WST_ROW, ECS_ROW, ETOT_ROW, A_ROW, D_ROW = 0, 8, 16, 24, 32, 40
TAB_ROWS = 41

LINKS_PER_GROUP = 49
STEPS = [(0, 0), (0, 1), (0, 2), (0, 3), (1, 1), (1, 0), (1, 3), (1, 2)]
DIAG = [0, 1, 3, 2]
READS_STATE = [n for n in range(8) if n not in (0, 4)]
MAKES_STATE = [n for n in range(8) if n not in (3, 7)]
SUM_BANK = [3, 6]
SCORE_BANK = [4, 5, 0, 1]
X_BANK = [6, 7, 4, 5]


class Step:

    def __init__(self, eng, sem):
        self.eng, self.sem, self.base, self.n = eng, sem, 0, 0

    def link(self, ins):
        self.n += 1
        ins.then_inc(self.sem, 1)
        self.eng.wait_ge(self.sem, self.base + self.n)

    def enter(self, i, start, per):
        self.base, self.n = i * per + start, 0

    def leave(self, turns, start, per):
        assert self.n == per, f"{self.n} links in a turn"
        self.base, self.n = start + turns * per, 0


def program(nc, hbm):
    with ExitStack() as ctx:
        def sem(name):
            return ctx.enter_context(nc.semaphore(name))

        place = [-(-nc.sbuf_base // 32) * 32]

        def sb(name, shape, dtype=F32):
            t = nc.alloc_sbuf_tensor_at(name, [P] + shape, dtype, offset=place[0])
            place[0] += int(np.prod(shape)) * 4
            place[0] = -(-place[0] // 32) * 32
            assert place[0] <= nc.sbuf_usable_end, (name, place[0])
            return t

        raw = sb("raw", [RING, UNIT])
        w_hi = sb("w_hi", [RING, UNIT], F32R)
        w_lo = sb("w_lo", [RING, UNIT], F32R)
        par = sb("par", [PARS])
        ident = sb("ident", [P])
        ones = sb("ones", [P])
        tri = sb("tri", [2, P], F32R)
        strict = sb("strict", [2, P], F32R)
        cond = sb("cond", [KT, 2])
        mod0 = sb("mod0", [32, 2])
        modl = sb("modl", [64, 2])
        us = sb("us", [KT, 2])
        ub = sb("ub", [KT, 2])
        stat = sb("stat", [64])
        region_u = place[0]
        u_hi = sb("u_hi", [KT, T], F32R)
        u_lo = sb("u_lo", [KT, T], F32R)
        region_l = place[0]

        ada0 = sb("ada0", [ADA0_RING, KT, P])
        cond_rows = sb("cond_rows", [2, D])
        products = sb("products", [D])
        xcm = sb("xcm", [2, XCM, T])
        utmp0 = sb("utmp0", [2, T])
        place[0] = region_l
        ada = sb("ada", [2, 4, ADA_K])
        condg = sb("condg", [2, ADA_K])
        part = sb("part", [ADAL, 2])
        sz = sb("sz", [NC, T])
        region_y = place[0]
        pad = sb("pad", [2, 2, TC + TAPS - 1])
        xbc = sb("xbc", [6, T])
        after_xbc = place[0]
        ccur = sb("ccur", [T])
        xtok = sb("xtok", [NC, T])
        y_t = xtok
        btok = sb("btok", [NC, P])
        cbs = sb("cbs", [2, NC, P])
        am = sb("am", [2, 2, 4, P], F32R)
        em = sb("em", [2, 4, P])
        tmp = sb("tmp", [T])
        xw = sb("xw", [T])
        y = sb("y", [NC, T])
        state = sb("state", [T])
        tab = sb("tab", [TAB_ROWS, 64])
        gt = sb("gt", [TAB_ROWS, HG])
        a_hi = sb("a_hi", [8, HG], F32R)
        a_lo = sb("a_lo", [8, HG], F32R)
        convg = sb("convg", [36])
        normg = sb("normg", [4])
        place[0] = region_u
        y_all = sb("y_all", [2 * KT, T])
        place[0] = region_l
        r_c = sb("r_c", [2, D])
        place[0] = region_y
        yr_hi = sb("yr_hi", [2, 2, T], F32R)
        yr_lo = sb("yr_lo", [2, 2, T], F32R)
        assert place[0] <= after_xbc
        r_x = sb("r_x", [2, D])
        region_rows = place[0]
        gate0 = sb("gate0", [2, D])
        wtmp = sb("wtmp", [2, T])
        place[0] = region_rows
        rows0 = sb("rows0", [2, D])
        utmp1 = sb("utmp1", [2, T])
        bn = sb("bn", [NC, 24])
        place[0] = region_l
        sq = sb("sq", [2, T])
        rsd = sb("rsd", [2, T])
        gate1 = sb("gate1", [D])
        gates = sb("gates", [HEADS, TC])
        kr = sb("kr", [T])
        assert place[0] <= region_y + 16384
        place[0] = region_rows
        cq = sb("cq", [4, TC])
        ckv = sb("ckv", [4, T])
        cq_hi = sb("cq_hi", [4, TC], F32R)
        cq_lo = sb("cq_lo", [4, TC], F32R)
        ckv_hi = sb("ckv_hi", [4, T], F32R)
        ckv_lo = sb("ckv_lo", [4, T], F32R)
        trig = sb("trig", [2, TC])
        rot = sb("rot", [P])
        place[0] = region_u
        og_hi = sb("og_hi", [HEADS, TC], F32R)
        og_lo = sb("og_lo", [HEADS, TC], F32R)
        region_h = place[0]
        qn = sb("qn", [4, TC])
        qr = sb("qr", [2, TC])
        qrt = sb("qrt", [2, TC])
        kn = sb("kn", [4, T])
        v = sb("v", [NC, T])
        prob = sb("prob", [2, T])
        prob_t = sb("prob_t", [NC, TC])
        place[0] = region_h
        rows1 = sb("rows1", [2, D])
        bn_out = sb("bn_out", [2, 24])

        ps = ctx.enter_context(nc.psum_tensor("ps", [P, 8, T], F32))

        par_loaded, const_loaded, xcm_loaded, rows_loaded = (
            sem("par_loaded"), sem("const_loaded"), [sem(f"xcm_loaded{q}") for q in range(KT // XCM)],
            sem("rows_loaded"))
        tri_loaded = sem("tri_loaded")
        raw_loaded = [sem(f"raw_loaded{q}") for q in range(RING)]
        ada0_loaded = [sem(f"ada0_loaded{q}") for q in range(ADA0_RING)]
        ada_loaded = [sem(f"ada_loaded{q}") for q in range(2)]
        hi_ready, lo_ready, w_used = sem("hi_ready"), sem("lo_ready"), sem("w_used")
        ada0_pe, ada0_dve, ada_used = sem("ada0_pe"), sem("ada0_dve"), sem("ada_used")
        condg_loaded, condg_ready, am_ready = sem("condg_loaded"), sem("condg_ready"), sem("am_ready")
        rot_loaded, dx_ready, taps_ready, tap_ready = (
            sem("rot_loaded"), sem("dx_ready"), sem("taps_ready"), sem("tap_ready"))
        cond_loaded, cond_ready, mod0_ready, ada0_taken, utmp0_ready = (
            sem("cond_loaded"), sem("cond_ready"), sem("mod0_ready"), sem("ada0_taken"), sem("utmp0_ready"))
        consts_ready = sem("consts_ready")
        utmp_ready, uhi_ready, u_ready = sem("utmp_ready"), sem("uhi_ready"), sem("u_ready")
        dt_abs, dt_exp, a_ready = sem("dt_abs"), sem("dt_exp"), sem("a_ready")
        arow_exp = sem("arow_exp")
        cs_full, cs_diff, cs_exp = sem("cs_full"), sem("cs_diff"), sem("cs_exp")
        pads_clear, tile_evac = sem("pads_clear"), sem("tile_evac")
        conv_done, silu_done = sem("conv_done"), sem("silu_done")
        xt_full, xtok_ready, bt_full, btok_ready = (
            sem("xt_full"), sem("xtok_ready"), sem("bt_full"), sem("btok_ready"))
        cb_full, cbs_ready, slice_ready = sem("cb_full"), sem("cbs_ready"), sem("slice_ready")
        seg_full, decay_ready, m_ready, xw_ready = (
            sem("seg_full"), sem("decay_ready"), sem("m_ready"), sem("xw_ready"))
        yd_full, yd_taken, yo_full, yo_taken = (
            sem("yd_full"), sem("yd_taken"), sem("yo_full"), sem("yo_taken"))
        st_full, state_ready = sem("st_full"), sem("state_ready")
        gated, sq_done, var_ready, root_ready, y_normed = (
            sem("gated"), sem("sq_done"), sem("var_ready"), sem("root_ready"), sem("y_normed"))
        ada_taken = sem("ada_taken")
        yt_full, yt_evac, y_spilled = sem("yt_full"), sem("yt_evac"), sem("y_spilled")
        y_loaded, res_loaded = [sem(f"y_loaded{g}") for g in range(GROUPS - 1)], sem("res_loaded")
        g0_full, g0_taken, g0_taken_act = sem("g0_full"), sem("g0_taken"), sem("g0_taken_act")
        yhi_ready, ylo_ready, wo_taken = (
            sem("yhi_ready"), sem("ylo_ready"), sem("wo_taken"))
        rows0_loaded, lnvar_ready, lnroot_ready, ln_ready = (
            sem("rows0_loaded"), sem("lnvar_ready"), sem("lnroot_ready"), sem("ln_ready"))
        rt_full = sem("rt_full")
        x1_ready, trig_loaded = sem("x1_ready"), sem("trig_loaded")
        g1_full, g1_taken = sem("g1_full"), sem("g1_taken")
        gt_taken = sem("gt_taken")
        lat_taken, sq_ready, sq_used = (
            sem("lat_taken"), sem("sq_ready"), sem("sq_used"))
        msv_ready, msroot_ready, cn_ready, chi_ready, clo_ready = (
            sem("msv_ready"), sem("msroot_ready"), sem("cn_ready"),
            sem("chi_ready"), sem("clo_ready"))
        kr_ready, krot_full = sem("kr_ready"), sem("krot_full")
        hq_act, hq_dve = sem("hq_act"), sem("hq_dve")
        qrot_full, qr_ready = sem("qrot_full"), sem("qr_ready")
        s_full, max_ready, p_ready, p_scaled = (
            sem("s_full"), sem("max_ready"), sem("p_ready"), sem("p_scaled"))
        pt_full, pt_ready, o_full, o_taken, ogh_ready, ogl_ready = (
            sem("pt_full"), sem("pt_ready"), sem("o_full"), sem("o_taken"),
            sem("ogh_ready"), sem("ogl_ready"))
        out_taken, rows1_loaded, fvar_ready, froot_ready, out_ready, stored = (
            sem("out_taken"), sem("rows1_loaded"), sem("fvar_ready"), sem("froot_ready"),
            sem("out_ready"), sem("stored"))
        dve_step = sem("dve_step")

        block = ctx.enter_context(nc.Block())

        @block.sync
        def _(sp):
            def load_unit(s, slot, first=False):
                if not first:
                    sp.wait_ge(lo_ready, s - RING + 1)
                sp.dma_start(raw[:, slot, :], hbm["stream"][s]).then_inc(raw_loaded[slot], 16)

            sp.dma_start(par[:], hbm["par"]).then_inc(par_loaded, 16)
            sp.dma_start(cond_rows[:], hbm["cond_rows"].to_broadcast([P, 2, D])).then_inc(cond_loaded, 16)
            for n in range(ADA0):
                if n >= ADA0_RING:
                    if n - ADA0_RING in ADA0_ON_PE:
                        sp.wait_ge(ada0_pe, ADA0_ON_PE.index(n - ADA0_RING) + 1)
                    else:
                        sp.wait_ge(ada0_dve, ADA0_ON_DVE.index(n - ADA0_RING) + 1)
                sp.dma_start(ada0[:, n % ADA0_RING], hbm["ada0"][n].rearrange("p (k n) -> p k n", k=KT)).then_inc(
                    ada0_loaded[n % ADA0_RING], 16)
                if n == 1:
                    for m, c in enumerate((ident, ones)):
                        sp.dma_start(c[:], hbm["consts"][m]).then_inc(const_loaded, 16)
                    sp.dma_start(utmp0[:, 0, :].rearrange("p (a b) -> p a b", a=4),
                                 hbm["consts"][3:7].rearrange("a p b -> p a b")).then_inc(tri_loaded, 16)
                if n in (1, 6, 16, 24):
                    q = (1, 6, 16, 24).index(n)
                    if q >= 2:
                        sp.wait_ge(utmp0_ready, XCM * (q - 1))
                    sp.dma_start(xcm[:, q % 2], hbm["x_cm"][:, XCM * q:XCM * q + XCM]).then_inc(xcm_loaded[q], 16)
                if n in (2, 4):
                    load_unit(n // 2 - 1, n // 2 - 1, first=True)
            for s in range(DT_UNITS, RING):
                load_unit(s, s, first=True)
            sp.wait_ge(u_ready, KT)
            sp.dma_start(y[:, 0, 0:128], hbm["dt_bias"].to_broadcast([P, 128])).then_inc(rows_loaded, 16)
            sp.dma_start(y[:, 1, 0:128], hbm["a_log"].to_broadcast([P, 128])).then_inc(rows_loaded, 16)
            sp.dma_start(tab[:, D_ROW, :], hbm["d_skip"].to_broadcast([P, 64])).then_inc(rows_loaded, 16)
            for s in range(RING, DT_UNITS + PROJ_UNITS):
                load_unit(s, s % RING)

            def load_ada(g, n):
                for u in (2 * n, 2 * n + 1):
                    if u >= 2 or not isinstance(g, int) or g > 0:
                        sp.wait_ge(ada_used, g * ADA_UNITS * ADA_DOTS + (u - 1) * ADA_DOTS)
                    sp.dma_start(ada[:, u % 2], hbm["ada"][g * ADA_UNITS + u]).then_inc(ada_loaded[u % 2], 16)

            def load_cond(g):
                if not isinstance(g, int) or g > 0:
                    sp.wait_ge(ada_used, g * ADA_UNITS * ADA_DOTS)
                sp.dma_start(condg[:], hbm["cond_groups"][g].to_broadcast([P, 2, ADA_K])).then_inc(condg_loaded, 16)

            def load_group(g):
                for j in range(PROJ_UNITS):
                    load_unit(DT_UNITS + PROJ_UNITS * (g + 1) + j, (DT_UNITS + j) % RING)
                    if j == 6:
                        load_cond(g)
                    if j % 2 == 0 and j >= 8:
                        load_ada(g, j // 2 - 4)
                load_ada(g, 6)
                load_ada(g, 7)

            load_group(0)
            with sp.Fori(1, GROUPS - 1) as i:
                load_group(i)
            for s in range(WOUT_AT, WOUT_AT + RING):
                load_unit(s, s % RING)
            sp.wait_ge(w_used, WOUT_AT)
            sp.wait_ge(y_spilled, 16 * (GROUPS - 2))
            for g in range(GROUPS - 1):
                if g == 1:
                    sp.wait_ge(y_spilled, 16 * (GROUPS - 1))
                sp.dma_start(y_all[:, g * GT:g * GT + GT, :], hbm["y"][g]).then_inc(y_loaded[g], 16)
            load_cond(GROUPS - 1)
            load_ada(GROUPS - 1, 0)
            for j in range(RING, PROJ_UNITS):
                load_unit(WOUT_AT + j, (WOUT_AT + j) % RING)
                if j % 2 == 0 and j < 18:
                    load_ada(GROUPS - 1, j // 2 - 1)
            late = WOUT_AT + PROJ_UNITS
            sp.wait_ge(y_normed, GROUPS)
            sp.wait_ge(ada_taken, GROUPS)
            for n, rows in enumerate((r_c, r_x)):
                sp.dma_start(rows[:], hbm["x_tm"][2 * n:2 * n + 2].rearrange("c p n -> p c n")).then_inc(
                    res_loaded, 16)
            with sp.Fori(0, (MLA_AT + RING - late) // RING) as i:
                for q in range(RING):
                    load_unit(i * RING + (late + q), (late + q) % RING)
            sp.wait_ge(wo_taken, NC * 4)
            for n in range(2):
                sp.dma_start(rows0[:, n, :], hbm["ln_rows"][0, n].to_broadcast([P, D])).then_inc(rows0_loaded, 16)
            sp.dma_start(trig[:], hbm["trig"]).then_inc(trig_loaded, 16)
            sp.dma_start(rot[:], hbm["consts"][2]).then_inc(rot_loaded, 16)
            with sp.Fori(0, (UNITS - MLA_AT - RING) // RING - 1) as i:
                for q in range(RING):
                    load_unit(i * RING + (MLA_AT + RING + q), (MLA_AT + q) % RING)
            sp.wait_ge(ogl_ready, HEADS)
            for n in range(2):
                sp.dma_start(rows1[:, n, :], hbm["ln_rows"][1, n].to_broadcast([P, D])).then_inc(rows1_loaded, 16)
            for s in range(MLA_AT + RING * ((UNITS - MLA_AT - RING) // RING), UNITS):
                load_unit(s, s % RING)
            for c in range(2):
                sp.wait_ge(out_ready, c + 1)
                sp.dma_start(hbm["out"][0, c * P:c * P + P, :], r_x[:, c]).then_inc(stored, 16)
            sp.wait_ge(stored, 32)

        @block.gpsimd
        def _(pool):
            def low(s, slot):
                pool.wait_ge(hi_ready, s + 1)
                nc.gpsimd.tensor_tensor(w_lo[:, slot], raw[:, slot], w_hi[:, slot].bitcast(F32),
                                        ALU.subtract).then_inc(lo_ready, 1)

            def low_u(layer, buffers):
                for k in range(KT):
                    pool.wait_ge(uhi_ready, layer * KT + k + 1)
                    nc.gpsimd.tensor_tensor(u_lo[:, k], buffers[:, k % 2], u_hi[:, k].bitcast(F32),
                                            ALU.subtract).then_inc(u_ready, 1)

            ahead = DT_UNITS + PROJ_UNITS + SPLIT_AHEAD
            for s in range(ahead):
                if s == DT_UNITS:
                    low_u(0, utmp0)
                low(s, s % RING)

            def group(g, proj):
                heads = lambda ap: ap.rearrange("p (h d) -> p h d", h=HG)
                for j in range(PROJ_UNITS):
                    if 2 <= j < 2 + NC:
                        c = j - 2
                        pool.wait_ge(xtok_ready, g * NC + NC)
                        pool.wait_ge(yt_full, g * GT)
                        pool.wait_ge(slice_ready, g + 1)
                        nc.gpsimd.tensor_tensor(heads(y[:, c]), heads(xtok[:, c]), gt[:, D_ROW, :].unsqueeze(
                            2).to_broadcast([P, HG, HD]), ALU.mult).then_inc(dx_ready, 1)
                    h, odd = divmod(j, 2)
                    if odd and h < 8:
                        c = DIAG[h // 2]
                        pool.wait_ge(slice_ready, g + 1)
                        pool.wait_ge(seg_full, g * 8 + h)
                        for n, a in enumerate((a_hi, a_lo)):
                            for d in range(2):
                                a4 = a[:, 2 * c + d, h % 2 * 4:h % 2 * 4 + 4].bitcast(F32)
                                ins = nc.gpsimd.tensor_tensor(
                                    am[:, n, d], tri[:, d].bitcast(F32).unsqueeze(1).to_broadcast([P, 4, P]),
                                    a4.unsqueeze(2).to_broadcast([P, 4, P]), ALU.mult)
                        ins.then_inc(am_ready, 1)
                    if proj:
                        low(g * PROJ_UNITS + (ahead + j), (ahead + j) % RING)
                    elif 0 <= j - EARLY_FROM < EARLY:
                        s = WOUT_AT + SPLIT_AHEAD + j - EARLY_FROM
                        low(s, s % RING)
                    n = j // 2 - 1
                    if j % 2 == 0 and n in MAKES_STATE:
                        d, c = STEPS[n]
                        pool.wait_ge(st_full, g * 6 + MAKES_STATE.index(n))
                        nc.gpsimd.tensor_tensor(heads(xw[:]), heads(xtok[:, c]), gt[:, WST_ROW + 2 * c + d, :].unsqueeze(
                            2).to_broadcast([P, HG, HD]), ALU.mult).then_inc(xw_ready, 1)

            pool.wait_ge(consts_ready, 1)
            group(0, True)
            with pool.Fori(1, GROUPS - 1) as i:
                group(i, True)
            group(GROUPS - 1, False)
            at = WOUT_AT + SPLIT_AHEAD + EARLY
            end = MLA_AT + SPLIT_AHEAD
            with pool.Fori(0, (end - at) // RING) as i:
                for q in range(RING):
                    low(i * RING + (at + q), (at + q) % RING)
            for s in range(end - (end - at) % RING, end):
                low(s, s % RING)
            low_u(1, utmp1)
            with pool.Fori(0, (UNITS - end) // RING) as i:
                for q in range(RING):
                    low(i * RING + (end + q), (end + q) % RING)
            for s in range(UNITS - (UNITS - end) % RING, UNITS):
                low(s, s % RING)

        @block.scalar
        def _(act):
            def split_high(s, slot, turn, first=False):
                act.wait_ge(raw_loaded[slot], 16 * turn)
                if not first:
                    act.wait_ge(w_used, s - RING + 1)
                nc.scalar.activation(w_hi[:, slot], raw[:, slot], ACT.Copy).then_inc(hi_ready, 1)

            def split_at(s):
                split_high(s, s % RING, turn=s // RING + 1, first=s < RING)

            act.wait_ge(par_loaded, 16)
            nc.scalar.activation(cond[:], par[:, COND_AT:COND_AT + 32].rearrange("p (k v) -> p k v", v=2),
                                 ACT.Silu).then_inc(cond_ready, 1)
            act.wait_ge(cond_loaded, 16)
            nc.scalar.activation(cond_rows[:], cond_rows[:], ACT.Silu).then_inc(cond_ready, 1)
            for s in range(DT_UNITS):
                split_at(s)
            act.wait_ge(consts_ready, 1)
            for k in range(KT):
                act.wait_ge(mod0_ready, k + 1)
                act.wait_ge(xcm_loaded[k // XCM], 16)
                if k >= 2:
                    act.wait_ge(u_ready, k - 1)
                for s in range(2):
                    ins = nc.scalar.activation(
                        utmp0[:, k % 2, s * TC:s * TC + TC], xcm[:, k // XCM % 2, k % XCM, s * TC:s * TC + TC],
                        ACT.Identity, scale=mod0[:, KT + k, s:s + 1], bias=mod0[:, k, s:s + 1])
                ins.then_inc(utmp0_ready, 1)
                act.wait_ge(utmp0_ready, k + 1)
                nc.scalar.activation(u_hi[:, k], utmp0[:, k % 2], ACT.Copy).then_inc(uhi_ready, 1)
            for s in range(DT_UNITS, DT_UNITS + SPLIT_AHEAD):
                split_at(s)
            act.wait_ge(rows_loaded, 48)
            nc.scalar.activation(y[:, 2, 0:128], y[:, 1, 0:128], ACT.Exp).then_inc(arow_exp, 1)
            act.wait_ge(dt_abs, 1)
            nc.scalar.activation(xw[:], y[:, 3], ACT.Exp, scale=-1.0).then_inc(dt_exp, 1)

            def evac_tile(g, t):
                act.wait_ge(w_used, DT_UNITS + PROJ_UNITS * g + 2 * t + 2)
                if not (isinstance(g, int) and g == 0 and t < 2):
                    act.wait_ge(conv_done, 6 * g + t - 1)
                else:
                    act.wait_ge(pads_clear, 1)
                nc.scalar.activation(pad[:, t % 2, :, 2:2 + TC],
                                     ps[:, t % 4].rearrange("p (s n) -> p s n", s=2),
                                     ACT.Copy).then_inc(tile_evac, 1)
                act.wait_ge(tile_evac, 10 * g + t + 1)
                act.wait_ge(taps_ready, g + 1)
                if not (isinstance(g, int) and g == 0):
                    act.wait_ge(silu_done, 6 * g)
                    act.wait_ge(xt_full, NC * g)
                    act.wait_ge(bt_full, g)
                    act.wait_ge(cbs_ready, g)
                nc.scalar.activation(xbc[:, t].rearrange("p (s n) -> p s n", s=2), pad[:, t % 2, :, 0:TC],
                                     ACT.Identity, scale=convg[:, 5 * t:5 * t + 1],
                                     bias=convg[:, 30 + t:31 + t]).then_inc(tap_ready, 1)

            def silu_tile(g, t):
                act.wait_ge(conv_done, 6 * g + t + 1)
                nc.scalar.activation(xbc[:, t], xbc[:, t], ACT.Silu).then_inc(silu_done, 1)

            def silu_z(g):
                for c in range(NC):
                    act.wait_ge(w_used, DT_UNITS + PROJ_UNITS * (g + 1))
                    nc.scalar.activation(sz[:, c], ps[:, c], ACT.Silu).then_inc(tile_evac, 1)

            for j in range(PROJ_UNITS):
                split_at(DT_UNITS + j + SPLIT_AHEAD)
                if j % 2 == 0 and 2 <= j < 14:
                    evac_tile(0, j // 2 - 1)
                if j == 5:
                    act.wait_ge(cs_diff, 1)
                    nc.scalar.activation(tab[:, ECS_ROW:ECS_ROW + 8].rearrange("p r h -> p (r h)"), ps[:, 5], ACT.Exp).then_inc(cs_exp, 1)
                    nc.scalar.activation(tab[:, ETOT_ROW:ETOT_ROW + 8].rearrange("p r h -> p (r h)"), ps[:, 6], ACT.Exp).then_inc(cs_exp, 1)
                    nc.scalar.activation(xw[:], xw[:], ACT.Exp).then_inc(cs_exp, 1)
            for t in range(6):
                silu_tile(0, t)
            silu_z(0)

            def y_high(u):
                u = u % WOUT_UNITS
                nc.scalar.activation(yr_hi[:, u % 2], y_all[:, 2 * u:2 * u + 2], ACT.Copy).then_inc(yhi_ready, 1)

            def group(g, proj):
                for j in range(PROJ_UNITS):
                    if not proj and j == EARLY_FROM - 1:
                        act.wait_ge(bt_full, GROUPS)
                        act.wait_ge(cbs_ready, GROUPS)
                        act.wait_ge(y_loaded[0], 16)
                        y_high(0)
                    if not proj and 0 <= j - EARLY_FROM < EARLY:
                        u = j - EARLY_FROM
                        s = WOUT_AT + u + SPLIT_AHEAD
                        split_high(s, s % RING, turn=s // RING + 1)
                        if u + 1 < EARLY:
                            act.wait_ge(y_loaded[(u + 1) // 2], 16)
                            y_high(u + 1)
                    if proj:
                        s = DT_UNITS + PROJ_UNITS + j + SPLIT_AHEAD
                        act.wait_ge(raw_loaded[s % RING], 16 * (s // RING + 1) + g * 16 * (PROJ_UNITS // RING))
                        act.wait_ge(w_used, g * PROJ_UNITS + (s - RING + 1))
                        nc.scalar.activation(w_hi[:, s % RING], raw[:, s % RING], ACT.Copy).then_inc(hi_ready, 1)
                        if j % 2 == 0 and 2 <= j < 14:
                            evac_tile(g + 1, j // 2 - 1)
                    if j == 1:
                        for c in range(NC):
                            act.wait_ge(xt_full, NC * g + c + 1)
                            act.wait_ge(y_spilled, 16 * g)
                            act.wait_ge(gated, NC * g)
                            nc.scalar.activation(xtok[:, c], ps[:, X_BANK[c]], ACT.Copy).then_inc(xtok_ready, 1)
                    if j == 2:
                        act.wait_ge(bt_full, g + 1)
                        act.wait_ge(st_full, 6 * g)
                        nc.scalar.activation(btok[:].rearrange("p c n -> p (c n)"), ps[:, 6], ACT.Copy).then_inc(btok_ready, 1)
                    if j == 3:
                        act.wait_ge(condg_loaded, 16 * g + 16)
                        nc.scalar.activation(condg[:], condg[:], ACT.Silu).then_inc(condg_ready, 1)
                    if j % 2 == 0 and 2 <= j < 18:
                        h = j // 2 - 1
                        act.wait_ge(seg_full, 8 * g + h + 1)
                        act.wait_ge(yd_full, 8 * g + max(h - 1, 0))
                        nc.scalar.activation(em[:, h % 2].rearrange("p a n -> p (a n)"), ps[:, 4 + h % 2],
                                             ACT.Exp).then_inc(decay_ready, 1)
                    if proj and j % 2 == 0 and j >= 8:
                        silu_tile(g + 1, j // 2 - 4)
                    if j in (13, 15, 17, 19):
                        m = (j - 13) // 2
                        c = STEPS[4 + m][1]
                        act.wait_ge(gated, NC * g + m + 1)
                        nc.scalar.activation(sz[:, c], y[:, c], ACT.Square,
                                             accum_out=stat[:, c:c + 1]).then_inc(sq_done, 1)
                act.wait_ge(var_ready, g + 1)
                nc.scalar.activation(stat[:, 8:12], stat[:, 4:8], ACT.Sqrt).then_inc(root_ready, 1)
                if proj:
                    silu_z(g + 1)
                for k in range(GT):
                    act.wait_ge(yt_full, GT * g + k + 1)
                    dst = y_t[:, k] if proj else y_all[:, GT * g + k]
                    nc.scalar.activation(dst, ps[:, 4 + k], ACT.Copy, scale=normg[:, k:k + 1]).then_inc(yt_evac, 1)
                if proj:
                    act.wait_ge(yt_evac, GT * g + GT)
                    act.dma_start(hbm["y"][g], y_t[:]).then_inc(y_spilled, 16)

            group(0, True)
            with act.Fori(1, GROUPS - 1) as i:
                group(i, True)
            group(GROUPS - 1, False)

            act.wait_ge(yt_evac, GT * GROUPS)
            y_high(EARLY)
            for b in range(4):
                act.wait_ge(g0_full, b + 1)
                nc.scalar.activation(gate0[:, 0, b * T:b * T + T], ps[:, 4 + b], ACT.Copy).then_inc(g0_taken_act, 1)
            for u in range(EARLY, WOUT_UNITS):
                s = WOUT_AT + u + SPLIT_AHEAD
                split_high(s, s % RING, turn=s // RING + 1)
                y_high(u + 1)
            with act.Fori(0, 3) as i:
                for u in range(WOUT_UNITS):
                    s = WOUT_AT + WOUT_UNITS + u + SPLIT_AHEAD
                    split_high(i * WOUT_UNITS + s, s % RING, turn=i * (WOUT_UNITS // RING) + (s // RING + 1))
                    y_high(u + 1)

            act.wait_ge(lnvar_ready, 1)
            nc.scalar.activation(stat[:, 20:24], stat[:, 16:20], ACT.Sqrt).then_inc(lnroot_ready, 1)
            for k in range(KT):
                act.wait_ge(utmp_ready, k + 1)
                nc.scalar.activation(u_hi[:, k], utmp1[:, k % 2], ACT.Copy).then_inc(uhi_ready, 1)

            with act.Fori(0, 4) as i:
                for t in range(4):
                    for half in range(2):
                        s = MLA_AT + 2 * t + half + SPLIT_AHEAD
                        split_high(i * 8 + s, s % RING, turn=i * 2 + (s // RING + 1))
                    act.wait_ge(w_used, i * 8 + (MLA_AT + 2 * t + 2))
                    nc.scalar.activation(gates[:, bass.ds(i * 4 + t, 1), :].rearrange("p a n -> p (a n)"),
                                         ps[:, t, 0:TC], ACT.Silu).then_inc(gt_taken, 1)
            def latent_root(m):
                n = (TC, T)[m]
                act.wait_ge(msv_ready, m + 1)
                nc.scalar.activation(rsd[:, m, 0:n], rsd[:, m, 0:n], ACT.Sqrt).then_inc(msroot_ready, 1)

            def latent_high(m):
                for t in range(4):
                    act.wait_ge(cn_ready, 4 * m + t + 1)
                    nc.scalar.activation((cq_hi, ckv_hi)[m][:, t], (cq, ckv)[m][:, t], ACT.Copy).then_inc(chi_ready, 1)

            lat = MLA_AT + GATE_UNITS
            for j in range(LATENT_UNITS):
                s = lat + j + SPLIT_AHEAD
                split_high(s, s % RING, turn=s // RING + 1)
                if j % 2 == 1:
                    t = j // 2
                    act.wait_ge(w_used, lat + j + 1)
                    if t == 0:
                        act.wait_ge(x1_ready, 1)
                    if t < 4:
                        src, dst = ps[:, 4 + t, 0:TC], cq[:, t]
                    elif t < 8:
                        src, dst = ps[:, t - 4], ckv[:, t - 4]
                    else:
                        src, dst = ps[:, 4], kr[:]
                    nc.scalar.activation(dst, src, ACT.Copy).then_inc(lat_taken, 1)
                    if t < 8:
                        if t >= 2:
                            act.wait_ge(sq_used, t - 1)
                        n = TC if t < 4 else T
                        nc.scalar.activation(sq[:, t % 2, 0:n], src, ACT.Square).then_inc(sq_ready, 1)
                    if t == 6:
                        latent_root(0)
                    if t == 8:
                        latent_high(0)
            latent_root(1)
            latent_high(1)

            for b in range(4):
                for j in range(HEAD_UNITS):
                    s = HEAD_AT + b * HEAD_UNITS + j + SPLIT_AHEAD
                    split_high(s, s % RING, turn=s // RING + 1)
                    if j < 2:
                        act.wait_ge(w_used, s - SPLIT_AHEAD + 1)
                        act.wait_ge(s_full, 8 * b)
                        nc.scalar.activation(qn[:, 2 * j:2 * j + 2].rearrange("p a n -> p (a n)"), ps[:, j], ACT.Copy).then_inc(hq_act, 1)
                    if j in (3, 4):
                        act.wait_ge(w_used, s - SPLIT_AHEAD + 1)
                        for n in range(2):
                            nc.scalar.activation(kn[:, 2 * (j - 3) + n], ps[:, 3 + 2 * (j - 3) + n], ACT.Copy).then_inc(hq_act, 1)
                act.wait_ge(w_used, HEAD_AT + HEAD_UNITS * (b + 1))
                act.wait_ge(o_full, 4 * b)
                for n in range(2):
                    nc.scalar.activation(v[:, n], ps[:, n], ACT.Copy).then_inc(hq_act, 1)

                def exp_scores(n):
                    m = 8 * b + n
                    act.wait_ge(max_ready, m + 1)
                    if m >= 2:
                        act.wait_ge(pt_full, m - 1)
                    nc.scalar.activation(prob[:, n % 2], ps[:, SCORE_BANK[n % 4]], ACT.Exp, bias=stat[:, 32 + n:33 + n],
                                         scale=SCALE, accum_out=stat[:, 40 + n:41 + n]).then_inc(p_ready, 1)

                def gated_high(hh):
                    act.wait_ge(o_taken, 4 * b + hh + 1)
                    nc.scalar.activation(og_hi[:, 4 * b + hh], sq[:, hh % 2, 0:TC], ACT.Copy).then_inc(ogh_ready, 1)

                for n in range(8):
                    exp_scores(n)
                    if n % 2 == 1 and n >= 3:
                        gated_high(n // 2 - 1)
                gated_high(3)

            with act.Fori(0, 3) as i:
                for u in range(WO_UNITS):
                    s = WO_AT + u + SPLIT_AHEAD
                    split_high(i * WO_UNITS + s, s % RING, turn=i * (WO_UNITS // RING) + (s // RING + 1))
            for s in range(WO_AT + 3 * WO_UNITS + SPLIT_AHEAD, UNITS):
                split_high(s, s % RING, turn=s // RING + 1)
            act.wait_ge(fvar_ready, 1)
            nc.scalar.activation(stat[:, 28:30], stat[:, 24:26], ACT.Sqrt).then_inc(froot_ready, 1)

        @block.vector
        def _(dve):
            step = Step(dve, dve_step)
            link = step.link
            vec = nc.vector

            dve.wait_ge(const_loaded, 32)
            dve.wait_ge(tri_loaded, 16)
            dve.wait_ge(par_loaded, 16)
            link(vec.tensor_copy(tri[:].rearrange("p a b -> p (a b)"), utmp0[:, 0, 0:256]))
            link(vec.tensor_copy(strict[:].rearrange("p a b -> p (a b)"), utmp0[:, 0, 256:512]))
            vec.memset(stat[:], 0.0).then_inc(consts_ready, 1)

            link(vec.tensor_copy(modl[:], par[:, ADAL_AT:ADAL_AT + ADAL].unsqueeze(2).to_broadcast([P, ADAL, 2])))

            dve.wait_ge(cond_ready, 2)
            pair = lambda ap, k: ap.rearrange("p (a k) v -> p a k v", a=2)[:, :, k]
            for n in range(ADA0):
                t = ADA0_ORDER[n]
                if n in ADA0_ON_DVE:
                    dve.wait_ge(ada0_loaded[n % ADA0_RING], 16 * (n // ADA0_RING + 1))
                    for s in range(2):
                        ins = vec.scalar_tensor_tensor(
                            out=products[:], in0=ada0[:, n % ADA0_RING].rearrange("p k n -> p (k n)"), scalar=1.0,
                            in1=cond_rows[:, s], op0=ALU.mult, op1=ALU.mult, accum_out=mod0[:, t, s:s + 1])
                        if s == 0:
                            link(ins)
                    ins.then_inc(ada0_dve, 1)
                    dve.wait_ge(ada0_dve, ADA0_ON_DVE.index(n) + 1)
                else:
                    m = ADA0_ON_PE.index(n)
                    dve.wait_ge(ada0_pe, m + 1)
                    vec.tensor_copy(mod0[:, t], ps[:, 4 + m % 4, 0:2]).then_inc(ada0_taken, 1)
                    dve.wait_ge(ada0_taken, m + 1)
                if n % 2 == 1:
                    k = n // 2
                    bias = par[:, ADA0_AT:ADA0_AT + 32].unsqueeze(2).to_broadcast([P, 32, 2])
                    link(vec.tensor_tensor(pair(mod0[:], k), pair(mod0[:], k), pair(bias, k), ALU.add))
                    vec.tensor_scalar(mod0[:, KT + k], mod0[:, KT + k], 1.0, None, ALU.add).then_inc(mod0_ready, 1)

            def modulate(k, dst, src, scale, shift):
                if k >= 2:
                    dve.wait_ge(u_ready, KT + k - 1)
                for s in range(2):
                    ins = vec.tensor_scalar(dst[:, s * TC:s * TC + TC], src[:, s * TC:s * TC + TC],
                                            scale[:, s:s + 1], shift[:, s:s + 1], ALU.mult, ALU.add)
                    if s == 0:
                        link(ins)
                return ins.then_inc(utmp_ready, 1)

            dve.wait_ge(u_ready, KT)
            link(vec.memset(pad[:, :, :, 0:2], 0.0))
            vec.memset(pad[:, :, :, 2 + TC:4 + TC], 0.0).then_inc(pads_clear, 1)

            def conv_weights(g_next):
                if isinstance(g_next, int):
                    src = par[:, CONV_AT + 36 * g_next:CONV_AT + 36 * g_next + 36]
                else:
                    src = par[:, bass.ds(g_next * 36 + CONV_AT, 36)]
                if not isinstance(g_next, int) or g_next > 0:
                    dve.wait_ge(tap_ready, 6 * g_next)
                vec.tensor_copy(convg[:], src).then_inc(taps_ready, 1)
                dve.wait_ge(taps_ready, g_next + 1)

            conv_weights(0)

            chunks = lambda ap: ap.rearrange("p (c h) -> p c h", c=NC)
            dve.wait_ge(w_used, DT_UNITS)
            dve.wait_ge(rows_loaded, 48)
            link(vec.tensor_tensor(chunks(tmp[:]), ps[:, 0:4, 0:128],
                                   y[:, 0, 0:128].unsqueeze(1).to_broadcast([P, NC, 128]), ALU.add))
            vec.scalar_tensor_tensor(out=y[:, 3], in0=tmp[:], scalar=-1.0, in1=tmp[:], op0=ALU.mult,
                                     op1=ALU.max).then_inc(dt_abs, 1)
            dve.wait_ge(dt_exp, 1)
            link(vec.tensor_scalar(y[:, 3], xw[:], 2.0, None, ALU.add))
            link(vec.reciprocal(y[:, 3], y[:, 3]))
            link(vec.tensor_tensor(y[:, 3], y[:, 3], xw[:], ALU.mult))
            link(vec.tensor_tensor(xw[:], y[:, 3], y[:, 3], ALU.mult))
            link(vec.tensor_scalar(state[:], xw[:], 1.0 / 15.0, None, ALU.mult))
            for m in (13, 11, 9, 7, 5, 3):
                link(vec.scalar_tensor_tensor(out=state[:], in0=state[:], scalar=1.0 / m, in1=xw[:],
                                              op0=ALU.add, op1=ALU.mult))
            link(vec.scalar_tensor_tensor(out=state[:], in0=state[:], scalar=1.0, in1=y[:, 3],
                                          op0=ALU.add, op1=ALU.mult))
            link(vec.tensor_scalar(tmp[:], tmp[:], 0.0, None, ALU.max))
            flat = lambda r: tab[:, r:r + 8].rearrange("p r h -> p (r h)")
            link(vec.scalar_tensor_tensor(out=flat(DT_ROW), in0=state[:], scalar=2.0, in1=tmp[:],
                                          op0=ALU.mult, op1=ALU.add))
            dve.wait_ge(arow_exp, 1)
            link(vec.tensor_tensor(chunks(flat(A_ROW)), chunks(flat(DT_ROW)),
                                   y[:, 2, 0:128].unsqueeze(1).to_broadcast([P, NC, 128]), ALU.mult))
            vec.tensor_scalar(flat(A_ROW), flat(A_ROW), -1.0, None, ALU.mult).then_inc(a_ready, 1)
            dve.wait_ge(cs_full, 1)
            link(vec.tensor_scalar(state[:], ps[:, 5], -1.0, None, ALU.mult))
            vec.tensor_tensor(xw[:], ps[:, 6], state[:], ALU.add).then_inc(cs_diff, 1)
            dve.wait_ge(cs_exp, 3)
            link(vec.tensor_tensor(flat(WST_ROW), xw[:], flat(DT_ROW), ALU.mult))

            def conv(g, t):
                out = xbc[:, t].rearrange("p (s n) -> p s n", s=2)
                dve.wait_ge(tap_ready, 6 * g + t + 1)
                for j in range(1, TAPS):
                    ins = vec.scalar_tensor_tensor(out=out, in0=pad[:, t % 2, :, j:j + TC],
                                                   scalar=convg[:, 5 * t + j:5 * t + j + 1], in1=out,
                                                   op0=ALU.mult, op1=ALU.add)
                    if j < TAPS - 1:
                        link(ins)
                ins.then_inc(conv_done, 1)

            for t in range(6):
                conv(0, t)

            def y_low(count, u):
                dve.wait_ge(yhi_ready, count)
                u = u % WOUT_UNITS
                vec.tensor_tensor(yr_lo[:, u % 2], y_all[:, 2 * u:2 * u + 2], yr_hi[:, u % 2].bitcast(F32),
                                  ALU.subtract).then_inc(ylo_ready, 1)

            def group(g, proj):
                if isinstance(g, int):
                    src = tab[:, :, g * HG:g * HG + HG]
                    nsrc = par[:, NORM_AT + GT * g:NORM_AT + GT * g + GT]
                else:
                    src = tab[:, :, bass.ds(g * HG, HG)]
                    nsrc = par[:, bass.ds(g * GT + NORM_AT, GT)]
                dve.wait_ge(am_ready, 8 * g)
                link(vec.tensor_copy(gt[:], src))
                link(vec.tensor_copy(a_hi[:], gt[:, A_ROW:A_ROW + 8]))
                vec.tensor_tensor(a_lo[:], gt[:, A_ROW:A_ROW + 8], a_hi[:].bitcast(F32),
                                  ALU.subtract).then_inc(slice_ready, 1)
                dve.wait_ge(yt_evac, GT * g)
                link(vec.tensor_copy(normg[:], nsrc))
                if proj:
                    conv_weights(g + 1)
                dve.wait_ge(ada_taken, g)

                dve.wait_ge(cb_full, g + 1)
                for d in range(2):
                    ins = vec.tensor_tensor(cbs[:, d], ps[:, 7].rearrange("p (c n) -> p c n", c=NC),
                                            tri[:, d].bitcast(F32).unsqueeze(1).to_broadcast([P, NC, P]), ALU.mult)
                link(ins)
                dve.wait_ge(yo_full, 6 * g)
                vec.tensor_copy(ccur[:], xbc[:, 5]).then_inc(cbs_ready, 1)

                heads = lambda ap: ap.rearrange("p (h d) -> p h d", h=HG)
                per_head = lambda row: gt[:, row, :].unsqueeze(2).to_broadcast([P, HG, HD])

                def weighed(h):
                    c = DIAG[h // 2]
                    row = lambda d, a: gt[:, DT_ROW + 2 * c + d, h % 2 * 4 + a:h % 2 * 4 + a + 1]
                    for a in range(4):
                        ins = vec.tensor_scalar(tmp[:, a * P:a * P + P], cbs[:, 0, c], row(0, a), None, ALU.mult)
                    link(ins)
                    for a in range(4):
                        ins = vec.scalar_tensor_tensor(out=tmp[:, a * P:a * P + P], in0=cbs[:, 1, c], scalar=row(1, a),
                                                       in1=tmp[:, a * P:a * P + P], op0=ALU.mult, op1=ALU.add)
                    link(ins)
                    dve.wait_ge(decay_ready, 8 * g + h + 1)
                    vec.tensor_tensor(em[:, h % 2], em[:, h % 2], tmp[:].rearrange("p (a n) -> p a n", a=4),
                                      ALU.mult).then_inc(m_ready, 1)

                def ada_share(n):
                    if n == 0:
                        dve.wait_ge(condg_ready, g + 1)
                    dve.wait_ge(m_ready, 8 * g + n + 1)
                    for u in (2 * n, 2 * n + 1):
                        dve.wait_ge(ada_loaded[u % 2], g * 16 * (ADA_UNITS // 2) + 16 * (u // 2 + 1))
                        for t in range(4):
                            for s in range(2):
                                m = u * ADA_DOTS + 2 * t + s
                                if m >= 2:
                                    dve.wait_ge(ada_used, g * ADA_UNITS * ADA_DOTS + (m - 1))
                                vec.scalar_tensor_tensor(
                                    out=tmp[:, s * ADA_K:s * ADA_K + ADA_K], in0=ada[:, u % 2, t], scalar=1.0, in1=condg[:, s],
                                    op0=ALU.mult, op1=ALU.mult, accum_out=part[:, 4 * u + t, s:s + 1]).then_inc(ada_used, 1)
                    dve.wait_ge(ada_used, g * ADA_UNITS * ADA_DOTS + (2 * n + 2) * ADA_DOTS)

                dve.wait_ge(xtok_ready, NC * g + NC)
                dve.wait_ge(cbs_ready, g + 1)
                for n in range(8):
                    d, c = STEPS[n]
                    weighed(n)
                    if not proj and 2 * n < EARLY:
                        y_low(2 * n + 1, 2 * n)
                    if n in READS_STATE:
                        dve.wait_ge(yo_full, 6 * g + READS_STATE.index(n) + 1)
                        dve.wait_ge(m_ready, 8 * g + n + 1)
                        vec.tensor_tensor(heads(tmp[:]), heads(ps[:, 7]), per_head(ECS_ROW + 2 * c + d),
                                          ALU.mult).then_inc(yo_taken, 1)
                    if n in MAKES_STATE and n in READS_STATE:
                        link(vec.tensor_tensor(heads(state[:]), heads(state[:]), per_head(ETOT_ROW + 2 * c + d), ALU.mult))
                    if d == 0:
                        dve.wait_ge(dx_ready, NC * g + n + 1)
                    if n in READS_STATE:
                        dve.wait_ge(yo_taken, 6 * g + READS_STATE.index(n) + 1)
                        link(vec.tensor_tensor(y[:, c], y[:, c], tmp[:], ALU.add))
                    if n in MAKES_STATE:
                        dve.wait_ge(st_full, 6 * g + MAKES_STATE.index(n) + 1)
                        if n in READS_STATE:
                            vec.tensor_tensor(state[:], state[:], ps[:, 7], ALU.add).then_inc(state_ready, 1)
                        else:
                            vec.tensor_copy(state[:], ps[:, 7]).then_inc(state_ready, 1)
                    if n % 2 == 1:
                        own = DIAG[n // 2]
                        dve.wait_ge(yd_full, 8 * g + n + 1)
                        vec.tensor_tensor(y[:, own], y[:, own], ps[:, 6], ALU.add).then_inc(yd_taken, 1)
                        dve.wait_ge(yd_taken, 4 * g + n // 2 + 1)
                    if d == 1:
                        dve.wait_ge(tile_evac, 10 * g + 7 + c)
                        vec.tensor_tensor(y[:, c], y[:, c], sz[:, c], ALU.mult).then_inc(gated, 1)
                    if proj and n < 6:
                        conv(g + 1, n)
                    if not proj and 2 * n + 1 < EARLY:
                        y_low(2 * n + 2, 2 * n + 1)
                    if n < 7:
                        ada_share(n)

                dve.wait_ge(sq_done, NC * g + NC)
                vec.tensor_scalar(stat[:, 4:8], stat[:, 0:4], 1.0 / T, RMS_EPS, ALU.mult,
                                  ALU.add).then_inc(var_ready, 1)
                dve.wait_ge(root_ready, g + 1)
                link(vec.reciprocal(stat[:, 12:16], stat[:, 8:12]))
                for c in range(NC):
                    ins = vec.tensor_scalar(y[:, c], y[:, c], stat[:, 12 + c:13 + c], None, ALU.mult)
                ins.then_inc(y_normed, 1)
                ada_share(7)
                vec.tensor_tensor(modl[:], modl[:], part[:], ALU.add).then_inc(ada_taken, 1)

            group(0, True)
            start = step.base + step.n
            with dve.Fori(1, GROUPS - 1) as i:
                step.enter(i - 1, start, LINKS_PER_GROUP)
                group(i, True)
            step.leave(GROUPS - 2, start, LINKS_PER_GROUP)
            group(GROUPS - 1, False)

            for u in range(EARLY, WOUT_UNITS):
                y_low(u + 1, u)
            for b in range(4):
                dve.wait_ge(g0_full, 4 + b + 1)
                vec.tensor_copy(gate0[:, 1, b * T:b * T + T], ps[:, 4 + b]).then_inc(g0_taken, 1)

            def add_block(block, bank):
                col = bass.ds(block * T, T)
                for c in range(NC):
                    dve.wait_ge(w_used, block * WOUT_UNITS + (WOUT_AT + WOUT_UNITS))
                    link(vec.tensor_tensor(wtmp[:, c % 2], ps[:, bank + c], gate0[:, c // 2, col], ALU.mult))
                    rows = (r_c if c < 2 else r_x)[:, c % 2, col]
                    vec.scalar_tensor_tensor(out=rows, in0=rows, scalar=ALPHA, in1=wtmp[:, c % 2],
                                             op0=ALU.mult, op1=ALU.add).then_inc(wo_taken, 1)

            def block_stats(block):
                for c in range(NC):
                    dve.wait_ge(wo_taken, block * NC + (c + 1))
                    ins = vec.bn_stats(bn[:, c, bass.ds(block * 6, 6)],
                                       (r_c if c < 2 else r_x)[:, c % 2, bass.ds(block * T, T)])
                link(ins)

            for u in range(2):
                if u == 1:
                    dve.wait_ge(g0_taken, 4)
                    dve.wait_ge(g0_taken_act, 4)
                    dve.wait_ge(res_loaded, 32)
                    add_block(0, 0)
                y_low(WOUT_UNITS + u + 1, u)
            block_stats(0)
            start = step.base + step.n
            with dve.Fori(1, 3) as i:
                step.enter(i - 1, start, NC + 1)
                for u in range(WOUT_UNITS):
                    if u == WOUT_UNITS - 1:
                        add_block(i, 4)
                    y_low(i * WOUT_UNITS + (u + 3), u + 2)
                block_stats(i)
            step.leave(2, start, NC + 1)
            for u in range(WOUT_UNITS - 2):
                y_low(3 * WOUT_UNITS + u + 3, u + 2)
            add_block(3, 4)
            block_stats(3)

            def normalise(stats, n, var_sem, root_sem, at):
                for c in range(n):
                    link(vec.bn_aggr(stat[:, 48 + 2 * c:50 + 2 * c], stats[:, c]))
                    ins = vec.tensor_scalar(stat[:, at + c:at + c + 1], stat[:, 49 + 2 * c:50 + 2 * c], LN_EPS, None, ALU.add)
                ins.then_inc(var_sem, 1)
                dve.wait_ge(root_sem, 1)
                link(vec.reciprocal(stat[:, 56:56 + n], stat[:, at + 4:at + 4 + n]))

            dve.wait_ge(wo_taken, NC * 4)
            rows = [r_c[:, 0], r_c[:, 1], r_x[:, 0], r_x[:, 1]]
            normalise(bn, 4, lnvar_ready, lnroot_ready, 16)
            for c in range(4):
                vec.tensor_scalar(rows[c], rows[c], stat[:, 48 + 2 * c:49 + 2 * c], stat[:, 56 + c:57 + c],
                                  ALU.subtract, ALU.mult).then_inc(ln_ready, 1)
            link(vec.tensor_scalar(us[:], modl[:, 32:48], 1.0, None, ALU.add))
            link(vec.tensor_tensor(ub[:], us[:], par[:, LNB_AT:LNB_AT + 16].unsqueeze(2).to_broadcast([P, KT, 2]), ALU.mult))
            link(vec.tensor_tensor(ub[:], ub[:], modl[:, 16:32], ALU.add))
            link(vec.tensor_tensor(us[:], us[:], par[:, LNG_AT:LNG_AT + 16].unsqueeze(2).to_broadcast([P, KT, 2]), ALU.mult))
            dve.wait_ge(ln_ready, 4)
            for k in range(KT):
                dve.wait_ge(rt_full, k + 1)
                modulate(k, utmp1[:, k % 2], ps[:, 4 + k % 4], us[:, k], ub[:, k])
            dve.wait_ge(rows0_loaded, 32)
            for c in range(2):
                link(vec.tensor_tensor(r_x[:, c], r_x[:, c], rows0[:, 0], ALU.mult))
                ins = vec.tensor_tensor(r_x[:, c], r_x[:, c], rows0[:, 1], ALU.add)
            ins.then_inc(x1_ready, 1)
            for b in range(4):
                dve.wait_ge(g1_full, b + 1)
                vec.tensor_copy(gate1[:, b * T:b * T + T], ps[:, 4 + b]).then_inc(g1_taken, 1)

            for m in range(2):
                n = (TC, T)[m]
                dve.wait_ge(sq_used, 4 * m + 4)
                vec.tensor_scalar(rsd[:, m, 0:n], ps[:, SUM_BANK[m], 0:n], 1.0 / RANK, RMS_EPS, ALU.mult,
                                  ALU.add).then_inc(msv_ready, 1)
                dve.wait_ge(msroot_ready, m + 1)
                link(vec.reciprocal(rsd[:, m, 0:n], rsd[:, m, 0:n]))
                for t in range(4):
                    src = (cq, ckv)[m][:, t]
                    w = par[:, (QN_AT, KVN_AT)[m] + t:(QN_AT, KVN_AT)[m] + t + 1]
                    dve.wait_ge(lat_taken, 4 * m + t + 1)
                    vec.scalar_tensor_tensor(out=src, in0=src, scalar=w, in1=rsd[:, m, 0:n], op0=ALU.mult,
                                             op1=ALU.mult).then_inc(cn_ready, 1)
                for t in range(4):
                    hi, lo = ((cq_hi, cq_lo), (ckv_hi, ckv_lo))[m]
                    dve.wait_ge(chi_ready, 4 * m + t + 1)
                    vec.tensor_tensor(lo[:, t], (cq, ckv)[m][:, t], hi[:, t].bitcast(F32),
                                      ALU.subtract).then_inc(clo_ready, 1)
            dve.wait_ge(krot_full, 1)
            dve.wait_ge(trig_loaded, 16)
            vec.tensor_tensor(sq[:, 0, 0:TC], ps[:, 7, 0:TC], trig[:, 1], ALU.mult)
            link(vec.tensor_tensor(kr[:, TC:T], kr[:, TC:T], trig[:, 0], ALU.mult))
            vec.tensor_tensor(kr[:, TC:T], kr[:, TC:T], sq[:, 0, 0:TC], ALU.add).then_inc(kr_ready, 1)

            for b in range(4):
                dve.wait_ge(w_used, HEAD_AT + HEAD_UNITS * b + 3)
                dve.wait_ge(s_full, 8 * b)
                vec.tensor_copy(qr[:].rearrange("p a n -> p (a n)"), ps[:, 2]).then_inc(hq_dve, 1)
                dve.wait_ge(qrot_full, b + 1)
                dve.wait_ge(hq_dve, 3 * b + 1)
                both = lambda ap: ap.unsqueeze(1).to_broadcast([P, 2, TC])
                vec.tensor_tensor(qrt[:], ps[:, 7].rearrange("p (a n) -> p a n", a=2), both(trig[:, 1]), ALU.mult)
                link(vec.tensor_tensor(qr[:], qr[:], both(trig[:, 0]), ALU.mult))
                vec.tensor_tensor(qr[:], qr[:], qrt[:], ALU.add).then_inc(qr_ready, 1)
                dve.wait_ge(w_used, HEAD_AT + HEAD_UNITS * (b + 1))
                dve.wait_ge(o_full, 4 * b)
                for n in range(2):
                    vec.tensor_copy(v[:, 2 + n], ps[:, 2 + n]).then_inc(hq_dve, 1)

                def max_scores(n):
                    m = 8 * b + n
                    dve.wait_ge(s_full, m + 1)
                    link(vec.reduce_max(stat[:, 32 + n:33 + n], ps[:, SCORE_BANK[n % 4]], AX.X))
                    vec.tensor_scalar(stat[:, 32 + n:33 + n], stat[:, 32 + n:33 + n], -SCALE, None,
                                      ALU.mult).then_inc(max_ready, 1)

                def scale_probs(n):
                    m = 8 * b + n
                    dve.wait_ge(p_ready, m + 1)
                    link(vec.reciprocal(stat[:, 40 + n:41 + n], stat[:, 40 + n:41 + n]))
                    vec.tensor_scalar(prob[:, n % 2], prob[:, n % 2], stat[:, 40 + n:41 + n], None,
                                      ALU.mult).then_inc(p_scaled, 1)

                def take_transposed(n):
                    m = 8 * b + n
                    dve.wait_ge(pt_full, m + 1)
                    if n % 2 == 0 and m >= 2:
                        dve.wait_ge(o_full, m // 2)
                    vec.tensor_copy(prob_t[:, :, n % 2 * P:n % 2 * P + P],
                                    ps[:, 6].rearrange("p (k q) -> p k q", k=4)).then_inc(pt_ready, 1)

                def gate_output(hh):
                    hd = 4 * b + hh
                    dve.wait_ge(o_full, hd + 1)
                    if hd >= 2:
                        dve.wait_ge(ogl_ready, hd - 1)
                    vec.tensor_tensor(sq[:, hh % 2, 0:TC], ps[:, 7, 0:TC], gates[:, hd], ALU.mult).then_inc(o_taken, 1)
                    dve.wait_ge(ogh_ready, hd + 1)
                    vec.tensor_tensor(og_lo[:, hd], sq[:, hh % 2, 0:TC], og_hi[:, hd].bitcast(F32),
                                      ALU.subtract).then_inc(ogl_ready, 1)

                max_scores(0)
                for n in range(8):
                    if n < 7:
                        max_scores(n + 1)
                    scale_probs(n)
                    take_transposed(n)
                    if n % 2 == 1 and n >= 3:
                        gate_output(n // 2 - 1)
                gate_output(3)

            dve.wait_ge(g1_taken, 4)
            dve.wait_ge(x1_ready, 1)
            vec.memset(stat[:, 63:64], 0.0).then_inc(out_taken, 4)
            for nb in range(4):
                for c in range(2):
                    dve.wait_ge(w_used, WO_AT + WO_UNITS * (nb + 1))
                    cols = slice(nb * T, nb * T + T)
                    link(vec.tensor_tensor(sq[:, c], ps[:, 2 * (nb % 2) + c], gate1[:, cols], ALU.mult))
                    ins = vec.scalar_tensor_tensor(out=r_x[:, c, cols], in0=r_x[:, c, cols], scalar=ALPHA,
                                                   in1=sq[:, c], op0=ALU.mult, op1=ALU.add)
                    ins.then_inc(out_taken, 1)
                for c in range(2):
                    dve.wait_ge(out_taken, 4 + 2 * nb + c + 1)
                    ins = vec.bn_stats(bn_out[:, c, 6 * nb:6 * nb + 6], r_x[:, c, cols])
                link(ins)
            normalise(bn_out, 2, fvar_ready, froot_ready, 24)
            dve.wait_ge(rows1_loaded, 32)
            for c in range(2):
                link(vec.scalar_tensor_tensor(out=r_x[:, c], in0=r_x[:, c], scalar=stat[:, 48 + 2 * c:49 + 2 * c],
                                              in1=rows1[:, 0], op0=ALU.subtract, op1=ALU.mult))
                vec.scalar_tensor_tensor(out=r_x[:, c], in0=r_x[:, c], scalar=stat[:, 56 + c:57 + c],
                                         in1=rows1[:, 1], op0=ALU.mult, op1=ALU.add).then_inc(out_ready, 1)

        @block.tensor
        def _(pe):
            mm = nc.tensor.matmul

            def product(out, lhs, rhs, first, last):
                mm(out, lhs[0], rhs[0], start=first, stop=False)
                mm(out, lhs[0], rhs[1], start=False, stop=False)
                return mm(out, lhs[1], rhs[0], start=False, stop=last)

            def weights(slot, cols):
                view = lambda w: w[:, slot].rearrange("p (k n) -> p k n", n=cols)
                return view(w_hi), view(w_lo)

            pe.wait_ge(cond_ready, 1)
            for n in range(ADA0 + 2 * ADA0_LAG):
                if n in ADA0_ON_PE:
                    m = ADA0_ON_PE.index(n)
                    pe.wait_ge(ada0_loaded[n % ADA0_RING], 16 * (n // ADA0_RING + 1))
                    if m >= 4:
                        pe.wait_ge(ada0_taken, m - 3)
                    for k in range(KT):
                        ins = mm(ps[:, 4 + m % 4, 0:2], ada0[:, n % ADA0_RING, k], cond[:, k],
                                 start=(k == 0), stop=(k == KT - 1))
                    ins.then_inc(ada0_pe, 1)
                kt = n // 2 - ADA0_LAG
                if n % 2 == 1 and kt >= 0:
                    half, k = divmod(kt, 8)
                    pe.wait_ge(lo_ready, half + 1)
                    pe.wait_ge(u_ready, kt + 1)
                    w = weights(half, P)
                    for c in range(NC):
                        cols = slice(c * P, c * P + P)
                        ins = product(ps[:, c, 0:P], (u_hi[:, kt, cols], u_lo[:, kt, cols]),
                                      (w[0][:, k], w[1][:, k]), kt == 0, kt == KT - 1)
                    if k == 7:
                        ins.then_inc(w_used, 1)

            def project(g, j):
                pe.wait_ge(lo_ready, PROJ_UNITS * g + (DT_UNITS + j + 1))
                slot = (DT_UNITS + j) % RING
                if j < 12:
                    t, half = divmod(j, 2)
                    w = weights(slot, P)
                    if half == 0:
                        if isinstance(g, int) and g == 0 and t < 4:
                            pe.wait_ge(dt_abs, 1)
                        else:
                            pe.wait_ge(tile_evac, 10 * g + max(t - 3, 0))
                    for k in range(8):
                        kt = half * 8 + k
                        ins = product(ps[:, t % 4], (w[0][:, k], w[1][:, k]), (u_hi[:, kt], u_lo[:, kt]),
                                      kt == 0, kt == KT - 1)
                else:
                    u = j - 12
                    w = weights(slot, T)
                    if u == 0:
                        pe.wait_ge(tile_evac, 10 * g + 6)
                    for c in range(NC):
                        for k in range(2):
                            kt = 2 * u + k
                            cols = slice(c * P, c * P + P)
                            ins = product(ps[:, c], (u_hi[:, kt, cols], u_lo[:, kt, cols]),
                                          (w[0][:, k], w[1][:, k]), kt == 0, kt == KT - 1)
                ins.then_inc(w_used, 1)

            for j in range(PROJ_UNITS):
                project(0, j)
                if j == 3:
                    pe.wait_ge(a_ready, 1)
                    pe.wait_ge(consts_ready, 1)
                    rows = tab[:, A_ROW:A_ROW + 8].rearrange("p (c d) h -> p c d h", d=2)
                    out = ps[:, 5].rearrange("p (c d h) -> p c d h", c=NC, d=2)
                    for d in range(2):
                        mm(out[:, :, d], tri[:, d].bitcast(F32), rows[:, :, d], start=True, stop=True)
                    mm(ps[:, 6], ones[:], tab[:, A_ROW:A_ROW + 8].rearrange("p r h -> p (r h)"),
                       start=True, stop=True).then_inc(cs_full, 1)

            def scan(g, j):
                if j == 1:
                    pe.wait_ge(silu_done, 6 * g + 6)
                    for c in range(NC):
                        if c == 0:
                            pe.wait_ge(yt_evac, GT * g)
                        for k in range(GT):
                            ins = nc.tensor.transpose(ps[:, X_BANK[c], k * P:k * P + P],
                                                      xbc[:, k, c * P:c * P + P], ident[:])
                        ins.then_inc(xt_full, 1)
                if j == 2:
                    pe.wait_ge(xtok_ready, NC * g + 1)
                    for c in range(NC):
                        ins = nc.tensor.transpose(ps[:, 6, c * P:c * P + P], xbc[:, 4, c * P:c * P + P], ident[:])
                    ins.then_inc(bt_full, 1)
                    pe.wait_ge(xtok_ready, NC * g + 2)
                    for c in range(NC):
                        ins = mm(ps[:, 7, c * P:c * P + P], xbc[:, 4, c * P:c * P + P],
                                 xbc[:, 5, c * P:c * P + P], start=True, stop=True)
                    ins.then_inc(cb_full, 1)
                if j % 2 == 0 and 2 <= j < 18:
                    h = j // 2 - 1
                    pe.wait_ge(am_ready, 8 * g + h + 1)
                    if h < 2:
                        pe.wait_ge(xtok_ready, NC * g + 3 + h)
                    else:
                        pe.wait_ge(decay_ready, 8 * g + h - 1)
                    for n in range(2):
                        for d in range(2):
                            ins = mm(ps[:, 4 + h % 2], strict[:, d], am[:, n, d].rearrange("p a n -> p (a n)"),
                                     start=(n == 0 and d == 0), stop=(n == 1 and d == 1))
                    ins.then_inc(seg_full, 1)
                n, half = divmod(j - 3, 2)
                if 3 <= j < 19 and half == 0 and n in READS_STATE:
                    c = STEPS[n][1]
                    pe.wait_ge(state_ready, 6 * g + len([m for m in MAKES_STATE if m < n]))
                    mm(ps[:, 7], ccur[:, c * P:c * P + P], state[:], start=True, stop=True).then_inc(yo_full, 1)
                if 3 <= j < 19 and half == 1 and n in MAKES_STATE:
                    c = STEPS[n][1]
                    if n == 0:
                        pe.wait_ge(btok_ready, g + 1)
                        pe.wait_ge(cbs_ready, g + 1)
                    pe.wait_ge(yo_taken, 6 * g + len([m for m in READS_STATE if m <= n]))
                    pe.wait_ge(xw_ready, 6 * g + MAKES_STATE.index(n) + 1)
                    mm(ps[:, 7], btok[:, c], xw[:], start=True, stop=True).then_inc(st_full, 1)
                if 3 <= j < 19 and half == 1:
                    c = DIAG[n // 2]
                    if n % 2 == 0:
                        pe.wait_ge(yd_taken, 4 * g + n // 2)
                    pe.wait_ge(m_ready, 8 * g + n + 1)
                    for a in range(4):
                        hd = 4 * (n % 2) + a
                        ins = mm(ps[:, 6, hd * HD:hd * HD + HD], em[:, n % 2, a], xtok[:, c, hd * HD:hd * HD + HD],
                                 start=True, stop=True)
                    ins.then_inc(yd_full, 1)

            def wout_unit(block, u, bank):
                pe.wait_ge(ylo_ready, block * WOUT_UNITS + (u + 1))
                pe.wait_ge(lo_ready, block * WOUT_UNITS + (WOUT_AT + u + 1))
                w = weights((WOUT_AT + u) % RING, T)
                for c in range(NC):
                    if u == 0 and bank:
                        pe.wait_ge(wo_taken, block * NC + (c + 1 - NC))
                    cols = slice(c * P, c * P + P)
                    for k in range(2):
                        ins = product(ps[:, bank + c], (yr_hi[:, u % 2, k, cols], yr_lo[:, u % 2, k, cols]),
                                      (w[0][:, k], w[1][:, k]), u == 0 and k == 0,
                                      u == WOUT_UNITS - 1 and k == 1)
                ins.then_inc(w_used, 1)

            def group(g, proj):
                for j in range(PROJ_UNITS):
                    scan(g, j)
                    if not proj and 0 <= j - EARLY_FROM < EARLY:
                        if j == EARLY_FROM:
                            pe.wait_ge(tile_evac, 10 * GROUPS)
                        wout_unit(0, j - EARLY_FROM, 0)
                    if proj:
                        project(g + 1, j)
                pe.wait_ge(y_normed, g + 1)
                pe.wait_ge(yd_taken, 4 * g + 4)
                for k in range(GT):
                    for c in range(NC):
                        ins = nc.tensor.transpose(ps[:, 4 + k, c * P:c * P + P], y[:, c, k * P:k * P + P], ident[:])
                    ins.then_inc(yt_full, 1)

            pe.wait_ge(cs_exp, 3)
            group(0, True)
            with pe.Fori(1, GROUPS - 1) as i:
                group(i, True)
            group(GROUPS - 1, False)

            pe.wait_ge(ada_taken, GROUPS)
            pe.wait_ge(yt_evac, GT * GROUPS)
            for s in range(2):
                if s == 1:
                    pe.wait_ge(g0_taken_act, 4)
                for t in range(KT):
                    ins = mm(ps[:, 4 + t // 4, t % 4 * P:t % 4 * P + P],
                             modl[:, t, s:s + 1].to_broadcast([P, P]), ident[:], start=True, stop=True)
                    if t % 4 == 3:
                        ins.then_inc(g0_full, 1)
                wout_unit(0, EARLY + s, 0)
            pe.wait_ge(g0_taken, 4)
            with pe.Fori(1, 4) as i:
                for u in range(WOUT_UNITS):
                    wout_unit(i, u, 4)

            pe.wait_ge(ln_ready, 4)
            for k in range(KT):
                if k >= 4:
                    pe.wait_ge(utmp_ready, k - 3)
                for c in range(NC):
                    ins = nc.tensor.transpose(ps[:, 4 + k % 4, c * P:c * P + P],
                                              (r_c, r_x)[c // 2][:, c % 2, k * P:k * P + P], ident[:])
                ins.then_inc(rt_full, 1)
            with pe.Fori(0, 4) as i:
                for t in range(4):
                    if t == 2:
                        pe.wait_ge(gt_taken, i * 4 + 1)
                    for half in range(2):
                        s = MLA_AT + 2 * t + half
                        pe.wait_ge(lo_ready, i * 8 + (s + 1))
                        w = weights(s % RING, P)
                        for k in range(8):
                            kt = half * 8 + k
                            if t == 0:
                                pe.wait_ge(u_ready, KT + kt + 1)
                            ins = product(ps[:, t, 0:TC], (w[0][:, k], w[1][:, k]),
                                          (u_hi[:, kt, TC:T], u_lo[:, kt, TC:T]), kt == 0, kt == KT - 1)
                        ins.then_inc(w_used, 1)
                pe.wait_ge(gt_taken, i * 4 + 2)

            def sum_squares(t):
                m, q = divmod(t, 4)
                n = (TC, T)[m]
                pe.wait_ge(sq_ready, t + 1)
                mm(ps[:, SUM_BANK[m], 0:n], ones[:], sq[:, t % 2, 0:n], start=(q == 0), stop=(q == 3)).then_inc(sq_used, 1)

            for t in range(KT):
                ins = mm(ps[:, 4 + t // 4, t % 4 * P:t % 4 * P + P],
                         modl[:, 48 + t, 1:2].to_broadcast([P, P]), ident[:], start=True, stop=True)
                if t % 4 == 3:
                    ins.then_inc(g1_full, 1)
            pe.wait_ge(gt_taken, HEADS)
            for j in range(LATENT_UNITS):
                t, half = divmod(j, 2)
                s = MLA_AT + GATE_UNITS + j
                pe.wait_ge(lo_ready, s + 1)
                if t == 7 and half == 0:
                    pe.wait_ge(msv_ready, 1)
                if t == 8 and half == 0:
                    pe.wait_ge(sq_ready, 1)
                if t < 4 and half == 0:
                    pe.wait_ge(g1_taken, t + 1)
                w = weights(s % RING, P)
                lo = TC if t < 4 else 0
                out = ps[:, 4 + t, 0:TC] if t < 4 else ps[:, t - 4] if t < 8 else ps[:, 4]
                for k in range(8):
                    kt = half * 8 + k
                    ins = product(out, (w[0][:, k], w[1][:, k]), (u_hi[:, kt, lo:T], u_lo[:, kt, lo:T]),
                                  kt == 0, kt == KT - 1)
                ins.then_inc(w_used, 1)
                if half == 1 and t >= 1:
                    sum_squares(t - 1)
            pe.wait_ge(lat_taken, 9)
            pe.wait_ge(rot_loaded, 16)
            mm(ps[:, 7, 0:TC], rot[:], kr[:, TC:T], start=True, stop=True).then_inc(krot_full, 1)

            for b in range(4):
                at = HEAD_AT + HEAD_UNITS * b
                for j in range(HEAD_UNITS):
                    s = at + j
                    pe.wait_ge(lo_ready, s + 1)
                    if j == 0:
                        pe.wait_ge(clo_ready, 4)
                        pe.wait_ge(hq_act, 8 * b)
                        pe.wait_ge(p_ready, 8 * b)
                        pe.wait_ge(hq_dve, 3 * b)
                        pe.wait_ge(lat_taken, 8)
                    if j == 3:
                        pe.wait_ge(clo_ready, 8)
                        pe.wait_ge(p_ready, 8 * b)
                        pe.wait_ge(pt_ready, 8 * b)
                    if j == 5:
                        pe.wait_ge(hq_act, 8 * b + 4)
                        pe.wait_ge(hq_dve, 3 * b + 1)
                    if j < 5:
                        w = weights(s % RING, 2 * P)
                        lat_hi, lat_lo = (cq_hi, cq_lo) if j < 3 else (ckv_hi, ckv_lo)
                        for a in range(2):
                            out = ps[:, j, a * TC:a * TC + TC] if j < 3 else ps[:, 3 + 2 * (j - 3) + a]
                            for k in range(4):
                                cols = slice(a * P, a * P + P)
                                ins = product(out, (w[0][:, k, cols], w[1][:, k, cols]),
                                              (lat_hi[:, k], lat_lo[:, k]), k == 0, k == 3)
                    else:
                        w = weights(s % RING, T)
                        for c in range(NC):
                            cols = slice(c * P, c * P + P)
                            for k in range(2):
                                kt = 2 * (j - 5) + k
                                ins = product(ps[:, c], (ckv_hi[:, kt, cols], ckv_lo[:, kt, cols]),
                                              (w[0][:, k], w[1][:, k]), kt == 0, kt == 3)
                    ins.then_inc(w_used, 1)
                    if j == 4:
                        pe.wait_ge(hq_dve, 3 * b + 1)
                        pe.wait_ge(o_taken, 4 * b)
                        if b == 0:
                            pe.wait_ge(kr_ready, 1)
                        mm(ps[:, 7], rot[:], qr[:].rearrange("p a n -> p (a n)"), start=True,
                           stop=True).then_inc(qrot_full, 1)

                def scores(n):
                    hh, qt = divmod(n, 2)
                    if n == 0:
                        pe.wait_ge(hq_act, 8 * b + 6)
                        pe.wait_ge(qr_ready, b + 1)
                    if n == 2:
                        pe.wait_ge(hq_act, 8 * b + 8)
                    if n >= 4:
                        pe.wait_ge(p_ready, 8 * b + n - 3)
                    q = slice(qt * P, qt * P + P)
                    half = slice(64 * (hh % 2), 64 * (hh % 2) + 64)
                    mm(ps[:, SCORE_BANK[n % 4]], qn[:, hh, q], kn[:, hh], start=True, stop=False)
                    mm(ps[:, SCORE_BANK[n % 4]], qr[half, hh // 2, q], kr[half, :], start=False, stop=True).then_inc(s_full, 1)

                def transpose_probs(n):
                    pe.wait_ge(p_scaled, 8 * b + n + 1)
                    pe.wait_ge(pt_ready, 8 * b + n)
                    for c in range(NC):
                        ins = nc.tensor.transpose(ps[:, 6, c * P:c * P + P], prob[:, n % 2, c * P:c * P + P], ident[:])
                    ins.then_inc(pt_full, 1)

                def head_output(hh):
                    pe.wait_ge(pt_ready, 8 * b + 2 * hh + 2)
                    pe.wait_ge(o_taken, 4 * b + hh)
                    pe.wait_ge(hq_act, 8 * b + 8)
                    pe.wait_ge(hq_dve, 3 * b + 3)
                    for c in range(NC):
                        ins = mm(ps[:, 7, 0:TC], v[:, c, hh * P:hh * P + P], prob_t[:, c], start=(c == 0), stop=(c == 3))
                    ins.then_inc(o_full, 1)

                scores(0)
                scores(1)
                for n in range(8):
                    if n < 6:
                        scores(n + 2)
                    if n % 2 == 0 and n >= 2:
                        head_output(n // 2 - 1)
                    transpose_probs(n)
                head_output(3)

            pe.wait_ge(ogl_ready, HEADS)
            with pe.Fori(0, 2) as i:
                for b in range(2):
                    pe.wait_ge(out_taken, i * 4 + (2 * b + 2))
                    for u in range(WO_UNITS):
                        s = WO_AT + b * WO_UNITS + u
                        pe.wait_ge(lo_ready, i * 2 * WO_UNITS + (s + 1))
                        w = weights(s % RING, T)
                        for c in range(2):
                            cols = slice(c * P, c * P + P)
                            for k in range(2):
                                kt = 2 * u + k
                                ins = product(ps[:, 2 * b + c], (og_hi[:, kt, cols], og_lo[:, kt, cols]),
                                              (w[0][:, k], w[1][:, k]), kt == 0, kt == KT - 1)
                        ins.then_inc(w_used, 1)


def _constants():
    eye = np.eye(P, dtype=np.float32)
    rot = np.zeros((P, P), np.float32)
    even = np.arange(0, P, 2)
    rot[even + 1, even] = -1.0
    rot[even, even + 1] = 1.0
    forward = np.triu(np.ones((P, P), np.float32))
    backward = np.tril(np.ones((P, P), np.float32))
    consts = np.stack([eye, np.ones((P, P), np.float32), rot, forward, backward,
                       1 - forward, 1 - backward])
    freq = np.float32(10000.0) ** (-np.arange(16, dtype=np.float32) / np.float32(16))
    token = np.arange(TC)
    ang = np.concatenate([(token // 64).astype(np.float32)[:, None] * freq,
                          (token % 64).astype(np.float32)[:, None] * freq], -1)
    ang = np.repeat(ang, 2, axis=1).T
    ang = np.concatenate([ang, ang])
    trig = np.stack([np.cos(ang), np.sin(ang)], 1).astype(np.float32)
    return consts.astype(np.float32), trig


def _stationary(w, cols, k_per_unit):
    k, n = w.shape
    w = w.reshape(k // (P * k_per_unit), k_per_unit, P, n // cols, cols)
    return w.transpose(3, 0, 2, 1, 4).reshape(-1, P, k_per_unit * cols)


def _layout(inp):
    def a(name):
        return np.asarray(inp[name])
    w_in = a("ssd_w_in")[0]
    inner, state_at = 4096, 2 * 4096
    units = [_stationary(w_in[:, 10240:10368], P, 8)]
    for g in range(GROUPS):
        x = w_in[:, inner + g * T:inner + (g + 1) * T]
        bm = w_in[:, state_at + g * P:state_at + (g + 1) * P]
        cm = w_in[:, state_at + 1024 + g * P:state_at + 1024 + (g + 1) * P]
        units += [_stationary(x, P, 8), _stationary(bm, P, 8), _stationary(cm, P, 8),
                  _stationary(w_in[:, g * T:(g + 1) * T], T, 2)]
    units.append(_stationary(a("ssd_w_out")[0], T, 2))
    m_in = a("mla_w_in")[0]
    kr = m_in[:, 1024:1088]
    units += [_stationary(m_in[:, 1088:], P, 8), _stationary(m_in[:, :1024], P, 8),
              _stationary(np.concatenate([kr, kr], 1), P, 8)]
    uq = a("mla_w_uq")[0].reshape(RANK, HEADS, 192)
    ukv = a("mla_w_ukv")[0].reshape(RANK, HEADS, 256)
    for b in range(4):
        h = slice(4 * b, 4 * b + 4)
        units += [_stationary(uq[:, h, :128].reshape(RANK, 512), 256, 4),
                  _stationary(uq[:, h, 128:].reshape(RANK, 256), 256, 4),
                  _stationary(ukv[:, h, :128].reshape(RANK, 512), 256, 4),
                  _stationary(ukv[:, h, 128:].reshape(RANK, 512), T, 2)]
    units.append(_stationary(a("mla_w_o")[0], T, 2))
    stream = np.concatenate(units)
    assert stream.shape == (UNITS, P, UNIT), stream.shape

    w0, w1 = a("ada_w")
    ada0 = [w0[:, t * P:t * P + P] for t in ADA0_ORDER]
    ada0 = np.stack([w.reshape(KT, P, P).transpose(1, 0, 2).reshape(P, D) if n in ADA0_ON_PE else w.T
                     for n, w in enumerate(ada0)])
    ada = np.concatenate([w0[:, ADA0 * P:], w1], 1).reshape(GROUPS, ADA_K, ADA_UNITS, 4, P)
    ada = ada.transpose(0, 2, 4, 3, 1).reshape(GROUPS * ADA_UNITS, P, 4, ADA_K)
    conds = np.stack([a("c_ctx"), a("c")[0]])

    def tiles(vec):
        return vec.reshape(-1, P).T

    conv_w, conv_b = a("ssd_conv_w")[0], a("ssd_conv_b")[0]
    par = []
    for g in range(GROUPS):
        cols = np.concatenate([np.arange(g * T, (g + 1) * T), inner + np.arange(g * P, (g + 1) * P),
                               inner + 1024 + np.arange(g * P, (g + 1) * P)])
        par.append(conv_w[:, cols].reshape(TAPS, 6, P).transpose(2, 1, 0).reshape(P, 30))
        par.append(tiles(conv_b[cols]))
    par += [tiles(a("ssd_norm_w")[0]), tiles(a("ada_b")[0]), tiles(a("ada_b")[1]),
            tiles(a("ln_g")[0]), tiles(a("ln_b")[0]), tiles(a("mla_q_norm")[0]), tiles(a("mla_kv_norm")[0]),
            np.stack([tiles(a("c_ctx")), tiles(a("c")[0])], -1).reshape(P, 32)]
    tokens = np.concatenate([a("ctx")[0], a("x")[0]])
    consts, trig = _constants()
    return {
        "stream": stream, "ada0": ada0, "ada": ada,
        "cond_rows": conds.reshape(1, 2, D),
        "cond_groups": conds.reshape(2, GROUPS, ADA_K).transpose(1, 0, 2).reshape(GROUPS, 1, 2, ADA_K),
         "par": np.concatenate(par, 1), "consts": consts, "trig": trig,
        "x_cm": tokens.T.reshape(KT, P, T).transpose(1, 0, 2), "x_tm": tokens.reshape(NC, P, D),
        "dt_bias": a("ssd_dt_bias")[0].reshape(1, P), "a_log": a("ssd_a_log")[0].reshape(1, P),
        "d_skip": a("ssd_d")[0].reshape(1, 64),
        "ln_rows": np.stack([a("ln_g"), a("ln_b")], 1).reshape(2, 2, 1, D),
    }


def kernel(**inputs):
    import concourse.bacc as bacc
    from concourse.bass_utils import run_bass_kernel_spmd

    nc = bacc.Bacc("TRN2", target_bir_lowering=False, num_devices=1)
    arrays = {f"in_{k}": np.ascontiguousarray(v) for k, v in _layout(inputs).items()}
    hbm = {k[3:]: nc.dram_tensor(k, v.shape, F32, kind="ExternalInput").ap() for k, v in arrays.items()}
    hbm["y"] = nc.dram_tensor("inner_rows", (GROUPS, P, GT, T), F32, kind="Internal").ap()
    hbm["out"] = nc.dram_tensor("out", (1, TC, D), F32, kind="ExternalOutput").ap()
    program(nc, hbm)
    r = run_bass_kernel_spmd(nc, [arrays], core_ids=[0])
    return r.results[0]["out"]
```
